# Optimizing a Trainium2 kernel written in Bass

```python
import math
import jax
import jax.numpy as jnp
from jax import lax
import numpy as np

D_MODEL = 1024
BATCH = 1
SEQ = 128
DEPTH = 2
DEC_BATCH = 1
DEC_SEQ = 128
PAST_LEN = 128

GRID_W = 64
N_EVEN = (DEPTH + 1) // 2
N_ODD = DEPTH // 2
N_MOD = 6
EPS = 1e-6
H_A = 4
DH_A = 64
W_A = H_A * 2 * DH_A
Q_BLOCK = 128
ROPE_BASE = 10000.0
AXIS_FREQS = DH_A // 4
H_B = 4
DK_B = 128
DV_B = 128
W_B = H_B * DV_B
CONV_K = 5
DELTA_CHUNK = 64
IN_EVEN = 3 * W_A + 4 * W_B + 4 * H_B
W_C = D_MODEL
C_GROUPS = 4
C_CHUNK = 128
N_GROUPS = 4
E_PER_GROUP = 8
N_EXPERTS = N_GROUPS * E_PER_GROUP
TOP_K = 2
D_EXPERT = 256

kernel_name = "hybrid_diff_deltanet_gmlp_hmoe_prefix_step"

def rms_norm(x, g):
    xf = x.astype(jnp.float32)
    y = xf * lax.rsqrt(jnp.mean(xf * xf, axis=-1, keepdims=True) + EPS)
    return y.astype(x.dtype) * g

def layer_norm(x, g, b):
    xf = x.astype(jnp.float32)
    mu = jnp.mean(xf, axis=-1, keepdims=True)
    var = jnp.mean(jnp.square(xf - mu), axis=-1, keepdims=True)
    return ((xf - mu) * lax.rsqrt(var + EPS)).astype(x.dtype) * g + b

def l2_normalize(x):
    xf = x.astype(jnp.float32)
    return (xf * lax.rsqrt(jnp.sum(xf * xf, axis=-1, keepdims=True) + EPS)).astype(x.dtype)

def rope_2d_tables(n_tok):
    rows = n_tok // GRID_W
    r, col = jnp.meshgrid(jnp.arange(rows), jnp.arange(GRID_W), indexing="ij")
    pos = jnp.stack([r.reshape(-1), col.reshape(-1)], axis=-1).astype(jnp.float32)
    inv = ROPE_BASE ** (-jnp.arange(AXIS_FREQS, dtype=jnp.float32) / AXIS_FREQS)
    ang = pos[:, :, None] * inv
    return jnp.cos(ang), jnp.sin(ang)

def apply_rope_2d(x, cos, sin):
    xs = x.reshape(x.shape[:-1] + (2, 2, AXIS_FREQS))
    x1, x2 = xs[..., 0, :], xs[..., 1, :]
    c = cos[None, :, None, None].astype(x.dtype)
    s = sin[None, :, None, None].astype(x.dtype)
    out = jnp.stack([x1 * c - x2 * s, x1 * s + x2 * c], axis=-2)
    return out.reshape(x.shape)

def diff_attention(q, k, v, lam):
    b, tq, h, e = q.shape
    nblk = tq // Q_BLOCK
    qb = q.reshape(b, nblk, Q_BLOCK, h, e).transpose(1, 0, 2, 3, 4)
    k1, k2 = k[..., :DH_A], k[..., DH_A:]
    scale = DH_A ** -0.5

    def block(qi):
        s1 = jnp.einsum("bqhd,bkhd->bhqk", qi[..., :DH_A], k1).astype(jnp.float32) * scale
        s2 = jnp.einsum("bqhd,bkhd->bhqk", qi[..., DH_A:], k2).astype(jnp.float32) * scale
        p = jax.nn.softmax(s1, axis=-1) - lam * jax.nn.softmax(s2, axis=-1)
        return jnp.einsum("bhqk,bkhe->bqhe", p.astype(v.dtype), v)

    o = lax.map(block, qb)
    return o.transpose(1, 0, 2, 3, 4).reshape(b, tq, h, e)

def short_conv(x, w):
    pad = (CONV_K - 1) // 2
    return lax.conv_general_dilated(x, w[:, None, :].astype(x.dtype), window_strides=(1,),
                                    padding=[(pad, pad)], dimension_numbers=("NWC", "WIO", "NWC"),
                                    feature_group_count=x.shape[-1])

def gated_delta_chunked(q, k, v, beta, g, s0):
    out_dtype = v.dtype
    q, k, v, beta, g, s0 = (a.astype(jnp.float32) for a in (q, k, v, beta, g, s0))
    b, t, h, _ = q.shape
    n = t // DELTA_CHUNK

    def chunks(a):
        a = a.reshape((b, n, DELTA_CHUNK) + a.shape[2:])
        return jnp.moveaxis(a, (1, 3), (0, 2))

    qc, kc, vc, bc = chunks(q), chunks(k), chunks(v), chunks(beta)
    gc = jnp.cumsum(chunks(g), axis=-1)
    idx = jnp.arange(DELTA_CHUNK)
    incl = idx[:, None] >= idx[None, :]
    strict = idx[:, None] > idx[None, :]
    diff = gc[..., :, None] - gc[..., None, :]
    decay = jnp.where(incl, jnp.exp(jnp.where(incl, diff, 0.0)), 0.0)
    kb = kc * bc[..., None]
    lmat = jnp.where(strict, jnp.einsum("nbhid,nbhjd->nbhij", kb, kc) * decay, 0.0)
    eye = jnp.eye(DELTA_CHUNK, dtype=jnp.float32)
    amat = eye + lmat
    tinv = lax.linalg.triangular_solve(amat, jnp.broadcast_to(eye, amat.shape), left_side=True,
                                       lower=True, unit_diagonal=True)
    u = tinv @ (vc * bc[..., None])
    w = tinv @ (kb * jnp.exp(gc)[..., None])
    att = jnp.where(incl, jnp.einsum("nbhid,nbhjd->nbhij", qc, kc) * decay, 0.0)

    def step(s, inp):
        q_i, k_i, u_i, w_i, g_i, a_i = inp
        v_new = u_i - w_i @ s
        o_i = (q_i * jnp.exp(g_i)[..., None]) @ s + a_i @ v_new
        g_last = g_i[..., -1:]
        s = s * jnp.exp(g_last)[..., None] + jnp.einsum(
            "bhcd,bhce->bhde", k_i * jnp.exp(g_last - g_i)[..., None], v_new)
        return s, o_i

    s_fin, o = lax.scan(step, s0, (qc, kc, u, w, gc, att))
    o = jnp.transpose(o, (1, 0, 3, 2, 4)).reshape(b, t, h, -1)
    return o.astype(out_dtype), s_fin

def even_mixer(h, w_in, conv_w, a_log, dt_bias, delta_norm, lam_q, lam_k, subln, w_out, lam_init, ctx):
    b, t, _ = h.shape
    proj = h @ w_in
    qa, ka, va, qkv_b, gate_b, ab = jnp.split(
        proj, [W_A, 2 * W_A, 3 * W_A, 3 * W_A + 3 * W_B, 3 * W_A + 4 * W_B], axis=-1)
    qa = qa.reshape(b, t, H_A, 2 * DH_A)
    ka = ka.reshape(b, t, H_A, 2 * DH_A)
    va = va.reshape(b, t, H_A, 2 * DH_A)
    lam = (jnp.exp(jnp.sum(lam_q[0] * lam_k[0])) - jnp.exp(jnp.sum(lam_q[1] * lam_k[1]))
           + lam_init).astype(jnp.float32)
    if ctx is None:
        keys, vals = ka, va
        s_f0 = jnp.zeros((b, H_B, DK_B, DV_B), jnp.float32)
        s_b0 = jnp.zeros((b, H_B, DK_B, DV_B), jnp.float32)
    else:
        k_ctx, v_ctx, s_f0, s_b0 = ctx
        cos, sin = rope_2d_tables(t)
        qa = apply_rope_2d(qa.reshape(b, t, H_A, 2, DH_A), cos, sin).reshape(b, t, H_A, 2 * DH_A)
        ka = apply_rope_2d(ka.reshape(b, t, H_A, 2, DH_A), cos, sin).reshape(b, t, H_A, 2 * DH_A)
        keys = jnp.concatenate([ka, k_ctx.astype(ka.dtype)], axis=1)
        vals = jnp.concatenate([va, v_ctx.astype(va.dtype)], axis=1)
    oa = rms_norm(diff_attention(qa, keys, vals, lam), subln) * (1.0 - lam_init)

    qkv_b = jax.nn.silu(short_conv(qkv_b, conv_w))
    qb, kb, vb = jnp.split(qkv_b, 3, axis=-1)
    qb = l2_normalize(qb.reshape(b, t, H_B, DK_B)) * (DK_B ** -0.5)
    kb = l2_normalize(kb.reshape(b, t, H_B, DK_B))
    vb = vb.reshape(b, t, H_B, DV_B)
    ab = ab.reshape(b, t, 2, 2, H_B).astype(jnp.float32)
    log_decay = -jnp.exp(a_log)[None, None] * jax.nn.softplus(ab[:, :, :, 0] + dt_bias[None, None])
    beta = jax.nn.sigmoid(ab[:, :, :, 1])
    o_f, s_f = gated_delta_chunked(qb, kb, vb, beta[:, :, 0], log_decay[:, :, 0], s_f0)
    o_br, s_bk = gated_delta_chunked(jnp.flip(qb, 1), jnp.flip(kb, 1), jnp.flip(vb, 1),
                                     jnp.flip(beta[:, :, 1], 1), jnp.flip(log_decay[:, :, 1], 1), s_b0)
    ob = rms_norm(o_f + jnp.flip(o_br, 1), delta_norm) * jax.nn.silu(gate_b.reshape(b, t, H_B, DV_B))
    out = jnp.concatenate([oa.reshape(b, t, W_A), ob.reshape(b, t, W_B)], axis=-1) @ w_out
    return out, (ka, va, s_f, s_bk)

def odd_mixer(h, w_in, ln_g, ln_b, w_s, b_s, w_out):
    b, t, _ = h.shape
    z = jax.nn.gelu(h @ w_in)
    u, v = jnp.split(z, 2, axis=-1)
    v = layer_norm(v, ln_g, ln_b)
    vc = v.reshape(b, t // C_CHUNK, C_CHUNK, C_GROUPS, W_C // C_GROUPS)
    mixed = jnp.einsum("gpq,bnqgc->bnpgc", w_s, vc) + b_s.T[None, None, :, :, None]
    return (u * mixed.reshape(b, t, W_C)) @ w_out

def hier_moe(h, w_rg, b_rg, w_re, b_re, w_g, w_u, w_d):
    b, t, d = h.shape
    x = h.reshape(-1, d)
    n = x.shape[0]
    g_prob = jax.nn.softmax((x @ w_rg + b_rg).astype(jnp.float32), axis=-1)
    p_group, g_idx = lax.top_k(g_prob, 1)
    e_logits = (x @ w_re + b_re).astype(jnp.float32).reshape(n, N_GROUPS, E_PER_GROUP)
    e_in = jnp.take_along_axis(e_logits, jnp.broadcast_to(g_idx[:, :, None], (n, 1, E_PER_GROUP)), axis=1)[:, 0]
    top_p, top_i = lax.top_k(jax.nn.softmax(e_in, axis=-1), TOP_K)
    wts = top_p / jnp.sum(top_p, axis=-1, keepdims=True) * p_group
    ids = g_idx * E_PER_GROUP + top_i
    gates = jnp.sum(jax.nn.one_hot(ids, N_EXPERTS, dtype=jnp.float32) * wts[..., None], axis=1)
    hid = jax.nn.silu(jnp.einsum("nd,edf->nef", x, w_g)) * jnp.einsum("nd,edf->nef", x, w_u)
    y = jnp.einsum("nef,efd->nd", hid * gates[:, :, None].astype(x.dtype), w_d)
    return y.reshape(b, t, d)

def setup_inputs(seed: int = 0) -> dict:
    key = jax.random.key(seed)
    ks = iter(jax.random.split(key, 40))
    nrm = lambda shape, s: jax.random.normal(next(ks), shape, jnp.float32) * s
    gain = lambda shape: 1.0 + nrm(shape, 0.1)
    d = D_MODEL
    return {
        "x_prompt": nrm((BATCH, SEQ, d), 1.0),
        "x_sample": nrm((DEC_BATCH, DEC_SEQ, d), 1.0),
        "cache_k": nrm((DEC_BATCH, N_EVEN, PAST_LEN, H_A, 2 * DH_A), 1.0),
        "cache_v": nrm((DEC_BATCH, N_EVEN, PAST_LEN, H_A, 2 * DH_A), 1.0),
        "state_fwd": nrm((DEC_BATCH, N_EVEN, H_B, DK_B, DV_B), 0.1),
        "state_bwd": nrm((DEC_BATCH, N_EVEN, H_B, DK_B, DV_B), 0.1),
        "c": nrm((DEC_BATCH, d), 1.0),
        "c_ctx": nrm((d,), 1.0),
        "norm_mix": gain((DEPTH, d)),
        "norm_ffn": gain((DEPTH, d)),
        "w_mod": nrm((DEPTH, d, N_MOD * d), d ** -0.5),
        "b_mod": nrm((DEPTH, N_MOD * d), 0.02),
        "w_in_even": nrm((N_EVEN, d, IN_EVEN), d ** -0.5),
        "conv_w": nrm((N_EVEN, CONV_K, 3 * W_B), CONV_K ** -0.5),
        "a_log": jnp.log(jax.random.uniform(next(ks), (N_EVEN, 2, H_B), jnp.float32, 1.0, 16.0)),
        "dt_bias": jnp.log(jnp.expm1(jax.random.uniform(next(ks), (N_EVEN, 2, H_B), jnp.float32, 0.001, 0.1))),
        "delta_norm": gain((N_EVEN, DV_B)),
        "lam_q": nrm((N_EVEN, 2, DH_A), 0.1),
        "lam_k": nrm((N_EVEN, 2, DH_A), 0.1),
        "subln": gain((N_EVEN, 2 * DH_A)),
        "w_out_even": nrm((N_EVEN, W_A + W_B, d), (W_A + W_B) ** -0.5),
        "w_in_odd": nrm((N_ODD, d, 2 * W_C), d ** -0.5),
        "sgu_ln_g": gain((N_ODD, W_C)),
        "sgu_ln_b": nrm((N_ODD, W_C), 0.02),
        "w_spatial": nrm((N_ODD, C_GROUPS, C_CHUNK, C_CHUNK), C_CHUNK ** -0.5),
        "b_spatial": 1.0 + nrm((N_ODD, C_GROUPS, C_CHUNK), 0.1),
        "w_out_odd": nrm((N_ODD, W_C, d), W_C ** -0.5),
        "w_router_group": nrm((DEPTH, d, N_GROUPS), d ** -0.5),
        "b_router_group": nrm((DEPTH, N_GROUPS), 0.01),
        "w_router_expert": nrm((DEPTH, d, N_EXPERTS), d ** -0.5),
        "b_router_expert": nrm((DEPTH, N_EXPERTS), 0.01),
        "w_exp_gate": nrm((DEPTH, N_EXPERTS, d, D_EXPERT), d ** -0.5),
        "w_exp_up": nrm((DEPTH, N_EXPERTS, d, D_EXPERT), d ** -0.5),
        "w_exp_down": nrm((DEPTH, N_EXPERTS, D_EXPERT, d), D_EXPERT ** -0.5),
        "final_norm": gain((d,)),
    }

def reference(x_prompt, x_sample, cache_k, cache_v, state_fwd, state_bwd, c, c_ctx,
              norm_mix, norm_ffn, w_mod, b_mod, w_in_even, conv_w, a_log, dt_bias, delta_norm,
              lam_q, lam_k, subln, w_out_even, w_in_odd, sgu_ln_g, sgu_ln_b, w_spatial, b_spatial,
              w_out_odd, w_router_group, b_router_group, w_router_expert, b_router_expert,
              w_exp_gate, w_exp_up, w_exp_down, final_norm):
    def run(x, cvec, latent):
        states = []
        for l in range(DEPTH):
            mod = jax.nn.silu(cvec) @ w_mod[l] + b_mod[l]
            sh1, sc1, g1, sh2, sc2, g2 = jnp.split(mod[:, None, :], N_MOD, axis=-1)
            h = rms_norm(x, norm_mix[l]) * (1.0 + sc1) + sh1
            i = l // 2
            if l % 2 == 0:
                ctx = (cache_k[:, i], cache_v[:, i], state_fwd[:, i], state_bwd[:, i]) if latent else None
                out, st = even_mixer(h, w_in_even[i], conv_w[i], a_log[i], dt_bias[i], delta_norm[i],
                                     lam_q[i], lam_k[i], subln[i], w_out_even[i],
                                     0.8 - 0.6 * math.exp(-0.3 * l), ctx)
                states.append(st)
            else:
                out = odd_mixer(h, w_in_odd[i], sgu_ln_g[i], sgu_ln_b[i], w_spatial[i], b_spatial[i],
                                w_out_odd[i])
            x = x + g1 * out
            h = rms_norm(x, norm_ffn[l]) * (1.0 + sc2) + sh2
            x = x + g2 * hier_moe(h, w_router_group[l], b_router_group[l], w_router_expert[l],
                                  b_router_expert[l], w_exp_gate[l], w_exp_up[l], w_exp_down[l])
        return rms_norm(x, final_norm), states

    y_prompt, st_p = run(x_prompt, c_ctx[None, :], False)
    y_sample, _ = run(x_sample, c, True)
    new_cache_k = jnp.stack([s[0] for s in st_p], axis=1)
    new_cache_v = jnp.stack([s[1] for s in st_p], axis=1)
    new_state_fwd = jnp.stack([s[2] for s in st_p], axis=1)
    new_state_bwd = jnp.stack([s[3] for s in st_p], axis=1)
    return (y_prompt, y_sample, new_cache_k, new_cache_v, new_state_fwd, new_state_bwd)


_drawn_inputs = setup_inputs


def setup_inputs(seed=0):
    import zlib

    import numpy as np

    out = dict(_drawn_inputs(seed))
    spreads = {}
    factors = {'b_router_group': 4.215, 'sgu_ln_b': 2.808, 'b_router_expert': 2.669}
    for name, (base, spread) in spreads.items():
        noise = np.random.default_rng([zlib.crc32(name.encode()), seed]).standard_normal(out[name].shape)
        drawn = base * np.exp(spread * noise) if base else spread * noise
        out[name] = jnp.asarray(drawn.astype(out[name].dtype))
    for name, factor in factors.items():
        out[name] = (out[name] * factor).astype(out[name].dtype)
    return out
```

```python
import numpy as np
from contextlib import ExitStack

import concourse.bass as bass
from concourse import mybir

F32 = mybir.dt.float32
I32 = mybir.dt.int32
ALU = mybir.AluOpType
ACT = mybir.ActivationFunctionType
AX = mybir.AxisListType

P = 128
D = 1024
KT = D // P
NB = 2
T = NB * P
DEPTH = 2
N_MOD = 6
MT = N_MOD * KT
EPS = 1e-6
H = 4
DH = 64
WA = H * P
LAM_INIT = 0.8 - 0.6
CONV_K = 5
IN_EVEN = 3 * WA + 4 * WA + 4 * H
NG, EG = 4, 8
NE = NG * EG
FE = 256
CAP = 64
PAIRS = NE // 2
LEVELS = 7
RING = 6
SLOT = 4096
BIG = 1e30
OVF = 8

C_ID, C_ONE, C_TRI = 0, P, 2 * P
C_LEV = C_TRI + 2 * P
C_SLOT = C_LEV + 2 * LEVELS * P
C_COS = C_SLOT + CAP
C_SIN = C_COS + DH
C_G4 = C_SIN + DH
C_E32 = C_G4 + NG
C_J8 = C_E32 + NE
C_EPS = C_J8 + OVF
NC_COLS = C_EPS + 2

V_BMOD = 0
V_NMIX = V_BMOD + DEPTH * MT
V_COND = V_NMIX + DEPTH * KT
V_NFFN = V_COND + NB * KT
V_FIN = V_NFFN + DEPTH * KT
V_CONV = V_FIN + KT
V_DN = V_CONV + CONV_K * 3 * H
V_SUB = V_DN + 1
NV = V_SUB + 1


def shape_constants():
    c = np.zeros((P, NC_COLS), np.float32)
    r = np.arange(P)[:, None]
    q = np.arange(P)[None, :]
    c[:, C_ID:C_ID + P] = r == q
    c[:, C_ONE:C_ONE + P] = 1
    c[:, C_TRI:C_TRI + P] = r <= q
    c[:, C_TRI + P:C_TRI + 2 * P] = r >= q
    for lev in range(LEVELS):
        s = 1 << lev
        m = (r // (2 * s) == q // (2 * s)) & (r % (2 * s) < s) & (q % (2 * s) >= s)
        o = C_LEV + lev * P
        c[:, o:o + P] = m
        c[:, o + LEVELS * P:o + LEVELS * P + P] = m.T
    c[:, C_SLOT:C_SLOT + CAP] = np.arange(1, CAP + 1)
    freqs = DH // 4
    tok = np.arange(P)
    pos = np.stack([tok // 64, tok % 64], -1).astype(np.float32)
    inv = (10000.0 ** (-np.arange(freqs, dtype=np.float32) / freqs)).astype(np.float32)
    ang = pos[:, :, None] * inv
    cos, sin = np.cos(ang), np.sin(ang)
    c[:, C_COS:C_COS + DH] = np.stack([cos, cos], 2).reshape(P, DH)
    c[:, C_SIN:C_SIN + DH] = np.stack([-sin, sin], 2).reshape(P, DH)
    c[:, C_G4:C_G4 + NG] = NG - np.arange(NG)
    c[:, C_E32:C_E32 + NE] = NE - np.arange(NE)
    c[:, C_J8:C_J8 + OVF] = np.arange(OVF)
    c[:, C_EPS] = EPS
    c[:, C_EPS + 1] = 1.0
    return c


class Semaphores:

    def __init__(self, sem):
        self.a_ab = sem("a_ab")
        self.a_at = sem("a_at")
        self.a_chain = sem("a_chain")
        self.a_cv = sem("a_cv")
        self.a_d0 = sem("a_d0")
        self.a_dec = sem("a_dec")
        self.a_e1 = sem("a_e1")
        self.a_egc = sem("a_egc")
        self.a_exp = sem("a_exp")
        self.a_fin = sem("a_fin")
        self.a_gelu = sem("a_gelu")
        self.a_gv = sem("a_gv")
        self.a_h = sem("a_h")
        self.a_hr = sem("a_hr")
        self.a_kd = sem("a_kd")
        self.a_l2 = sem("a_l2")
        self.a_lnr = sem("a_lnr")
        self.a_lx = sem("a_lx")
        self.a_mrow = sem("a_mrow")
        self.a_ors = sem("a_ors")
        self.a_osq = sem("a_osq")
        self.a_pt = sem("a_pt")
        self.a_qg = sem("a_qg")
        self.a_qkv = sem("a_qkv")
        self.a_rexp = sem("a_rexp")
        self.a_rstd = sem("a_rstd")
        self.a_silu = sem("a_silu")
        self.a_silu_c = sem("a_silu_c")
        self.a_sq = sem("a_sq")
        self.a_sqc = sem("a_sqc")
        self.a_sqv = sem("a_sqv")
        self.a_st = sem("a_st")
        self.a_vn = sem("a_vn")
        self.a_ws = sem("a_ws")
        self.a_xt = sem("a_xt")
        self.g_bm = sem("g_bm")
        self.g_set = sem("g_set")
        self.ld_attn = sem("ld_attn")
        self.ld_const = sem("ld_const")
        self.ld_odd = sem("ld_odd")
        self.ld_router = sem("ld_router")
        self.ld_small = sem("ld_small")
        self.ld_state = sem("ld_state")
        self.ld_vec = sem("ld_vec")
        self.ld_x = sem("ld_x")
        self.m_dn = sem("m_dn")
        self.m_gat = sem("m_gat")
        self.m_hid = sem("m_hid")
        self.m_p = sem("m_p")
        self.m_sg = sem("m_sg")
        self.m_td = sem("m_td")
        self.m_turn = sem("m_turn")
        self.m_xg0 = sem("m_xg0")
        self.m_xg1 = sem("m_xg1")
        self.m_yr0 = sem("m_yr0")
        self.m_yr1 = sem("m_yr1")
        self.stored = sem("stored")
        self.t_ab = sem("t_ab")
        self.t_at = sem("t_at")
        self.t_bb = sem("t_bb")
        self.t_cv = sem("t_cv")
        self.t_dt = sem("t_dt")
        self.t_fin = sem("t_fin")
        self.t_gc = sem("t_gc")
        self.t_gcb = sem("t_gcb")
        self.t_hr = sem("t_hr")
        self.t_kk = sem("t_kk")
        self.t_ks = sem("t_ks")
        self.t_l2 = sem("t_l2")
        self.t_last = sem("t_last")
        self.t_ld = sem("t_ld")
        self.t_lg = sem("t_lg")
        self.t_lx = sem("t_lx")
        self.t_mod = sem("t_mod")
        self.t_ms = sem("t_ms")
        self.t_mx = sem("t_mx")
        self.t_o = sem("t_o")
        self.t_os = sem("t_os")
        self.t_pos = sem("t_pos")
        self.t_pt = sem("t_pt")
        self.t_qk = sem("t_qk")
        self.t_qkv = sem("t_qkv")
        self.t_sc = sem("t_sc")
        self.t_st = sem("t_st")
        self.t_u = sem("t_u")
        self.t_v = sem("t_v")
        self.t_vec = sem("t_vec")
        self.t_vn = sem("t_vn")
        self.t_wo = sem("t_wo")
        self.t_ws = sem("t_ws")
        self.t_x = sem("t_x")
        self.used = sem("used")
        self.v_a = sem("v_a")
        self.v_ab = sem("v_ab")
        self.v_abx = sem("v_abx")
        self.v_att = sem("v_att")
        self.v_cen = sem("v_cen")
        self.v_chain = sem("v_chain")
        self.v_cols = sem("v_cols")
        self.v_conv = sem("v_conv")
        self.v_cv = sem("v_cv")
        self.v_dd = sem("v_dd")
        self.v_dt0 = sem("v_dt0")
        self.v_fin = sem("v_fin")
        self.v_gc = sem("v_gc")
        self.v_gd = sem("v_gd")
        self.v_gll = sem("v_gll")
        self.v_h = sem("v_h")
        self.v_hr = sem("v_hr")
        self.v_kd = sem("v_kd")
        self.v_l2 = sem("v_l2")
        self.v_last = sem("v_last")
        self.v_ln = sem("v_ln")
        self.v_lv = sem("v_lv")
        self.v_mask = sem("v_mask")
        self.v_mix = sem("v_mix")
        self.v_mixed = sem("v_mixed")
        self.v_mod = sem("v_mod")
        self.v_p = sem("v_p")
        self.v_pos = sem("v_pos")
        self.v_qkv = sem("v_qkv")
        self.v_r = sem("v_r")
        self.v_rexp = sem("v_rexp")
        self.v_rope = sem("v_rope")
        self.v_route = sem("v_route")
        self.v_sub = sem("v_sub")
        self.v_x = sem("v_x")
        self.v_xn = sem("v_xn")
        self.v_xt = sem("v_xt")
        self.v_y = sem("v_y")


class FurtherSemaphores:

    def __init__(self, sem, l):
        self.f_act = sem(f"f_act{l}")
        self.f_dve = sem(f"f_dve{l}")
        self.f_idx = sem(f"f_idx{l}")
        self.f_pe = sem(f"f_pe{l}")
        self.f_vpre = sem(f"f_vpre{l}")
        self.f_w = sem(f"f_w{l}")


def build(nc, I, O):
    ctx = ExitStack()
    with ctx:
        def sem(name):
            return ctx.enter_context(nc.semaphore(name))

        S = Semaphores(sem)
        FS = [FurtherSemaphores(sem, l) for l in range(DEPTH)]
        full = [ctx.enter_context(nc.semaphore(f"slot_full{i}")) for i in range(RING)]

        def sb(name, shape, dt=F32):
            return ctx.enter_context(nc.sbuf_tensor(name, shape, dt))

        ring = sb("ring", [P, RING, SLOT])
        xT = sb("xT", [P, KT, NB, P])
        hT = sb("hT", [P, KT, NB, P])
        const = sb("const", [P, NC_COLS])
        cols = sb("cols", [P, NV])
        condT = sb("condT", [P, NB, KT])
        modT = sb("modT", [P, DEPTH * MT, NB])
        mulA = sb("mulA", [P, 2 * DEPTH, KT, NB])
        rstd = sb("rstd", [P, T])
        wab = sb("wab", [P, KT, 4 * H])
        wrt = sb("wrt", [P, DEPTH, KT, NG + NE])
        brt = sb("brt", [P, DEPTH, NG + NE])
        mrow = wrt[:, :, :, :].rearrange("p l k n -> p (l k n)")[:, 0:512]
        small = sb("small", [P, 512])
        route_i = sb("route_i", [1, DEPTH, 16], I32)
        scratch = sb("scratch", [P, 19552])
        zeros = sb("zeros", [32, 640], mybir.dt.bfloat16)
        psum = ctx.enter_context(nc.psum_tensor("psum", [P, 8, 512], F32))

        ident = const[:, C_ID:C_ID + P]
        ones = const[:, C_ONE:C_ONE + P]
        tri = [const[:, C_TRI + d * P:C_TRI + d * P + P] for d in range(2)]
        epsc = const[:, C_EPS:C_EPS + 1]
        onec = const[:, C_EPS + 1:C_EPS + 2]

        def level(d, lev):
            o = C_LEV + (d * LEVELS + lev) * P
            return const[:, o:o + P]

        def part(at, shape):
            n = int(np.prod(shape))
            v = scratch[:, at:at + n]
            if len(shape) == 2:
                v = v.rearrange("p (a b) -> p a b", b=shape[1])
            elif len(shape) == 3:
                v = v.rearrange("p (a b c) -> p a b c", b=shape[1], c=shape[2])
            elif len(shape) == 4:
                v = v.rearrange("p (a b c d) -> p a b c d", b=shape[1], c=shape[2], d=shape[3])
            return v

        def bcast_mid(v, n):
            return v.unsqueeze(1).to_broadcast([P, n, v.shape[1]])

        def bcast_last(v, n):
            return v.unsqueeze(2).to_broadcast([P, v.shape[1], n])

        bank = [psum[:, b, :] for b in range(8)]

        def heads(v):
            return v.rearrange("p (h n) -> p h n", h=H)

        vec1 = part(0, (P,))
        vec2 = part(P, (P,))
        xin = part(2 * P, (NB, D))
        convT = part(0, (3 * H, NB, P))
        gateT = part(3072, (H, NB, P))
        ktok = part(4096, (H * P,))
        vtok = part(4608, (NB, H * P))
        E0 = 5632
        raw = part(E0, (3 * H, NB, P + 4))
        qkvt = part(E0 + 3168, (NB, 3 * WA))
        rq = part(E0 + 6240, (2 * WA,))
        rtmp = part(E0 + 7264, (2 * WA,))
        attT = part(E0 + 8288, (5, WA))
        ckv = part(E0 + 10848, (2, WA))
        expS = part(E0 + 11872, (2 * H, T))
        PT = part(E0 + 7264, (2, WA))
        sqx = part(E0 + 11872, (KT, T))
        osq = [part(E0 + 8288 + t * 2 * WA, (WA,)) for t in range(NB)]
        ors = [part(E0 + 8288 + t * 2 * WA + WA, (WA,)) for t in range(NB)]
        g_Lt = [part(E0 + g * 3072, (WA,)) for g in range(4)]
        g_att = [part(E0 + g * 3072 + 512, (WA,)) for g in range(4)]
        g_D = [part(E0 + g * 3072 + 1024, (WA,)) for g in range(4)]
        g_DT = [part(E0 + g * 3072 + 1536, (WA,)) for g in range(4)]
        g_X = [part(E0 + g * 3072 + 2048, (WA,)) for g in range(4)]
        g_B = [part(E0 + g * 3072 + 2560, (WA,)) for g in range(4)]
        g_q = [None, None, part(E0 + 12288, (WA,)), part(E0 + 12800, (WA,))]
        S0 = hT[:, H:2 * H, :, :].rearrange("p h t n -> p (h t n)").rearrange("p (d x) -> p d x", d=2)
        uT = part(0, (KT, T))
        vtk = part(2048, (NB, D))
        sqo = part(4096, (KT, T))
        vsq = part(6144, (D,))
        lng = part(14200, (D,))
        lnb = part(15224, (D,))
        wsp = part(16248, (4, P))
        wsT = part(16760, (4, P))
        bsp = scratch[0:1, 17272:17784]
        hrow = part(0, (NB, KT, P))
        xg = part(2048, (KT, 2 * CAP))
        hid = part(3072, (FE,))
        sg = part(3328, (FE,))
        turned = part(3584, (4, P))
        hidT = turned[:, 0:2, :]
        pgT = turned[:, 2:4, :].rearrange("p a n -> p (a n)")
        yr = part(4608, (KT, P))
        Pm = part(5888, (NB, 2 * CAP))
        PG = part(6144, (NB, 2 * CAP))
        sqm = part(6400, (KT, T))
        R0 = 8448
        lg = part(R0, (NB, NG + NE))
        em = part(R0 + 72, (NB, NE))
        em2 = part(R0 + 136, (NB, NE))
        cnd = part(R0 + 200, (NB, NE))
        oh1 = part(R0 + 264, (NB, NE))
        oh2 = part(R0 + 328, (NB, NE))
        pos = part(R0 + 392, (NB, NE + 2))
        gat = part(R0 + 460, (NB, NE + 2))
        msk = part(R0 + 528, (NB, NE))
        rs = part(R0 + 592, (64,))
        cnt = part(R0 + 656, (NE,))
        nov = part(R0 + 688, (NE,))
        cumA = part(R0 + 720, (NE,))
        cumB = part(R0 + 752, (NE,))
        lej = part(R0 + 784, (OVF, NE))
        tj = part(R0 + 1040, (OVF, NE))
        ovs = part(R0 + 1296, (64,))
        pos2 = part(R0 + 1360, (NB, OVF))
        gat2 = part(R0 + 1376, (NB, OVF))
        gcls = part(R0 + 1392, (NB, NG))
        yrow = part(12000, (NB, D))
        sqf = part(14100, (KT, T))

        ab = small[:, 0:32]
        gdec = small[:, 32:48]
        beta = small[:, 48:64]
        t16a = small[:, 64:80]
        t16b = small[:, 80:96]
        alog = small[:, 96:104]
        dtb = small[:, 104:112]
        lamc = small[:, 112:113]
        lame = small[:, 114:116]
        subl = small[:, 116:117]
        gcc = small[:, 128:144]
        gll = small[:, 144:160]
        egc = small[:, 160:176]
        ekd = small[:, 176:184]
        lamq = small[:, 192:320]
        lamk = small[:, 320:448]
        smx = small[:, 448:456]
        ssm = small[:, 456:464]
        lnm = small[:, 464:466]
        lns = small[:, 466:468]
        lnr = small[:, 468:470]

        MODC = MT // 4
        stream = []

        def put(kind, *a):
            stream.append((kind,) + a)

        for j in range(4):
            put("mod", 0, j)
        for j in range(7):
            put("in0", j)
        for j in range(4, MODC):
            put("mod", 0, j)
        for j in range(MODC):
            put("mod", 1, j)
        for j in range(2):
            put("out0", j)
        moe_at = [len(stream)]
        stream += [("moe", 0)] * (3 * PAIRS)
        for j in range(4):
            put("in1", j)
        for j in range(2):
            put("out1", j)
        moe_at.append(len(stream))
        stream += [("moe", 1)] * (3 * PAIRS)
        index = {s: n for n, s in enumerate(stream) if s[0] != "moe"}

        wm = I["w_mod"].rearrange("l (k p) n -> l p k n", p=P)
        wi0 = I["w_in_even"][0].rearrange("(k p) n -> p k n", p=P)
        wi1 = I["w_in_odd"][0].rearrange("(k p) n -> p k n", p=P)
        wo0 = I["w_out_even"][0].rearrange("(k p) n -> p k n", p=P)
        wo1 = I["w_out_odd"][0].rearrange("(k p) n -> p k n", p=P)
        source = {"in0": wi0, "in1": wi1, "out0": wo0, "out1": wo1}

        def slot_kn(s):
            return ring[:, s, :].rearrange("p (k n) -> p k n", k=KT)

        def chunk_full(eng, name):
            c = index[name]
            eng.wait_ge(full[c % RING], 32 * (c // RING + 1))
            return c % RING

        block = ctx.enter_context(nc.Block())

        @block.sync
        def _(sp):
            def load(c, slot, halves):
                if c is not None and c >= RING:
                    sp.wait_ge(S.used, c - RING + 1)
                for dst, src in halves:
                    sp.dma_start(dst, src).then_inc(full[slot], 16)

            def moe_layer(l):
                wg = I["w_exp_gate"][l].rearrange("(i e) (p k) f -> i e p (k f)", e=4, k=KT)
                wu = I["w_exp_up"][l].rearrange("(i e) (p k) f -> i e p (k f)", e=4, k=KT)
                wd = I["w_exp_down"][l].rearrange("(i e) (a p) n -> i e p a n", e=4, a=2)
                with sp.Fori(0, PAIRS // 2) as i:
                    for u in range(2):
                        for e in range(2):
                            c = moe_at[l] + 3 * u + e
                            sp.wait_ge(S.used, i * 6 + (c - RING + 1))
                            s = c % RING
                            sp.dma_start(ring[:, s, 0:2048], wg[i, 2 * u + e]).then_inc(full[s], 16)
                            sp.dma_start(ring[:, s, 2048:4096], wu[i, 2 * u + e]).then_inc(full[s], 16)
                        c = moe_at[l] + 3 * u + 2
                        sp.wait_ge(S.used, i * 6 + (c - RING + 1))
                        s = c % RING
                        for e in range(2):
                            dst = ring[:, s, 2048 * e:2048 * e + 2048].rearrange("p (a n) -> p a n", a=2)
                            sp.dma_start(dst, wd[i, 2 * u + e]).then_inc(full[s], 16)

            def moe_further(l):
                f = FS[l]
                wg = I["w_exp_gate"][l].rearrange("e (p k) f -> e p (k f)", k=KT)
                wu = I["w_exp_up"][l].rearrange("e (p k) f -> e p (k f)", k=KT)
                wd = I["w_exp_down"][l].rearrange("e (a p) n -> e p a n", a=2)
                end = moe_at[l] + 3 * PAIRS
                sp.wait_ge(S.v_route, l + 1)
                n = sp.value_load(route_i[0:1, l, 0:1], min_val=0, max_val=OVF // 2)
                with sp.If(n > 0):
                    sp.wait_ge(f.f_idx, 1)
                    sp.wait_ge(S.used, end)
                    with sp.Fori(0, n) as i:
                        sp.wait_ge(f.f_pe, i * 6 + 1)
                        for e in range(2):
                            x = sp.value_load(route_i[0:1, l, bass.ds(i * 2 + (1 + e), 1)], min_val=0, max_val=NE - 1)
                            sp.dma_start(ring[:, e, 0:2048], wg[x]).then_inc(f.f_w, 16)
                            sp.dma_start(ring[:, e, 2048:4096], wu[x]).then_inc(f.f_w, 16)
                            dst = ring[:, 2, 2048 * e:2048 * e + 2048].rearrange("p (a n) -> p a n", a=2)
                            sp.dma_start(dst, wd[x]).then_inc(f.f_w, 16)
                    sp.wait_ge(S.t_fin, l + 1)
                with sp.Else():
                    sp.nop()

            c = 0
            while c < len(stream):
                kind = stream[c][0]
                if kind == "moe":
                    moe_layer(stream[c][1])
                    moe_further(stream[c][1])
                    c += 3 * PAIRS
                    continue
                s = c % RING
                if kind == "mod":
                    _, l, j = stream[c]
                    src = wm[l][:, :, 512 * j:512 * j + 512]
                else:
                    j = stream[c][1]
                    src = source[kind][:, :, 512 * j:512 * j + 512]
                dst = slot_kn(s)
                load(c, s, [(dst[:, 0:4], src[:, 0:4]), (dst[:, 4:8], src[:, 4:8])])
                c += 1
            y = [O["y_prompt"][0], O["y_sample"][0]]
            for t in range(NB):
                sp.wait_ge(S.v_fin, t + 1)
                sp.wait_ge(S.a_fin, t + 1)
                sp.dma_start(y[t], yrow[:, t, :]).then_inc(S.stored, 16)
            sp.wait_ge(S.stored, 16 * 6)

        @block.tensor
        def _(pe):
            mm = nc.tensor.matmul

            def used(ins):
                ins.then_inc(S.used, 1)

            pe.wait_ge(S.ld_const, 16)
            pe.wait_ge(S.ld_vec, 16 * 9)
            nc.tensor.transpose(bank[0][:, 0:P], vec1[:, :], ident)
            nc.tensor.transpose(bank[0][:, P:P + 86], vec2[0:86, :], const[0:86, C_ID:C_ID + 86]).then_inc(S.t_vec, 1)
            pe.wait_ge(S.ld_x, 32)
            for b in range(4):
                t, kh = b // 2, b % 2
                for k in range(4):
                    last = nc.tensor.transpose(bank[1 + b][:, k * P:(k + 1) * P],
                                               xin[:, t, (kh * 4 + k) * P:(kh * 4 + k + 1) * P], ident)
                last.then_inc(S.t_x, 1)

            def mod_chunk(l, j):
                s = chunk_full(pe, ("mod", l, j))
                w = slot_kn(s)
                g, at = l * MODC // 4 + j // 4, j % 4 * P
                if g > 0 and at == 0:
                    pe.wait_ge(S.a_mrow, g)
                for k in range(KT):
                    for m in range(4):
                        last = mm(bank[7][32 * m:32 * m + NB, at:at + P], condT[:, :, k], w[:, k, m * P:(m + 1) * P],
                                  start=(k == 0), stop=(k == KT - 1))
                used(last)

            def mod_turn(g):
                pe.wait_ge(S.a_mrow, g + 1)
                if g > 0:
                    pe.wait_ge(S.v_mod, g)
                for j in range(4):
                    last = nc.tensor.transpose(bank[6][:, j * P:(j + 1) * P], mrow[:, j * P:(j + 1) * P], ident)
                last.then_inc(S.t_mod, 1)

            pe.wait_ge(S.g_set, 1)
            mm(bank[7], zeros[:, 512:640], zeros[:, 0:512], start=True, stop=True)
            pe.wait_ge(S.a_silu_c, 1)
            for j in range(4):
                mod_chunk(0, j)
            mod_turn(0)

            def mean_square(n, sq, b):
                pe.wait_ge(S.a_sq, n)
                for k in range(KT):
                    last = mm(bank[b][:, 0:T], ones, sq[:, k, :], start=(k == 0), stop=(k == KT - 1))
                last.then_inc(S.t_ms, 1)

            mean_square(1, sqx, 5)

            pe.wait_ge(S.v_h, 1)
            pe.wait_ge(S.a_h, 1)
            for n in range(3):
                s = chunk_full(pe, ("in0", n))
                w = slot_kn(s)
                for t in range(NB):
                    for k in range(KT):
                        last = mm(bank[2 * n + t], hT[:, k, t, :], w[:, k, :], start=(k == 0), stop=(k == KT - 1))
                    if t == 0:
                        last.then_inc(S.t_qkv, 1)
                used(last)
            for u in range(8):
                b = u if u < 6 else u - 6
                if u < 6:
                    pe.wait_ge(S.v_qkv if u % 2 == 0 else S.a_qkv, u // 2 + 1)
                else:
                    pe.wait_ge(S.v_cv if u == 6 else S.a_cv, 1)
                if u % 2 == 0:
                    s = chunk_full(pe, ("in0", 3 + u // 2))
                w = slot_kn(s)
                for c2 in range(2):
                    m = (u % 2) * 2 + c2
                    for k in range(KT):
                        last = mm(bank[b][:, c2 * T:(c2 + 1) * T], w[:, k, m * P:(m + 1) * P], hT[:, k, :, :],
                                  start=(k == 0), stop=(k == KT - 1))
                if u % 2 == 1:
                    used(last)
                else:
                    last.then_inc(S.t_cv, 1)
            pe.wait_ge(S.ld_small, 16 * 5)
            pe.wait_ge(S.v_cv, 2)
            for t in range(NB):
                for k in range(KT):
                    last = mm(bank[2][:, t * 16:t * 16 + 16], hT[:, k, t, :], wab[:, k, :],
                              start=(k == 0), stop=(k == KT - 1))
            last.then_inc(S.t_ab, 1)
            for j in range(4, MODC):
                mod_chunk(0, j)
                if j % 4 == 3:
                    mod_turn(j // 4)

            pe.wait_ge(S.a_cv, 5)
            for n in range(5):
                if n == 2:
                    pe.wait_ge(S.v_ab, 1)
                    pe.wait_ge(S.v_rope, 1)
                if n == 4:
                    pe.wait_ge(S.ld_attn, 32)
                    pe.wait_ge(S.v_cv, 3)
                src = [qkvt[:, 0, 0:WA], qkvt[:, 0, WA:2 * WA], rq[:, 0:WA], rq[:, WA:2 * WA], ckv[:, 0, :]][n]
                for h in range(H):
                    last = nc.tensor.transpose(bank[n][:, h * P:(h + 1) * P], src[:, h * P:(h + 1) * P], ident)
                last.then_inc(S.t_at, 1)

            def scores(t):
                pe.wait_ge(S.a_at, 5)
                for hh in range(2 * H):
                    h, half = hh // 2, hh % 2
                    r = slice(half * DH, half * DH + DH)
                    q = attT[r, 2 * t, h * P:(h + 1) * P]
                    keys = [attT[r, 2 * t + 1, h * P:(h + 1) * P]]
                    if t == 1:
                        keys.append(attT[r, 4, h * P:(h + 1) * P])
                    for n, k in enumerate(keys):
                        if t == 0:
                            o = bank[half][:, h * P:(h + 1) * P]
                        else:
                            o = bank[2 + 2 * half + h // 2][:, (h % 2) * T + n * P:(h % 2) * T + (n + 1) * P]
                        last = mm(o, q, k, start=True, stop=True)
                last.then_inc(S.t_sc, 1)

            def values(t):
                pe.wait_ge(S.v_p, t + 1)
                for kt in range(1 + t):
                    for h in range(H):
                        last = nc.tensor.transpose(bank[2 * t + kt][:, h * P:(h + 1) * P],
                                                   expS[:, h, kt * P:(kt + 1) * P], ident)
                last.then_inc(S.t_pt, 1)
                pe.wait_ge(S.a_pt, t + 1)
                for h in range(H):
                    for kt in range(1 + t):
                        v = qkvt[:, t, 2 * WA + h * P:2 * WA + (h + 1) * P] if kt == 0 else ckv[:, 1, h * P:(h + 1) * P]
                        last = mm(bank[1 + 3 * t][:, h * P:(h + 1) * P], v, PT[:, kt, h * P:(h + 1) * P],
                                  start=(kt == 0), stop=(kt == t))
                last.then_inc(S.t_o, 1)
                pe.wait_ge(S.a_osq, t + 1)
                mm(bank[2 * t], ones, osq[t], start=True, stop=True).then_inc(S.t_os, 1)

            scores(0)
            scores(1)
            for j in range(4):
                mod_chunk(1, j)
            values(0)
            mod_turn(3)
            for j in range(4, 8):
                mod_chunk(1, j)
            values(1)
            mod_turn(4)
            for j in range(8, MODC):
                mod_chunk(1, j)
            mod_turn(5)

            pe.wait_ge(S.v_mixed, 2)
            pe.wait_ge(S.a_silu, 3)
            for n in range(2):
                for h in range(H):
                    last = nc.tensor.transpose(bank[4 + n][:, h * P:(h + 1) * P], convT[:, 2 * H + h, n, :], ident)
                last.then_inc(S.t_at, 1)
            pe.wait_ge(S.a_sqc, 1)
            for n in range(2 * H):
                last = mm(bank[n // 2][:, (n % 2) * T:(n % 2 + 1) * T], ones, sqx[:, n, :], start=True, stop=True)
            last.then_inc(S.t_l2, 1)
            pe.wait_ge(S.v_gd, 1)
            pe.wait_ge(S.v_mod, 6)
            for g in range(4):
                t, d = g // 2, g % 2
                last = mm(bank[6][:, g * H:(g + 1) * H], tri[d], gdec[:, g * H:(g + 1) * H], start=True, stop=True)
            last.then_inc(S.t_gc, 1)
            pe.wait_ge(S.v_l2, 1)
            pe.wait_ge(S.a_at, 7)
            for h in range(H):
                last = nc.tensor.transpose(bank[4][:, h * P:(h + 1) * P], convT[:, H + h, 0, :], ident)
            last.then_inc(S.t_at, 1)
            pe.wait_ge(S.a_at, 8)

            def qh(h, t):
                return convT[:, h, t, :]

            def kh(h, t):
                return convT[:, H + h, t, :]

            def delta_tables(g):
                t, d = g // 2, g % 2
                b = 3 * (g % 2)
                if g >= 2:
                    pe.wait_ge(S.v_att, g - 1)
                    pe.wait_ge(S.a_d0, g - 1)
                for h in range(H):
                    last = mm(bank[b][:, h * P:(h + 1) * P], gdec[:, g * H + h:g * H + h + 1].to_broadcast([P, P]),
                              tri[d], start=True, stop=True)
                last.then_inc(S.t_gcb, 1)
                for h in range(H):
                    last = mm(bank[b + 1][:, h * P:(h + 1) * P],
                              beta[:, g * H + h:g * H + h + 1].to_broadcast([P, P]), ident, start=True, stop=True)
                last.then_inc(S.t_bb, 1)
                for h in range(H):
                    last = mm(bank[b + 2][:, h * P:(h + 1) * P], kh(h, t), kh(h, t), start=True, stop=True)
                last.then_inc(S.t_kk, 1)

            def delta_tables2(g):
                t, d = g // 2, g % 2
                b = 3 * (g % 2)
                pe.wait_ge(S.a_dec, g + 1)
                for h in range(H):
                    last = mm(bank[b][:, h * P:(h + 1) * P], kh(h, t), qh(h, t), start=True, stop=True)
                last.then_inc(S.t_qk, 1)
                pe.wait_ge(S.v_dt0, g + 1)
                for h in range(H):
                    last = nc.tensor.transpose(bank[b + 1][:, h * P:(h + 1) * P], g_DT[g][:, h * P:(h + 1) * P], ident)
                last.then_inc(S.t_dt, 1)

            for pair in range(2):
                for g in (2 * pair, 2 * pair + 1):
                    delta_tables(g)
                for g in (2 * pair, 2 * pair + 1):
                    delta_tables2(g)
            pe.wait_ge(S.v_att, 4)
            pe.wait_ge(S.a_d0, 4)

            for lev in range(1, LEVELS):
                for pair in range(2):
                    gs = (2 * pair, 2 * pair + 1)
                    n = (lev - 1) * 4
                    for g in gs:
                        b = 3 * (g % 2)
                        pe.wait_ge(S.g_bm, n + g + 1)
                        if lev > 1:
                            pe.wait_ge(S.v_lv, n - 4 + g + 1)
                        for h in range(H):
                            q = slice(h * P, (h + 1) * P)
                            last = mm(bank[b][:, q], g_B[g][:, q], g_D[g][:, q], start=True, stop=True)
                        last.then_inc(S.t_lx, 1)
                    for g in gs:
                        b = 3 * (g % 2)
                        pe.wait_ge(S.a_lx, n + g + 1)
                        if n + g >= 2:
                            pe.wait_ge(S.v_lv, n + g - 1)
                        for h in range(H):
                            q = slice(h * P, (h + 1) * P)
                            if lev < LEVELS - 1:
                                mm(bank[b + 1][:, q], g_DT[g][:, q], g_X[g][:, q], start=True, stop=True)
                            last = mm(bank[b + 2][:, q], g_X[g][:, q], g_DT[g][:, q], start=True, stop=True)
                        last.then_inc(S.t_ld, 1)

            pe.wait_ge(S.ld_state, 32)
            pe.wait_ge(S.v_lv, 24)
            for g in (2, 3):
                for h in range(H):
                    q = slice(h * P, (h + 1) * P)
                    last = mm(bank[3 * (g % 2)][:, q], kh(h, 1), S0[:, g % 2, q], start=True, stop=True)
                last.then_inc(S.t_ks, 1)
            VB = [1, 4, 2, 5]
            for g in range(4):
                pe.wait_ge(S.v_r, g + 1)
                for h in range(H):
                    q = slice(h * P, (h + 1) * P)
                    last = mm(bank[VB[g]][:, q], g_DT[g][:, q], g_X[g][:, q], start=True, stop=True)
                last.then_inc(S.t_vn, 1)
            for t in range(NB):
                pe.wait_ge(S.a_vn, 2 * t + 2)
                for h in range(H):
                    q = slice(h * P, (h + 1) * P)
                    terms = []
                    for d in range(2):
                        g = 2 * t + d
                        terms.append((g_B[g][:, q], g_att[g][:, q]))
                        if t == 1:
                            terms.append((S0[:, d, q], g_q[g][:, q]))
                    for n, (a, b) in enumerate(terms):
                        last = mm(bank[6 if t == 0 else 0][:, q], a, b, start=(n == 0), stop=(n == len(terms) - 1))
                last.then_inc(S.t_o, 1)
                if t == 0:
                    for g in range(2):
                        pe.wait_ge(S.v_kd, g + 1)
                        for h in range(H):
                            q = slice(h * P, (h + 1) * P)
                            last = mm(bank[3 if g == 0 else 1][:, q], g_D[g][:, q], g_B[g][:, q], start=True, stop=True)
                        last.then_inc(S.t_st, 1)
            for t in range(NB):
                pe.wait_ge(S.a_osq, NB + t + 1)
                mm(bank[4 + t], ones, g_X[t], start=True, stop=True).then_inc(S.t_os, 1)

            def project_out(name, ready, need):
                pe.wait_ge(ready, need)
                for m in range(KT):
                    if m % 4 == 0:
                        s = chunk_full(pe, (name, m // 4))
                        w = slot_kn(s)
                    for k in range(KT):
                        last = mm(bank[m // 2][:, (m % 2) * T:(m % 2 + 1) * T], w[:, k, (m % 4) * P:(m % 4 + 1) * P],
                                  hT[:, k, :, :], start=(k == 0), stop=(k == KT - 1))
                    if m % 4 == 3:
                        used(last)
                    elif m % 2 == 1:
                        last.then_inc(S.t_wo, 1)

            project_out("out0", S.v_mixed, 4)

            def moe(l):
                mean_square(2 * l + 2, sqm, 5)
                pe.wait_ge(S.v_h, 2 * l + 2)
                pe.wait_ge(S.a_h, 2 * l + 2)
                pe.wait_ge(S.ld_router, 16 * 6)
                for t in range(NB):
                    for k in range(KT):
                        last = mm(bank[0][:, t * 36:t * 36 + 36], hT[:, k, t, :], wrt[:, l, k, :],
                                  start=(k == 0), stop=(k == KT - 1))
                last.then_inc(S.t_lg, 1)
                for n in range(4):
                    t, half = n // 2, n % 2
                    if n == 3:
                        pe.wait_ge(S.a_hr, 2 * l + 1)
                    for k in range(4):
                        last = nc.tensor.transpose(bank[1 + n % 3][:, k * P:(k + 1) * P], hT[:, half * 4 + k, t, :], ident)
                    last.then_inc(S.t_hr, 1)
                pe.wait_ge(S.g_set, 2)
                for b in range(4):
                    last = mm(bank[4 + b], zeros[:, 512:640], zeros[:, 0:512], start=True, stop=True, skip_group_check=True)
                
                pe.wait_ge(S.v_mask, l + 1)
                for t in range(NB):
                    mm(bank[0][:, t * NE:(t + 1) * NE], tri[0], msk[:, t, :], start=True, stop=(t == 0))
                    if t == 1:
                        mm(bank[0][:, NE:2 * NE], ones, msk[:, 0, :], start=False, stop=True)
                for t in range(NB):
                    last = mm(bank[0][:, 2 * NE:3 * NE], ones, msk[:, t, :], start=(t == 0), stop=(t == 1))
                last.then_inc(S.t_pos, 1)

            def gather(half, b, sem):
                for k in range(4):
                    for t in range(NB):
                        last = mm(bank[b][:, k * P:(k + 1) * P], hrow[:, t, half * 4 + k, :], Pm[:, t, :],
                                  start=(t == 0), stop=(t == 1))
                last.then_inc(sem, 1)

            def experts_up(s0, s1, sem, n):
                for k in range(KT):
                    for e in range(2):
                        w = ring[:, (s0, s1)[e], :].rearrange("p (a k f) -> p k a f", a=2, k=KT)[:, k, :, :]
                        last = mm(bank[0][e * CAP:(e + 1) * CAP, :], xg[:, k, e * CAP:(e + 1) * CAP], w,
                                  start=(k == 0), stop=(k == KT - 1))
                last.then_inc(sem, n)

            def turn(sem):
                for a in range(2):
                    nc.tensor.transpose(bank[0][:, a * P:(a + 1) * P], hid[:, a * P:(a + 1) * P], ident)
                for t in range(NB):
                    last = nc.tensor.transpose(bank[0][:, (2 + t) * P:(3 + t) * P], PG[:, t, :], ident)
                last.then_inc(sem, 1)

            def experts_down(half, s):
                for a in range(2):
                    for e in range(2):
                        base = e * 2048 + a * D + half * 512
                        last = mm(bank[1 + half][e * CAP:(e + 1) * CAP, :], hidT[:, a, e * CAP:(e + 1) * CAP],
                                  ring[:, s, base:base + 512], start=(a == 0), stop=(a == 1))
                return last

            def scatter():
                for k in range(KT):
                    last = mm(bank[4 + k // 2][:, (k % 2) * T:(k % 2 + 1) * T], yr[:, k, :], pgT,
                              start=False, stop=True, skip_group_check=True)
                return last

            def moe_experts(l):
                n0 = l * PAIRS
                q0 = l * (PAIRS + 1)
                pe.wait_ge(S.a_hr, 2 * l + 2)
                pe.wait_ge(S.v_hr, 2 * l + 2)
                pe.wait_ge(S.v_pos, l + 1)
                pe.wait_ge(S.m_p, 2 * q0 + 1)
                gather(0, 3, S.m_gat)
                gather(1, 0, S.m_gat)
                with pe.Fori(0, PAIRS // 2) as i:
                    for u in range(2):
                        c = moe_at[l] + 3 * u
                        s0, s1, s2 = c % RING, (c + 1) % RING, (c + 2) % RING
                        n = n0 + u
                        q = q0 + u
                        pe.wait_ge(S.m_xg0, i * 2 + (q + 1))
                        pe.wait_ge(S.m_xg1, i * 2 + (q + 1))
                        pe.wait_ge(full[s0], i * 32 + 32 * (c // RING + 1))
                        pe.wait_ge(full[s1], i * 32 + 32 * ((c + 1) // RING + 1))
                        experts_up(s0, s1, S.used, 2)
                        pe.wait_ge(S.m_yr0, i * 2 + (q + 1))
                        pe.wait_ge(S.m_yr1, i * 2 + (q + 1))
                        scatter()
                        pe.wait_ge(S.m_hid, i * 2 + (n + 1))
                        pe.wait_ge(S.m_p, i * 4 + (2 * q + 2))
                        turn(S.m_turn)
                        pe.wait_ge(S.m_p, i * 4 + (2 * q + 3))
                        gather(0, 3, S.m_gat)
                        pe.wait_ge(S.m_td, i * 2 + (n + 1))
                        gather(1, 0, S.m_gat)
                        pe.wait_ge(full[s2], i * 32 + 32 * ((c + 2) // RING + 1))
                        experts_down(0, s2).then_inc(S.m_dn, 1)
                        used(experts_down(1, s2))
                pe.wait_ge(S.m_yr0, (l + 1) * (PAIRS + 1))
                pe.wait_ge(S.m_yr1, (l + 1) * (PAIRS + 1))
                scatter()

            def moe_further(l):
                f = FS[l]
                pe.wait_ge(S.v_route, l + 1)
                pe.wait_ge(S.m_xg0, (l + 1) * (PAIRS + 1))
                pe.wait_ge(S.m_xg1, (l + 1) * (PAIRS + 1))
                n = pe.value_load(route_i[0:1, l, 0:1], min_val=0, max_val=OVF // 2)
                with pe.If(n > 0):
                    pe.sem_inc(f.f_pe, 1)
                    with pe.Fori(0, n) as i:
                        pe.wait_ge(f.f_dve, i * 5 + 1)
                        gather(0, 3, f.f_pe)
                        gather(1, 0, f.f_pe)
                        pe.wait_ge(f.f_dve, i * 5 + 3)
                        pe.wait_ge(f.f_act, i * 4 + 1)
                        pe.wait_ge(f.f_w, i * 96 + 96)
                        experts_up(0, 1, f.f_pe, 1)
                        pe.wait_ge(f.f_dve, i * 5 + 4)
                        turn(f.f_pe)
                        pe.wait_ge(f.f_act, i * 4 + 3)
                        experts_down(0, 2)
                        experts_down(1, 2).then_inc(f.f_pe, 1)
                        pe.wait_ge(f.f_act, i * 4 + 4)
                        pe.wait_ge(f.f_dve, i * 5 + 5)
                        scatter().then_inc(f.f_pe, 1)
                with pe.Else():
                    pe.nop()
                mm(bank[0][:, 0:16], zeros[:, 512:640], zeros[:, 0:16], start=True, stop=True).then_inc(S.t_fin, 1)

            moe(0)
            moe_experts(0)
            moe_further(0)

            mean_square(3, sqo, 1)
            pe.wait_ge(S.v_h, 3)
            pe.wait_ge(S.a_h, 3)
            for j in range(2):
                s = chunk_full(pe, ("in1", j))
                w = slot_kn(s)
                for m in range(4):
                    b = 2 * j + m // 2
                    for k in range(KT):
                        last = mm(bank[b][:, (m % 2) * T:(m % 2 + 1) * T], w[:, k, m * P:(m + 1) * P], hT[:, k, :, :],
                                  start=(k == 0), stop=(k == KT - 1))
                    if m == 1:
                        last.then_inc(S.t_u, 1)
                used(last)
            pe.wait_ge(S.v_y, 1)
            for j in range(2):
                s = chunk_full(pe, ("in1", 2 + j))
                w = slot_kn(s)
                for t in range(NB):
                    for k in range(KT):
                        last = mm(bank[4 + 2 * j + t], hT[:, k, t, :], w[:, k, :], start=(k == 0), stop=(k == KT - 1))
                    if t == 0:
                        last.then_inc(S.t_v, 1)
                used(last)
            pe.wait_ge(S.ld_odd, 16 * 4)
            pe.wait_ge(S.a_gelu, 1)
            for g in range(4):
                last = nc.tensor.transpose(bank[0][:, g * P:(g + 1) * P], wsp[:, g, :], ident)
            last.then_inc(S.t_ws, 1)
            pe.wait_ge(S.a_ws, 1)
            pe.wait_ge(S.a_gelu, 4)
            for t in range(NB):
                pe.wait_ge(S.v_ln, t + 1)
                for m in range(KT):
                    g = m // 2
                    o = bank[2 * t + m // 4][:, (m % 4) * P:(m % 4 + 1) * P]
                    mm(o, vtk[:, t, m * P:(m + 1) * P], wsT[:, g, :], start=True, stop=False)
                    last = mm(o, const[0:1, C_ONE:C_ONE + P], bsp[:, g * P:(g + 1) * P], start=False, stop=True)
                    if m % 4 == 3:
                        last.then_inc(S.t_mx, 1)
            project_out("out1", S.v_mix, 4)
            moe(1)
            moe_experts(1)
            moe_further(1)

            mean_square(5, sqf, 1)
            pe.wait_ge(S.v_last, 1)
            for n in range(4):
                t, half = n // 2, n % 2
                for k in range(4):
                    last = nc.tensor.transpose(bank[2 + n][:, k * P:(k + 1) * P], hT[:, half * 4 + k, t, :], ident)
                last.then_inc(S.t_last, 1)

        @block.scalar
        def _(act):
            A = nc.scalar.activation

            act.dma_start(const[:, :], I["consts"]).then_inc(S.ld_const, 16)
            act.dma_start(vec1[0:DEPTH * MT, :], I["b_mod"].rearrange("l (m p) -> (l m) p", p=P)).then_inc(S.ld_vec, 16)
            act.dma_start(vec1[96:112, :], I["norm_mix"].rearrange("l (m p) -> (l m) p", p=P)).then_inc(S.ld_vec, 16)
            act.dma_start(vec1[112:120, :], I["c_ctx"].rearrange("(m p) -> m p", p=P)).then_inc(S.ld_vec, 16)
            act.dma_start(vec1[120:128, :], I["c"][0].rearrange("(m p) -> m p", p=P)).then_inc(S.ld_vec, 16)
            act.dma_start(vec2[0:16, :], I["norm_ffn"].rearrange("l (m p) -> (l m) p", p=P)).then_inc(S.ld_vec, 16)
            act.dma_start(vec2[16:24, :], I["final_norm"].rearrange("(m p) -> m p", p=P)).then_inc(S.ld_vec, 16)
            act.dma_start(vec2[24:84, :], I["conv_w"][0].rearrange("j (m p) -> (j m) p", p=P)).then_inc(S.ld_vec, 16)
            act.dma_start(vec2[84:85, :], I["delta_norm"]).then_inc(S.ld_vec, 16)
            act.dma_start(vec2[85:86, :], I["subln"]).then_inc(S.ld_vec, 16)
            act.dma_start(xin[:, 0, :], I["x_prompt"][0]).then_inc(S.ld_x, 16)
            act.dma_start(xin[:, 1, :], I["x_sample"][0]).then_inc(S.ld_x, 16)
            act.dma_start(wab[:, :, :], wi0[:, :, 7 * 512:IN_EVEN]).then_inc(S.ld_small, 16)
            act.dma_start(alog, I["a_log"][0].rearrange("a b -> (a b)").partition_broadcast(P)).then_inc(S.ld_small, 16)
            act.dma_start(dtb, I["dt_bias"][0].rearrange("a b -> (a b)").partition_broadcast(P)).then_inc(S.ld_small, 16)
            act.dma_start(lamq, I["lam_q"][0].rearrange("a b -> (a b)").partition_broadcast(P)).then_inc(S.ld_small, 16)
            act.dma_start(lamk, I["lam_k"][0].rearrange("a b -> (a b)").partition_broadcast(P)).then_inc(S.ld_small, 16)
            act.dma_start(ckv[:, 0, :], I["cache_k"][0, 0].rearrange("t h e -> t (h e)")).then_inc(S.ld_attn, 16)
            act.dma_start(ckv[:, 1, :], I["cache_v"][0, 0].rearrange("t h e -> t (h e)")).then_inc(S.ld_attn, 16)
            act.dma_start(brt[:, :, 0:NG], I["b_router_group"].partition_broadcast(P)).then_inc(S.ld_router, 16)
            act.dma_start(brt[:, :, NG:], I["b_router_expert"].partition_broadcast(P)).then_inc(S.ld_router, 16)

            def inv_root(dst, src, scale, ev, n):
                A(dst, src, ACT.Ln, bias=epsc, scale=scale).then_inc(S.a_chain, 1)
                count[0] += 1
                act.wait_ge(S.a_chain, count[0])
                A(dst, dst, ACT.Exp, scale=-0.5).then_inc(ev, 1)

            count = [0]

            def norm(n, sq, b, l, shift):
                A(sq.rearrange("p k n -> p (k n)"), xT[:, :, :, :].rearrange("p k t n -> p (k t n)"), ACT.Square).then_inc(S.a_sq, 1)
                act.wait_ge(S.t_ms, n)
                inv_root(rstd[:, :], bank[b][:, 0:T], 1.0 / D, S.a_rstd, n)
                if l is None:
                    return
                act.wait_ge(S.v_xn, n)
                for k in range(KT):
                    last = A(hT[:, k, 1, :], hT[:, k, 1, :], ACT.Identity, scale=mulA[:, n - 1, k, 1:2],
                             bias=modT[:, l * MT + shift + k, 1:2])
                last.then_inc(S.a_h, 1)

            def mod_row(g):
                act.wait_ge(S.used, index[("mod", g // 3, 4 * (g % 3) + 3)] + 1)
                if g > 0:
                    act.wait_ge(S.t_mod, g)
                A(mrow, bank[7], ACT.Copy).then_inc(S.a_mrow, 1)

            act.wait_ge(S.v_cols, 1)
            A(condT[:, :, :].rearrange("p t k -> p (t k)"), cols[:, V_COND:V_COND + NB * KT], ACT.Silu).then_inc(S.a_silu_c, 1)
            for b in (2, 3):
                act.wait_ge(S.t_x, b + 1)
                A(xT[:, (b % 2) * 4:(b % 2) * 4 + 4, 1, :], heads(bank[1 + b]), ACT.Copy).then_inc(S.a_xt, 1)
            mod_row(0)
            act.wait_ge(S.a_xt, 2)
            act.wait_ge(S.v_xt, 2)
            norm(1, sqx, 5, 0, 0)

            for n in range(3):
                act.wait_ge(S.used, index[("in0", n)] + 1)
                A(qkvt[:, 1, n * WA:(n + 1) * WA], bank[2 * n + 1], ACT.Copy).then_inc(S.a_qkv, 1)
            act.wait_ge(S.g_set, 2)
            for u in (1, 3, 5):
                act.wait_ge(S.used, index[("in0", 3 + u // 2)] + 1)
                A(raw[:, 2 * u:2 * u + 2, :, 2:P + 2].rearrange("p c t n -> p (c t) n"),
                  bank[u].rearrange("p (c n) -> p c n", n=P), ACT.Copy).then_inc(S.a_cv, 1)
            for u in (6, 7):
                if u == 6:
                    act.wait_ge(S.t_cv, 4)
                else:
                    act.wait_ge(S.used, index[("in0", 6)] + 1)
                A(gateT[:, 2 * (u - 6):2 * (u - 6) + 2, :, :].rearrange("p c t n -> p (c t n)"), bank[u - 6], ACT.Silu).then_inc(S.a_cv, 1)
            act.wait_ge(S.v_qkv, 3)
            act.dma_start(O["new_cache_k"][0, 0].rearrange("t h e -> t (h e)"), qkvt[:, 0, WA:2 * WA]).then_inc(S.stored, 16)
            act.dma_start(O["new_cache_v"][0, 0].rearrange("t h e -> t (h e)"), qkvt[:, 0, 2 * WA:3 * WA]).then_inc(S.stored, 16)
            act.wait_ge(S.t_ab, 1)
            act.dma_start(S0[:, 0, :].rearrange("p (h n) -> p h n", h=H), I["state_fwd"][0, 0].rearrange("h k v -> k h v")).then_inc(S.ld_state, 16)
            act.dma_start(S0[:, 1, :].rearrange("p (h n) -> p h n", h=H), I["state_bwd"][0, 0].rearrange("h k v -> k h v")).then_inc(S.ld_state, 16)
            act.wait_ge(S.v_abx, 1)
            A(t16a, t16a, ACT.Exp).then_inc(S.a_e1, 1)
            A(alog, alog, ACT.Exp).then_inc(S.a_e1, 1)
            A(beta, beta, ACT.Exp, scale=-1.0).then_inc(S.a_e1, 1)
            A(lame, lame, ACT.Exp).then_inc(S.a_e1, 1)
            act.wait_ge(S.a_e1, 4)
            A(t16a, t16a, ACT.Ln, bias=onec).then_inc(S.a_ab, 1)

            mod_row(1)
            mod_row(2)
            for n in range(5):
                act.wait_ge(S.t_at, n + 1)
                A(attT[:, n, :], bank[n], ACT.Copy).then_inc(S.a_at, 1)
            for t in range(NB):
                act.wait_ge(S.v_sub, t + 1)
                w = P * (1 + t)
                A(expS[:, :, 0:w], expS[:, :, 0:w], ACT.Exp, scale=DH ** -0.5).then_inc(S.a_exp, 1)
                act.wait_ge(S.v_p, t + 1)
                if t == 0:
                    act.wait_ge(S.t_pt, 1)
                    A(PT[:, 0, :], bank[0], ACT.Copy).then_inc(S.a_pt, 1)
                else:
                    act.wait_ge(S.t_pt, 2)
                    act.wait_ge(S.t_o, 1)
                    A(PT[:, :, :], psum[:, 2:4, :], ACT.Copy).then_inc(S.a_pt, 1)
                act.wait_ge(S.t_o, t + 1)
                A(osq[t], bank[1 + 3 * t], ACT.Square).then_inc(S.a_osq, 1)
                act.wait_ge(S.t_os, t + 1)
                inv_root(ors[t], bank[2 * t], 1.0 / P, S.a_ors, t + 1)
                mod_row(3 + t)
            mod_row(5)
            act.wait_ge(S.t_mod, 6)
            for l in range(DEPTH):
                act.dma_start(wrt[:, l, :, 0:NG], I["w_router_group"][l].rearrange("(k p) n -> p k n", p=P)).then_inc(S.ld_router, 16)
                act.dma_start(wrt[:, l, :, NG:], I["w_router_expert"][l].rearrange("(k p) n -> p k n", p=P)).then_inc(S.ld_router, 16)

            for n in range(3):
                act.wait_ge(S.v_conv, 4 * 12 + 4 * (n + 1))
                v = convT[:, 4 * n:4 * n + 4, :, :].rearrange("p h t n -> p (h t n)")
                A(v, v, ACT.Silu).then_inc(S.a_silu, 1)
            act.wait_ge(S.a_silu, 2)
            A(sqx.rearrange("p k n -> p (k n)"), convT[:, 0:8, :, :].rearrange("p h t n -> p (h t n)"), ACT.Square).then_inc(S.a_sqc, 1)
            for n in range(2):
                act.wait_ge(S.t_at, 5 + n + 1)
                A(vtok[:, n, :], bank[4 + n], ACT.Copy).then_inc(S.a_at, 1)
            act.wait_ge(S.t_l2, 1)
            inv_root(sqx.rearrange("p k n -> p (k n)"), psum[:, 0:4, :].rearrange("p b n -> p (b n)"), 1.0, S.a_l2, 1)
            act.wait_ge(S.v_gc, 1)
            A(egc, gcc, ACT.Exp).then_inc(S.a_egc, 1)
            act.wait_ge(S.t_at, 8)
            A(ktok, bank[4], ACT.Copy).then_inc(S.a_at, 1)
            for pair in range(2):
                for g in (2 * pair, 2 * pair + 1):
                    act.wait_ge(S.v_dd, g + 1)
                    if g >= 2:
                        A(g_q[g], bank[3 * (g % 2)], ACT.Exp).then_inc(S.a_qg, 1)
                    A(g_D[g], g_D[g], ACT.Exp).then_inc(S.a_dec, 1)
                for g in (2 * pair, 2 * pair + 1):
                    act.wait_ge(S.t_dt, g + 1)
                    act.wait_ge(S.v_att, g + 1)
                    A(g_D[g], bank[3 * (g % 2) + 1], ACT.Copy).then_inc(S.a_d0, 1)
            act.wait_ge(S.v_gll, 1)
            A(ekd, ekd, ACT.Exp).then_inc(S.a_kd, 1)
            for lev in range(1, LEVELS):
                for g in range(4):
                    act.wait_ge(S.t_lx, (lev - 1) * 4 + g + 1)
                    A(g_X[g], bank[3 * (g % 2)], ACT.Copy).then_inc(S.a_lx, 1)
            VB = [1, 4, 2, 5]
            for g in range(4):
                act.wait_ge(S.t_vn, g + 1)
                A(g_B[g], bank[VB[g]], ACT.Copy).then_inc(S.a_vn, 1)
            act.wait_ge(S.t_o, 3)
            A(g_X[0], bank[6], ACT.Square).then_inc(S.a_osq, 1)
            for g in range(2):
                act.wait_ge(S.t_st, g + 1)
                A(g_Lt[g], bank[3 if g == 0 else 1], ACT.Copy).then_inc(S.a_st, 1)
                act.wait_ge(S.a_st, g + 1)
                out = [O["new_state_fwd"], O["new_state_bwd"]][g]
                act.dma_start(out[0, 0].rearrange("h k v -> k h v"), heads(g_Lt[g])).then_inc(S.stored, 16)
            act.wait_ge(S.t_o, 4)
            A(g_X[1], bank[0], ACT.Square).then_inc(S.a_osq, 1)
            for t in range(NB):
                act.wait_ge(S.t_os, NB + t + 1)
                inv_root(g_X[2 + t], bank[4 + t], 1.0 / P, S.a_ors, NB + t + 1)

            def moe(l):
                act.wait_ge(S.v_x, l + 1)
                norm(2 * l + 2, sqm, 5, l, 3 * KT)
                if l == 0:
                    act.dma_start(wsp[:, :, :], I["w_spatial"][0].rearrange("g p q -> p g q")).then_inc(S.ld_odd, 16)
                    act.dma_start(bsp, I["b_spatial"].rearrange("a g p -> a (g p)")).then_inc(S.ld_odd, 16)
                    act.dma_start(lng, I["sgu_ln_g"][0].partition_broadcast(P)).then_inc(S.ld_odd, 16)
                    act.dma_start(lnb, I["sgu_ln_b"][0].partition_broadcast(P)).then_inc(S.ld_odd, 16)
                for n in (0, 2):
                    act.wait_ge(S.t_hr, 4 * l + n + 1)
                    tokens_row(n, A).then_inc(S.a_hr, 1)
                act.wait_ge(S.v_rexp, 2 * l + 1)
                A(rs[:, 8:16], rs[:, 8:16], ACT.Exp).then_inc(S.a_rexp, 1)
                act.wait_ge(S.v_rexp, 2 * l + 2)
                A(rs[:, 24:26], rs[:, 24:26], ACT.Exp).then_inc(S.a_rexp, 1)

            def tokens_row(n, op):
                t, half = n // 2, n % 2
                return op(hrow[:, t, :, half * 64:half * 64 + 64],
                          bank[1 + n % 3].rearrange("p (a k) -> p k a", k=KT), ACT.Copy)

            def moe_experts(l):
                n0, q0 = l * PAIRS, l * (PAIRS + 1)
                act.wait_ge(S.g_set, 2)
                A(yr[:, 0:4, :], bcast_mid(ones, 4), ACT.Copy, scale=0.0).then_inc(S.m_yr0, 1)
                act.wait_ge(S.m_gat, 2 * q0 + 2)
                A(xg[:, 4:8, :], heads(bank[0]), ACT.Copy).then_inc(S.m_xg1, 1)
                with act.Fori(0, PAIRS // 2) as i:
                    for u in range(2):
                        n, q = n0 + u, q0 + u
                        c = moe_at[l] + 3 * u
                        act.wait_ge(S.used, i * 6 + (c + 2))
                        A(sg, bank[0][:, 0:FE], ACT.Silu).then_inc(S.m_sg, 1)
                        act.wait_ge(S.m_turn, i * 2 + (n + 1))
                        A(turned, heads(bank[0]), ACT.Copy).then_inc(S.m_td, 1)
                        act.wait_ge(S.m_gat, i * 4 + (2 * q + 4))
                        A(xg[:, 4:8, :], heads(bank[0]), ACT.Copy).then_inc(S.m_xg1, 1)
                        act.wait_ge(S.m_dn, i * 2 + (n + 1))
                        A(yr[:, 0:4, :], heads(bank[1]), ACT.Copy).then_inc(S.m_yr0, 1)

            def moe_further(l):
                f = FS[l]
                act.wait_ge(S.v_route, l + 1)
                n = act.value_load(route_i[0:1, l, 0:1], min_val=0, max_val=OVF // 2)
                with act.If(n > 0):
                    with act.Fori(0, n) as i:
                        act.wait_ge(f.f_pe, i * 6 + 3)
                        A(xg[:, 4:8, :], heads(bank[0]), ACT.Copy).then_inc(f.f_act, 1)
                        act.wait_ge(f.f_pe, i * 6 + 4)
                        A(sg, bank[0][:, 0:FE], ACT.Silu).then_inc(f.f_act, 1)
                        act.wait_ge(f.f_pe, i * 6 + 5)
                        A(turned, heads(bank[0]), ACT.Copy).then_inc(f.f_act, 1)
                        act.wait_ge(f.f_pe, i * 6 + 6)
                        A(yr[:, 0:4, :], heads(bank[1]), ACT.Copy).then_inc(f.f_act, 1)
                with act.Else():
                    act.nop()

            moe(0)
            moe_experts(0)
            moe_further(0)

            act.wait_ge(S.v_y, 1)
            norm(3, sqo, 1, 1, 0)
            for b in range(4):
                if b % 2 == 0:
                    act.wait_ge(S.t_u, b // 2 + 1)
                else:
                    act.wait_ge(S.used, index[("in1", b // 2)] + 1)
                A(uT[:, 2 * b:2 * b + 2, :].rearrange("p k n -> p (k n)"), bank[b], ACT.Gelu_apprx_tanh).then_inc(S.a_gelu, 1)
            for n in range(4):
                j, t = n // 2, n % 2
                if t == 0:
                    act.wait_ge(S.t_v, j + 1)
                else:
                    act.wait_ge(S.used, index[("in1", 2 + j)] + 1)
                A(vtk[:, t, j * 512:(j + 1) * 512], bank[4 + n], ACT.Gelu_apprx_tanh).then_inc(S.a_gv, 1)
            act.wait_ge(S.t_ws, 1)
            A(wsT[:, :, :].rearrange("p g n -> p (g n)"), bank[0], ACT.Copy).then_inc(S.a_ws, 1)
            for t in range(NB):
                act.wait_ge(S.v_cen, t + 1)
                if t == 1:
                    act.wait_ge(S.a_sqv, 1)
                A(vsq, vtk[:, t, :], ACT.Square, accum_out=lns[:, t:t + 1]).then_inc(S.a_sqv, 1)
            act.wait_ge(S.a_sqv, 2)
            inv_root(lnr, lns, 1.0 / D, S.a_lnr, 1)

            moe(1)
            moe_experts(1)
            moe_further(1)

            act.wait_ge(S.v_y, 2)
            norm(5, sqf, 1, None, 0)
            for n in (1, 3):
                act.wait_ge(S.t_last, n + 1)
                A(yrow[:, n // 2, 512:1024], bank[2 + n], ACT.Copy).then_inc(S.a_fin, 1)

        @block.gpsimd
        def _(pool):
            pool.memset(zeros[:, :], 0.0).then_inc(S.g_set, 1)
            pool.memset(raw[:, :, :, 0:2].rearrange("p c t n -> p (c t) n"), 0.0)
            pool.memset(raw[:, :, :, P + 2:P + 4].rearrange("p c t n -> p (c t) n"), 0.0).then_inc(S.g_set, 1)
            for lev in range(1, LEVELS):
                for g in range(4):
                    if lev == 1:
                        pool.wait_ge(S.v_att, g + 1)
                    else:
                        pool.wait_ge(S.t_lx, (lev - 2) * 4 + g + 1)
                    nc.gpsimd.tensor_tensor(heads(g_B[g]), heads(g_Lt[g]), bcast_mid(level(g % 2, lev), H), ALU.mult).then_inc(S.g_bm, 1)

        @block.vector
        def _(dve):
            V = nc.vector
            chain = [0]

            def link(ins):
                chain[0] += 1
                ins.then_inc(S.v_chain, 1)
                dve.wait_ge(S.v_chain, chain[0])

            dve.wait_ge(S.t_vec, 1)
            V.tensor_copy(cols[:, :], bank[0][:, 0:NV]).then_inc(S.v_cols, 1)
            for b in (0, 1):
                dve.wait_ge(S.t_x, b + 1)
                V.tensor_copy(xT[:, b * 4:b * 4 + 4, 0, :], heads(bank[1 + b])).then_inc(S.v_xt, 1)
            dve.wait_ge(S.v_cols, 1)

            def modulation(g):
                dve.wait_ge(S.t_mod, g + 1)
                a = g * 16
                V.tensor_tensor(modT[:, a:a + 16, :].rearrange("p (j m) t -> p j m t", m=4),
                                bank[6].rearrange("p (j m x) -> p j m x", j=4, m=4)[:, :, :, 0:NB],
                                cols[:, V_BMOD + a:V_BMOD + a + 16].rearrange("p (j m) -> p j m", m=4).unsqueeze(3).to_broadcast([P, 4, 4, NB]),
                                ALU.add).then_inc(S.v_mod, 1)

            def gain(n, l, at, norm_col):
                V.scalar_tensor_tensor(mulA[:, n, :, :], modT[:, l * MT + at:l * MT + at + KT, :], 1.0,
                                       bcast_last(cols[:, norm_col:norm_col + KT], NB), ALU.add, ALU.mult).then_inc(S.v_a, 1)

            modulation(0)
            dve.wait_ge(S.v_mod, 1)
            gain(0, 0, KT, V_NMIX)

            def norm(n, l, shift):
                dve.wait_ge(S.a_rstd, n)
                V.tensor_tensor(hT[:, :, :, :].rearrange("p k t n -> p k (t n)"), xT[:, :, :, :].rearrange("p k t n -> p k (t n)"),
                                bcast_mid(rstd[:, :], KT), ALU.mult).then_inc(S.v_xn, 1)
                dve.wait_ge(S.v_xn, n)
                dve.wait_ge(S.v_a, 1 if n == 1 else 4)
                for k in range(KT):
                    last = V.tensor_scalar(hT[:, k, 0, :], hT[:, k, 0, :], mulA[:, n - 1, k, 0:1],
                                           modT[:, l * MT + shift + k, 0:1], ALU.mult, ALU.add)
                last.then_inc(S.v_h, 1)

            norm(1, 0, 0)

            for n in range(3):
                dve.wait_ge(S.t_qkv, n + 1)
                V.tensor_copy(qkvt[:, 0, n * WA:(n + 1) * WA], bank[2 * n]).then_inc(S.v_qkv, 1)
            dve.wait_ge(S.g_set, 2)
            for u in (0, 2, 4):
                dve.wait_ge(S.t_cv, u // 2 + 1)
                V.tensor_copy(raw[:, 2 * u:2 * u + 2, :, 2:P + 2].rearrange("p c t n -> p (c t) n"),
                              bank[u].rearrange("p (c n) -> p c n", n=P)).then_inc(S.v_cv, 1)

            dve.wait_ge(S.a_qkv, 2)
            qk = qkvt[:, 1, 0:2 * WA]
            link(V.tensor_tensor(rtmp.rearrange("p (a n) -> p a n", n=DH), qk.rearrange("p (a n) -> p a n", n=DH),
                                 bcast_mid(const[:, C_COS:C_COS + DH], 16), ALU.mult))
            sinv = const[:, C_SIN:C_SIN + DH].rearrange("p (x s f) -> p x s f", x=2, s=2)
            qv = qk.rearrange("p (a x s f) -> p a x s f", x=2, s=2, f=16)
            rv = rq.rearrange("p (a x s f) -> p a x s f", x=2, s=2, f=16)
            for s in range(2):
                last = V.tensor_tensor(rv[:, :, :, s, :], qv[:, :, :, 1 - s, :],
                                       sinv[:, :, s, :].unsqueeze(1).to_broadcast([P, 16, 2, 16]), ALU.mult)
            link(last)
            V.tensor_tensor(rq, rq, rtmp, ALU.add).then_inc(S.v_rope, 1)

            dve.wait_ge(S.t_ab, 1)
            V.tensor_copy(ab, bank[2][:, 0:32]).then_inc(S.v_ab, 1)
            dve.wait_ge(S.v_ab, 1)
            dve.wait_ge(S.ld_small, 16 * 5)
            abv = ab.rearrange("p (t d w h) -> p t d w h", t=2, d=2, w=2)
            g4 = t16a.rearrange("p (t d h) -> p t d h", t=2, d=2)
            link(V.tensor_tensor(g4, abv[:, :, :, 0, :],
                                 dtb.rearrange("p (d h) -> p d h", d=2).unsqueeze(1).to_broadcast([P, 2, 2, H]), ALU.add))
            link(V.tensor_scalar(t16b, t16a, 0.0, None, ALU.max))
            link(V.scalar_tensor_tensor(t16a, t16a, -1.0, t16a, ALU.mult, ALU.min))
            V.tensor_scalar(beta.rearrange("p (t d h) -> p t d h", t=2, d=2), abv[:, :, :, 1, :], -80.0, None, ALU.max)
            link(V.tensor_tensor(lamq, lamq, lamk, ALU.mult))
            V.tensor_reduce(lame, lamq.rearrange("p (a n) -> p a n", a=2), AX.X, ALU.add).then_inc(S.v_abx, 1)
            dve.wait_ge(S.a_ab, 1)
            link(V.tensor_tensor(t16a, t16a, t16b, ALU.add))
            V.scalar_tensor_tensor(gdec.rearrange("p (t x) -> p t x", t=2), t16a.rearrange("p (t x) -> p t x", t=2), -1.0,
                                   bcast_mid(alog, 2), ALU.mult, ALU.mult)
            link(V.tensor_scalar(beta, beta, 1.0, None, ALU.add))
            link(V.reciprocal(beta, beta))
            V.tensor_scalar(subl, cols[:, V_SUB:V_SUB + 1], 1.0 - LAM_INIT, None, ALU.mult)
            V.scalar_tensor_tensor(lamc, lame[:, 0:1], LAM_INIT, lame[:, 1:2], ALU.add, ALU.subtract).then_inc(S.v_gd, 1)

            modulation(1)
            modulation(2)
            for t in range(NB):
                dve.wait_ge(S.t_sc, t + 1)
                w = P * (1 + t)
                sc = psum[:, 0:2, :] if t == 0 else psum[:, 2:6, :]
                sc = sc.rearrange("p b (h n) -> p (b h) n", n=w)
                link(V.tensor_reduce(smx, sc, AX.X, ALU.max))
                if t == 1:
                    dve.wait_ge(S.t_pt, 1)
                V.tensor_tensor(expS[:, :, 0:w], sc, bcast_last(smx, w), ALU.subtract).then_inc(S.v_sub, 1)
                dve.wait_ge(S.a_exp, t + 1)
                link(V.tensor_reduce(ssm, expS[:, :, 0:w], AX.X, ALU.add))
                link(V.reciprocal(ssm, ssm))
                link(V.tensor_scalar(ssm[:, H:], ssm[:, H:], lamc, None, ALU.mult))
                link(V.tensor_tensor(expS[:, :, 0:w], expS[:, :, 0:w], bcast_last(ssm, w), ALU.mult))
                V.tensor_tensor(expS[:, 0:H, 0:w], expS[:, 0:H, 0:w], expS[:, H:, 0:w], ALU.subtract).then_inc(S.v_p, 1)

            modulation(3)
            modulation(4)
            dve.wait_ge(S.a_cv, 3)
            dve.wait_ge(S.v_cv, 3)
            for j in range(CONV_K):
                for ch in range(12):
                    tap = cols[:, V_CONV + 12 * j + ch:V_CONV + 12 * j + ch + 1]
                    src = raw[:, ch, :, j:j + P]
                    if j == 0:
                        ins = V.tensor_scalar(convT[:, ch, :, :], src, tap, None, ALU.mult)
                    else:
                        dve.wait_ge(S.v_conv, 12 * (j - 1) + ch + 1)
                        ins = V.scalar_tensor_tensor(convT[:, ch, :, :], src, tap, convT[:, ch, :, :], ALU.mult, ALU.add)
                    ins.then_inc(S.v_conv, 1)

            for t in range(NB):
                dve.wait_ge(S.a_ors, t + 1)
                V.scalar_tensor_tensor(hT[:, 0:H, t, :], heads(bank[1 + 3 * t]), subl, heads(ors[t]), ALU.mult, ALU.mult).then_inc(S.v_mixed, 1)
            modulation(5)
            dve.wait_ge(S.v_mod, 6)
            gain(1, 0, 4 * KT, V_NFFN)
            gain(2, 1, KT, V_NMIX + KT)
            gain(3, 1, 4 * KT, V_NFFN + KT)

            dve.wait_ge(S.a_l2, 1)
            qn = convT[:, 0:H, :, :].rearrange("p h t n -> p (h t n)")
            kn = convT[:, H:2 * H, :, :].rearrange("p h t n -> p (h t n)")
            rl = sqx.rearrange("p k n -> p (k n)")
            V.scalar_tensor_tensor(qn, qn, P ** -0.5, rl[:, 0:1024], ALU.mult, ALU.mult)
            V.tensor_tensor(kn, kn, rl[:, 1024:2048], ALU.mult).then_inc(S.v_l2, 1)
            dve.wait_ge(S.t_gc, 1)
            V.tensor_copy(gcc, bank[6][:, 0:16]).then_inc(S.v_gc, 1)
            dve.wait_ge(S.v_gc, 1)
            for pair in range(2):
                for g in (2 * pair, 2 * pair + 1):
                    d = g % 2
                    b = 3 * d
                    if g == 0:
                        dve.wait_ge(S.v_l2, 1)
                        dve.wait_ge(S.stored, 16 * 2)
                    dve.wait_ge(S.t_gcb, g + 1)
                    if g < 2:
                        e = P - 1 if d == 0 else 0
                        V.tensor_copy(gll[:, g * H:(g + 1) * H], heads(bank[b])[:, :, e])
                    link(V.tensor_tensor(heads(g_D[g]), heads(bank[b]), bcast_last(gcc[:, g * H:(g + 1) * H], P), ALU.subtract))
                    V.tensor_tensor(heads(g_D[g]), heads(g_D[g]), bcast_mid(tri[d], H), ALU.mult).then_inc(S.v_dd, 1)
                for g in (2 * pair, 2 * pair + 1):
                    t, d = g // 2, g % 2
                    b = 3 * d
                    dve.wait_ge(S.a_dec, g + 1)
                    link(V.tensor_tensor(heads(g_D[g]), heads(g_D[g]), bcast_mid(tri[d], H), ALU.mult))
                    dve.wait_ge(S.t_kk, g + 1)
                    link(V.tensor_tensor(g_Lt[g], bank[b + 2], g_D[g], ALU.mult))
                    link(V.tensor_tensor(g_Lt[g], bank[b + 1], g_Lt[g], ALU.mult))
                    link(V.tensor_tensor(heads(g_DT[g]), heads(g_Lt[g]), bcast_mid(level(d, 0), H), ALU.mult))
                    V.tensor_tensor(heads(g_DT[g]), bcast_mid(ident, H), heads(g_DT[g]), ALU.subtract).then_inc(S.v_dt0, 1)
                    if g >= 2:
                        dve.wait_ge(S.a_qg, g - 1)
                        V.tensor_tensor(heads(g_q[g]), heads(g_q[g]), convT[:, 0:H, t, :], ALU.mult)
                    dve.wait_ge(S.t_qk, g + 1)
                    V.tensor_tensor(g_att[g], bank[b], g_D[g], ALU.mult).then_inc(S.v_att, 1)
                if pair == 0:
                    V.tensor_tensor(ekd, gll[:, 0:8], gcc[:, 0:8], ALU.subtract).then_inc(S.v_gll, 1)
            for lev in range(1, LEVELS):
                for g in range(4):
                    b = 3 * (g % 2)
                    dve.wait_ge(S.t_ld, (lev - 1) * 4 + g + 1)
                    if lev == 1:
                        dve.wait_ge(S.a_d0, g + 1)
                    if lev < LEVELS - 1:
                        V.tensor_tensor(g_D[g], g_D[g], bank[b + 1], ALU.subtract)
                    V.tensor_tensor(g_DT[g], g_DT[g], bank[b + 2], ALU.subtract).then_inc(S.v_lv, 1)
            dve.wait_ge(S.a_at, 8)
            dve.wait_ge(S.a_egc, 1)
            for g in range(4):
                t = g // 2
                if t == 0:
                    V.tensor_tensor(heads(g_X[g]), heads(vtok[:, 0, :]), bcast_last(beta[:, g * H:(g + 1) * H], P), ALU.mult).then_inc(S.v_r, 1)
                else:
                    dve.wait_ge(S.t_ks, g - 1)
                    link(V.tensor_tensor(heads(g_X[g]), heads(bank[3 * (g % 2)]), bcast_last(egc[:, g * H:(g + 1) * H], P), ALU.mult))
                    link(V.tensor_tensor(g_X[g], vtok[:, 1, :], g_X[g], ALU.subtract))
                    V.tensor_tensor(heads(g_X[g]), heads(g_X[g]), bcast_last(beta[:, g * H:(g + 1) * H], P), ALU.mult).then_inc(S.v_r, 1)
            dve.wait_ge(S.a_kd, 1)
            for g in range(2):
                V.tensor_tensor(heads(g_D[g]), heads(ktok), bcast_last(ekd[:, g * H:(g + 1) * H], P), ALU.mult).then_inc(S.v_kd, 1)
            for t in range(NB):
                dve.wait_ge(S.a_ors, NB + t + 1)
                link(V.scalar_tensor_tensor(g_X[t], bank[6 if t == 0 else 0], cols[:, V_DN:V_DN + 1], g_X[2 + t], ALU.mult, ALU.mult))
                V.tensor_tensor(hT[:, H:2 * H, t, :], heads(g_X[t]), gateT[:, :, t, :], ALU.mult).then_inc(S.v_mixed, 1)

            def residual(name, l, n0):
                for b in range(4):
                    if b % 2 == 0:
                        dve.wait_ge(S.t_wo, n0 + b // 2 + 1)
                    else:
                        dve.wait_ge(S.used, index[(name, b // 2)] + 1)
                    last = add_scaled(bank[b], b, l * MT + 2 * KT)
                last.then_inc(S.v_x, 1)

            def add_scaled(src, b, at):
                for m in (2 * b, 2 * b + 1):
                    for t in range(NB):
                        o = (m % 2) * T + t * P
                        ins = V.scalar_tensor_tensor(xT[:, m, t, :], src[:, o:o + P], modT[:, at + m, t:t + 1],
                                                     xT[:, m, t, :], ALU.mult, ALU.add)
                return ins

            residual("out0", 0, 0)

            def moe(l):
                norm(2 * l + 2, l, 3 * KT)
                dve.wait_ge(S.t_lg, l + 1)
                dve.wait_ge(S.stored, 16 * 4)
                link(V.tensor_tensor(lg, bank[0][:, 0:72].rearrange("p (t n) -> p t n", t=2),
                                     brt[:, l, :].unsqueeze(1).to_broadcast([P, 2, 36]), ALU.add))
                gm, gcm, gs, pg = rs[:, 0:2], rs[:, 2:4], rs[:, 4:6], rs[:, 6:8]
                ge = rs[:, 8:16].rearrange("p (t n) -> p t n", t=2)
                gl = lg[:, :, 0:NG]
                link(V.tensor_reduce(gm, gl, AX.X, ALU.max))
                V.tensor_tensor(ge, gl, bcast_last(gm, NG), ALU.subtract).then_inc(S.v_rexp, 1)
                link(V.tensor_tensor(gcls, gl, bcast_last(gm, NG), ALU.is_equal))
                link(V.tensor_tensor(gcls, gcls, bcast_mid(const[:, C_G4:C_G4 + NG], 2), ALU.mult))
                link(V.tensor_reduce(gcm, gcls, AX.X, ALU.max))
                link(V.tensor_tensor(gcls, gcls, bcast_last(gcm, NG), ALU.is_equal))
                link(V.tensor_scalar(gcls, gcls, BIG, -BIG, ALU.mult, ALU.add))
                e3 = em.rearrange("p t (g e) -> p t g e", g=NG)
                link(V.tensor_tensor(e3, lg[:, :, NG:].rearrange("p t (g e) -> p t g e", g=NG),
                                     gcls.unsqueeze(3).to_broadcast([P, 2, NG, EG]), ALU.add))
                m1, m2, c1 = rs[:, 16:18], rs[:, 18:20], rs[:, 20:22]
                e32 = const[:, C_E32:C_E32 + NE]

                def first_of_max(src, m, oh):
                    link(V.tensor_reduce(m, src, AX.X, ALU.max))
                    link(V.tensor_tensor(cnd, src, bcast_last(m, NE), ALU.is_equal))
                    link(V.tensor_tensor(cnd, cnd, bcast_mid(e32, 2), ALU.mult))
                    link(V.tensor_reduce(c1, cnd, AX.X, ALU.max))
                    link(V.tensor_tensor(oh, cnd, bcast_last(c1, NE), ALU.is_equal))

                first_of_max(em, m1, oh1)
                link(V.scalar_tensor_tensor(em2.rearrange("p t e -> p (t e)"), oh1.rearrange("p t e -> p (t e)"), -3 * BIG,
                                            em.rearrange("p t e -> p (t e)"), ALU.mult, ALU.add))
                first_of_max(em2, m2, oh2)
                V.tensor_tensor(rs[:, 24:26], m2, m1, ALU.subtract).then_inc(S.v_rexp, 1)
                V.tensor_tensor(msk, oh1, oh2, ALU.add).then_inc(S.v_mask, 1)
                V.memset(pos[:, :, NE:], 0.0)
                V.memset(gat[:, :, NE:], 0.0)
                for n in (1, 3):
                    dve.wait_ge(S.t_hr, 4 * l + n + 1)
                    t, half = n // 2, n % 2
                    V.tensor_copy(hrow[:, t, :, half * 64:half * 64 + 64],
                                  bank[1 + n % 3].rearrange("p (a k) -> p k a", k=KT)).then_inc(S.v_hr, 1)
                dve.wait_ge(S.a_rexp, 2 * l + 1)
                link(V.tensor_reduce(gs, ge, AX.X, ALU.add))
                link(V.reciprocal(pg, gs))
                dve.wait_ge(S.a_rexp, 2 * l + 2)
                w1, w2 = rs[:, 28:30], rs[:, 30:32]
                link(V.tensor_scalar(w1, rs[:, 24:26], 1.0, None, ALU.add))
                link(V.reciprocal(w1, w1))
                link(V.tensor_tensor(w1, w1, pg, ALU.mult))
                link(V.tensor_tensor(w2, w1, rs[:, 24:26], ALU.mult))
                V.tensor_tensor(oh1, oh1, bcast_last(w1, NE), ALU.mult)
                link(V.tensor_tensor(oh2, oh2, bcast_last(w2, NE), ALU.mult))
                link(V.tensor_tensor(gat[:, :, 0:NE], oh1, oh2, ALU.add))
                dve.wait_ge(S.t_pos, l + 1)
                link(V.tensor_tensor(pos[:, :, 0:NE], bank[0][:, 0:64].rearrange("p (t e) -> p t e", t=2), msk, ALU.mult))
                V.tensor_copy(cnt, bank[0][:, 64:96]).then_inc(S.v_pos, 1)
                dve.wait_ge(S.v_pos, l + 1)
                link(V.tensor_scalar(nov, cnt, float(CAP), None, ALU.is_gt))
                for r in range(2, T // CAP):
                    link(V.scalar_tensor_tensor(nov, cnt, float(CAP * r), nov, ALU.is_gt, ALU.add))
                link(V.tensor_reduce(ovs[:, 0:1], nov, AX.X, ALU.add))
                link(V.tensor_scalar(ovs[:, 1:2], ovs[:, 0:1], 0.0, None, ALU.is_gt))
                for r in range(1, OVF // 2):
                    link(V.scalar_tensor_tensor(ovs[:, 1:2], ovs[:, 0:1], 2.0 * r, ovs[:, 1:2], ALU.is_gt, ALU.add))
                V.tensor_copy(route_i[0:1, l, 0:1], ovs[0:1, 1:2]).then_inc(S.v_route, 1)

            def one_hot(dst, positions):
                return V.tensor_tensor(dst.rearrange("p t (e s) -> p t e s", e=2),
                                       const[:, C_SLOT:C_SLOT + CAP].unsqueeze(1).unsqueeze(1).to_broadcast([P, 2, 2, CAP]),
                                       positions.unsqueeze(3).to_broadcast([P, 2, 2, CAP]), ALU.is_equal)

            def weighted(gates):
                return V.tensor_tensor(PG.rearrange("p t (e s) -> p t e s", e=2), Pm.rearrange("p t (e s) -> p t e s", e=2),
                                       gates.unsqueeze(3).to_broadcast([P, 2, 2, CAP]), ALU.mult)

            def hidden(ev):
                V.tensor_tensor(hid, bank[0][:, FE:2 * FE], sg, ALU.mult).then_inc(ev, 1)

            def moe_experts(l):
                n0, q0 = l * PAIRS, l * (PAIRS + 1)
                one_hot(Pm, pos[:, :, 0:2]).then_inc(S.m_p, 1)
                dve.wait_ge(S.m_p, 2 * q0 + 1)
                weighted(gat[:, :, 0:2]).then_inc(S.m_p, 1)
                V.memset(turned, 0.0)
                V.memset(yr[:, 4:8, :], 0.0).then_inc(S.m_yr1, 1)
                dve.wait_ge(S.m_gat, 2 * q0 + 1)
                V.tensor_copy(xg[:, 0:4, :], heads(bank[3])).then_inc(S.m_xg0, 1)
                with dve.Fori(0, PAIRS // 2) as i:
                    for u in range(2):
                        n, q = n0 + u, q0 + u
                        c = moe_at[l] + 3 * u
                        dve.wait_ge(S.m_gat, i * 4 + (2 * q + 2))
                        dve.wait_ge(S.m_p, i * 4 + (2 * q + 2))
                        one_hot(Pm, pos[:, :, bass.ds(i * 4 + (2 * u + 2), 2)]).then_inc(S.m_p, 1)
                        dve.wait_ge(S.m_sg, i * 2 + (n + 1))
                        hidden(S.m_hid)
                        dve.wait_ge(S.m_turn, i * 2 + (n + 1))
                        dve.wait_ge(S.m_p, i * 4 + (2 * q + 3))
                        weighted(gat[:, :, bass.ds(i * 4 + (2 * u + 2), 2)]).then_inc(S.m_p, 1)
                        dve.wait_ge(S.m_gat, i * 4 + (2 * q + 3))
                        V.tensor_copy(xg[:, 0:4, :], heads(bank[3])).then_inc(S.m_xg0, 1)
                        dve.wait_ge(S.used, i * 6 + (c + 3))
                        V.tensor_copy(yr[:, 4:8, :], heads(bank[2])).then_inc(S.m_yr1, 1)

            def moe_further(l):
                f = FS[l]
                dve.wait_ge(S.v_route, l + 1)
                n = dve.value_load(route_i[0:1, l, 0:1], min_val=0, max_val=OVF // 2)
                with dve.If(n > 0):
                    pre = [0]

                    def flink(ins):
                        pre[0] += 1
                        ins.then_inc(f.f_vpre, 1)
                        dve.wait_ge(f.f_vpre, pre[0])

                    a, b = nov, cumA
                    for sft in (1, 2, 4, 8, 16):
                        V.tensor_copy(b[:, 0:sft], a[:, 0:sft])
                        flink(V.tensor_tensor(b[:, sft:], a[:, sft:], a[:, 0:NE - sft], ALU.add))
                        a, b = b, (cumB if b is cumA else cumA)
                    upto = a
                    flink(V.tensor_tensor(lej, bcast_mid(upto, OVF), bcast_last(const[:, C_J8:C_J8 + OVF], NE), ALU.is_le))
                    ex, exc, rj, en = ovs[:, 8:16], ovs[:, 16:24], ovs[:, 24:32], ovs[:, 32:40]
                    flink(V.tensor_reduce(ex, lej, AX.X, ALU.add))
                    flink(V.tensor_tensor(tj, lej, bcast_mid(nov, OVF), ALU.mult))
                    flink(V.tensor_reduce(exc, tj, AX.X, ALU.add))
                    flink(V.tensor_tensor(rj, const[:, C_J8:C_J8 + OVF], exc, ALU.subtract))
                    flink(V.tensor_scalar(rj, rj, float(CAP), float(CAP), ALU.mult, ALU.add))
                    flink(V.tensor_scalar(en, ex, -1.0, float(NE), ALU.mult, ALU.add))
                    flink(V.tensor_tensor(lej, bcast_mid(const[:, C_E32:C_E32 + NE], OVF), bcast_last(en, NE), ALU.is_equal))
                    for t in range(NB):
                        flink(V.tensor_tensor(tj, lej, bcast_mid(pos[:, t, 0:NE], OVF), ALU.mult))
                        flink(V.tensor_reduce(pos2[:, t, :], tj, AX.X, ALU.add))
                        flink(V.tensor_tensor(tj, lej, bcast_mid(gat[:, t, 0:NE], OVF), ALU.mult))
                        flink(V.tensor_reduce(gat2[:, t, :], tj, AX.X, ALU.add))
                    flink(V.tensor_tensor(pos2, pos2, bcast_mid(rj, 2), ALU.subtract))
                    flink(V.tensor_scalar(ex, ex, float(NE - 1), None, ALU.min))
                    V.tensor_copy(route_i[0:1, l, 1:1 + OVF], ex[0:1, :]).then_inc(f.f_idx, 1)
                    dve.wait_ge(S.m_gat, 2 * (l + 1) * (PAIRS + 1))
                    with dve.Fori(0, n) as i:
                        dve.wait_ge(f.f_pe, i * 6 + 1)
                        one_hot(Pm, pos2[:, :, bass.ds(i * 2, 2)]).then_inc(f.f_dve, 1)
                        dve.wait_ge(f.f_dve, i * 5 + 1)
                        weighted(gat2[:, :, bass.ds(i * 2, 2)]).then_inc(f.f_dve, 1)
                        dve.wait_ge(f.f_pe, i * 6 + 2)
                        V.tensor_copy(xg[:, 0:4, :], heads(bank[3])).then_inc(f.f_dve, 1)
                        dve.wait_ge(f.f_act, i * 4 + 2)
                        hidden(f.f_dve)
                        dve.wait_ge(f.f_pe, i * 6 + 6)
                        V.tensor_copy(yr[:, 4:8, :], heads(bank[2])).then_inc(f.f_dve, 1)
                with dve.Else():
                    dve.nop()
                dve.wait_ge(S.t_fin, l + 1)
                for b in range(4):
                    last = add_scaled(bank[4 + b], b, l * MT + 5 * KT)
                last.then_inc(S.v_y, 1)

            moe(0)
            moe_experts(0)
            moe_further(0)

            norm(3, 1, 0)
            for t in range(NB):
                dve.wait_ge(S.a_gv, 3 + t)
                link(V.tensor_reduce(lnm[:, t:t + 1], vtk[:, t, :], AX.X, ALU.add))
                link(V.tensor_scalar(lnm[:, t:t + 1], lnm[:, t:t + 1], 1.0 / D, None, ALU.mult))
                V.tensor_scalar(vtk[:, t, :], vtk[:, t, :], lnm[:, t:t + 1], None, ALU.subtract).then_inc(S.v_cen, 1)
            dve.wait_ge(S.a_lnr, 1)
            dve.wait_ge(S.ld_odd, 16 * 4)
            for t in range(NB):
                link(V.scalar_tensor_tensor(vtk[:, t, :], vtk[:, t, :], lnr[:, t:t + 1], lng, ALU.mult, ALU.mult))
                V.tensor_tensor(vtk[:, t, :], vtk[:, t, :], lnb, ALU.add).then_inc(S.v_ln, 1)
            for n in range(4):
                t, half = n // 2, n % 2
                dve.wait_ge(S.t_mx, n + 1)
                V.tensor_tensor(hT[:, 4 * half:4 * half + 4, t, :], heads(bank[n]),
                                uT[:, 4 * half:4 * half + 4, t * P:(t + 1) * P], ALU.mult).then_inc(S.v_mix, 1)
            residual("out1", 1, 2)
            moe(1)
            moe_experts(1)
            moe_further(1)

            dve.wait_ge(S.a_rstd, 5)
            for k in range(KT):
                last = V.scalar_tensor_tensor(hT[:, k, :, :].rearrange("p t n -> p (t n)"), xT[:, k, :, :].rearrange("p t n -> p (t n)"),
                                              cols[:, V_FIN + k:V_FIN + k + 1], rstd[:, :], ALU.mult, ALU.mult)
            last.then_inc(S.v_last, 1)
            for t in range(NB):
                dve.wait_ge(S.t_last, 2 * t + 1)
                V.tensor_copy(yrow[:, t, 0:512], bank[2 + 2 * t]).then_inc(S.v_fin, 1)


_INS = ["x_prompt", "x_sample", "cache_k", "cache_v", "state_fwd", "state_bwd", "c", "c_ctx", "norm_mix", "norm_ffn",
        "w_mod", "b_mod", "w_in_even", "conv_w", "a_log", "dt_bias", "delta_norm", "lam_q", "lam_k", "subln",
        "w_out_even", "w_in_odd", "sgu_ln_g", "sgu_ln_b", "w_spatial", "b_spatial", "w_out_odd", "w_router_group",
        "b_router_group", "w_router_expert", "b_router_expert", "w_exp_gate", "w_exp_up", "w_exp_down", "final_norm"]
_OUTS = {"y_prompt": (1, P, D), "y_sample": (1, P, D), "new_cache_k": (1, 1, P, H, P), "new_cache_v": (1, 1, P, H, P),
         "new_state_fwd": (1, 1, H, P, P), "new_state_bwd": (1, 1, H, P, P)}


def kernel(**inputs):
    import concourse.bacc as bacc
    from concourse.bass_utils import run_bass_kernel_spmd as run

    nc = bacc.Bacc("TRN2", target_bir_lowering=False, num_devices=1)
    arrays = {f"in_{n}": np.ascontiguousarray(inputs[n]) for n in _INS}
    arrays["in_consts"] = shape_constants()
    ins = {n[3:]: nc.dram_tensor(n, a.shape, mybir.dt.from_np(a.dtype), kind="ExternalInput").ap() for n, a in arrays.items()}
    outs = {n: nc.dram_tensor(f"out_{n}", s, F32, kind="ExternalOutput").ap() for n, s in _OUTS.items()}
    build(nc, ins, outs)
    r = run(nc, [arrays], core_ids=[0])
    return tuple(r.results[0][f"out_{n}"] for n in _OUTS)
```

```python
import numpy as np
from contextlib import ExitStack

import concourse.bass as bass
from concourse import mybir

F32 = mybir.dt.float32
I32 = mybir.dt.int32
BF16 = mybir.dt.bfloat16
ALU = mybir.AluOpType
ACT = mybir.ActivationFunctionType
AX = mybir.AxisListType

P = 128
D = 1024
KT = D // P
NB = 2
T = NB * P
DEPTH = 2
N_MOD = 6
MT = N_MOD * KT
EPS = 1e-6
H = 4
DH = 64
WA = H * P
LAM_INIT = 0.8 - 0.6
CONV_K = 5
IN_EVEN = 3 * WA + 4 * WA + 4 * H
NG, EG = 4, 8
NE = NG * EG
FE = 256
CAP = 64
PAIRS = NE // 2
LEVELS = 7
RING = 6
SLOT = 4096
BIG = 1e30
OVF = 8

SQ0 = [None, 0, 1, 5, 9, 13]
MS0 = [None, 0, 1, 3, 4, 6]

C_ID, C_ONE, C_TRI = 0, P, 2 * P
C_SLOT = C_TRI + 2 * P
C_COS = C_SLOT + CAP
C_SIN = C_COS + DH
C_G4 = C_SIN + DH
C_E32 = C_G4 + NG
C_J8 = C_E32 + NE
C_EPS = C_J8 + OVF
C_LEV = C_EPS + 2
NC_COLS = C_LEV + 2 * LEVELS * P

V_BMOD = 0
V_NMIX = V_BMOD + DEPTH * MT
V_COND = V_NMIX + DEPTH * KT
V_NFFN = V_COND + NB * KT
V_FIN = V_NFFN + DEPTH * KT
V_CONV = V_FIN + KT
V_DN = V_CONV + CONV_K * 3 * H
V_SUB = V_DN + 1
NV = V_SUB + 1


def shape_constants():
    c = np.zeros((P, NC_COLS), np.float32)
    r = np.arange(P)[:, None]
    q = np.arange(P)[None, :]
    c[:, C_ID:C_ID + P] = r == q
    c[:, C_ONE:C_ONE + P] = 1
    c[:, C_TRI:C_TRI + P] = r <= q
    c[:, C_TRI + P:C_TRI + 2 * P] = r >= q
    for lev in range(LEVELS):
        s = 1 << lev
        m = (r // (2 * s) == q // (2 * s)) & (r % (2 * s) < s) & (q % (2 * s) >= s)
        o = C_LEV + lev * P
        c[:, o:o + P] = m
        c[:, o + LEVELS * P:o + LEVELS * P + P] = m.T
    c[:, C_SLOT:C_SLOT + CAP] = np.arange(1, CAP + 1)
    freqs = DH // 4
    tok = np.arange(P)
    pos = np.stack([tok // 64, tok % 64], -1).astype(np.float32)
    inv = (10000.0 ** (-np.arange(freqs, dtype=np.float32) / freqs)).astype(np.float32)
    ang = pos[:, :, None] * inv
    cos, sin = np.cos(ang), np.sin(ang)
    c[:, C_COS:C_COS + DH] = np.stack([cos, cos], 2).reshape(P, DH)
    c[:, C_SIN:C_SIN + DH] = np.stack([-sin, sin], 2).reshape(P, DH)
    c[:, C_G4:C_G4 + NG] = NG - np.arange(NG)
    c[:, C_E32:C_E32 + NE] = NE - np.arange(NE)
    c[:, C_J8:C_J8 + OVF] = np.arange(OVF)
    c[:, C_EPS] = EPS
    c[:, C_EPS + 1] = 1.0
    return c


class Semaphores:

    def __init__(self, sem):
        self.a_ab = sem("a_ab")
        self.a_at = sem("a_at")
        self.a_chain = sem("a_chain")
        self.a_cv = sem("a_cv")
        self.a_d0 = sem("a_d0")
        self.a_dec = sem("a_dec")
        self.a_e1 = sem("a_e1")
        self.a_egc = sem("a_egc")
        self.a_exp = sem("a_exp")
        self.a_fin = sem("a_fin")
        self.a_gelu = sem("a_gelu")
        self.a_gv = sem("a_gv")
        self.a_h = sem("a_h")
        self.a_hr = sem("a_hr")
        self.a_kd = sem("a_kd")
        self.a_l2 = sem("a_l2")
        self.a_lnr = sem("a_lnr")
        self.a_lx = sem("a_lx")
        self.a_mrow = sem("a_mrow")
        self.a_ors = sem("a_ors")
        self.a_osq = sem("a_osq")
        self.a_pt = sem("a_pt")
        self.a_qg = sem("a_qg")
        self.a_qkv = sem("a_qkv")
        self.a_rexp = sem("a_rexp")
        self.a_rstd = sem("a_rstd")
        self.a_silu = sem("a_silu")
        self.a_silu_c = sem("a_silu_c")
        self.a_sq = sem("a_sq")
        self.a_sqc = sem("a_sqc")
        self.a_sqv = sem("a_sqv")
        self.a_st = sem("a_st")
        self.a_vn = sem("a_vn")
        self.a_ws = sem("a_ws")
        self.a_xt = sem("a_xt")
        self.g_bm = sem("g_bm")
        self.g_h = sem("g_h")
        self.g_s0 = sem("g_s0")
        self.g_set = sem("g_set")
        self.ld_attn = sem("ld_attn")
        self.ld_const = sem("ld_const")
        self.ld_levels = sem("ld_levels")
        self.ld_odd = sem("ld_odd")
        self.ld_router = sem("ld_router")
        self.ld_small = sem("ld_small")
        self.ld_state = sem("ld_state")
        self.ld_vec = sem("ld_vec")
        self.ld_x = sem("ld_x")
        self.m_dn = sem("m_dn")
        self.m_gat = sem("m_gat")
        self.m_hid = sem("m_hid")
        self.m_p = sem("m_p")
        self.m_sg = sem("m_sg")
        self.m_td = sem("m_td")
        self.m_turn = sem("m_turn")
        self.m_v = sem("m_v")
        self.m_xg0 = sem("m_xg0")
        self.m_xg1 = sem("m_xg1")
        self.m_yr0 = sem("m_yr0")
        self.m_yr1 = sem("m_yr1")
        self.stored = sem("stored")
        self.t_ab = sem("t_ab")
        self.t_at = sem("t_at")
        self.t_bb = sem("t_bb")
        self.t_cv = sem("t_cv")
        self.t_dt = sem("t_dt")
        self.t_fin = sem("t_fin")
        self.t_gc = sem("t_gc")
        self.t_gcb = sem("t_gcb")
        self.t_hr = sem("t_hr")
        self.t_kk = sem("t_kk")
        self.t_ks = sem("t_ks")
        self.t_l2 = sem("t_l2")
        self.t_last = sem("t_last")
        self.t_ld = sem("t_ld")
        self.t_lg = sem("t_lg")
        self.t_lx = sem("t_lx")
        self.t_mod = sem("t_mod")
        self.t_ms = sem("t_ms")
        self.t_mx = sem("t_mx")
        self.t_o = sem("t_o")
        self.t_os = sem("t_os")
        self.t_pos = sem("t_pos")
        self.t_pt = sem("t_pt")
        self.t_qk = sem("t_qk")
        self.t_qkv = sem("t_qkv")
        self.t_sc = sem("t_sc")
        self.t_st = sem("t_st")
        self.t_u = sem("t_u")
        self.t_v = sem("t_v")
        self.t_vec = sem("t_vec")
        self.t_vn = sem("t_vn")
        self.t_wo = sem("t_wo")
        self.t_ws = sem("t_ws")
        self.t_x = sem("t_x")
        self.used = sem("used")
        self.v_a = sem("v_a")
        self.v_ab = sem("v_ab")
        self.v_abx = sem("v_abx")
        self.v_att = sem("v_att")
        self.v_cen = sem("v_cen")
        self.v_chain = sem("v_chain")
        self.v_cols = sem("v_cols")
        self.v_conv = sem("v_conv")
        self.v_cv = sem("v_cv")
        self.v_dd = sem("v_dd")
        self.v_dt0 = sem("v_dt0")
        self.v_fin = sem("v_fin")
        self.v_gc = sem("v_gc")
        self.v_gd = sem("v_gd")
        self.v_gll = sem("v_gll")
        self.v_h = sem("v_h")
        self.v_kd = sem("v_kd")
        self.v_l2 = sem("v_l2")
        self.v_last = sem("v_last")
        self.v_ln = sem("v_ln")
        self.v_lv = sem("v_lv")
        self.v_mask = sem("v_mask")
        self.v_mix = sem("v_mix")
        self.v_mixed = sem("v_mixed")
        self.v_mod = sem("v_mod")
        self.v_p = sem("v_p")
        self.v_pos = sem("v_pos")
        self.v_qkv = sem("v_qkv")
        self.v_r = sem("v_r")
        self.v_rexp = sem("v_rexp")
        self.v_rope = sem("v_rope")
        self.v_route = sem("v_route")
        self.v_sub = sem("v_sub")
        self.v_x = sem("v_x")
        self.v_xn = sem("v_xn")
        self.v_xt = sem("v_xt")
        self.v_y = sem("v_y")


class FurtherSemaphores:

    def __init__(self, sem, l):
        self.f_act = sem(f"f_act{l}")
        self.f_dve = sem(f"f_dve{l}")
        self.f_idx = sem(f"f_idx{l}")
        self.f_pe = sem(f"f_pe{l}")
        self.f_v = sem(f"f_v{l}")
        self.f_vpre = sem(f"f_vpre{l}")
        self.f_w = sem(f"f_w{l}")


def build(nc, I, O):
    ctx = ExitStack()
    with ctx:
        def sem(name):
            return ctx.enter_context(nc.semaphore(name))

        S = Semaphores(sem)
        FS = [FurtherSemaphores(sem, l) for l in range(DEPTH)]
        full = [ctx.enter_context(nc.semaphore(f"slot_full{i}")) for i in range(RING)]

        def sb(name, shape, dt=F32):
            return ctx.enter_context(nc.sbuf_tensor(name, shape, dt))

        ring = sb("ring", [P, RING, SLOT])
        xT = sb("xT", [P, KT, NB, P])
        hT = sb("hT", [P, KT, NB, P])
        const = sb("const", [P, NC_COLS])
        cols = sb("cols", [P, NV])
        condT = sb("condT", [P, NB, KT])
        modT = sb("modT", [P, DEPTH * MT, NB])
        mulA = sb("mulA", [P, 2 * DEPTH, KT, NB])
        rstd = sb("rstd", [P, T])
        wab = sb("wab", [P, KT, 4 * H])
        wrt = sb("wrt", [P, DEPTH, KT, NG + NE])
        brt = sb("brt", [P, DEPTH, NG + NE])
        mrow = wrt[:, :, :, :].rearrange("p l k n -> p (l k n)")[:, 0:512]
        small = sb("small", [P, 512])
        route_i = sb("route_i", [1, DEPTH, 16], I32)
        scratch = sb("scratch", [P, 19552])
        zeros = sb("zeros", [32, 640], mybir.dt.bfloat16)
        psum = ctx.enter_context(nc.psum_tensor("psum", [P, 8, 512], F32))

        YR = 1 + PAIRS
        HR = [1, 4, 6, 7]

        ident = const[:, C_ID:C_ID + P]
        ones = const[:, C_ONE:C_ONE + P]
        tri = [const[:, C_TRI + d * P:C_TRI + d * P + P] for d in range(2)]
        epsc = const[:, C_EPS:C_EPS + 1]
        onec = const[:, C_EPS + 1:C_EPS + 2]

        def level(d, lev):
            o = C_LEV + (d * LEVELS + lev) * P
            return const[:, o:o + P]

        def part(at, shape):
            n = int(np.prod(shape))
            v = scratch[:, at:at + n]
            if len(shape) == 2:
                v = v.rearrange("p (a b) -> p a b", b=shape[1])
            elif len(shape) == 3:
                v = v.rearrange("p (a b c) -> p a b c", b=shape[1], c=shape[2])
            elif len(shape) == 4:
                v = v.rearrange("p (a b c d) -> p a b c d", b=shape[1], c=shape[2], d=shape[3])
            return v

        def bcast_mid(v, n):
            return v.unsqueeze(1).to_broadcast([P, n, v.shape[1]])

        def bcast_last(v, n):
            return v.unsqueeze(2).to_broadcast([P, v.shape[1], n])

        bank = [psum[:, b, :] for b in range(8)]

        def heads(v):
            return v.rearrange("p (h n) -> p h n", h=H)

        vec1 = part(0, (P,))
        vec2 = part(P, (P,))
        xin = part(2 * P, (NB, D))
        convT = part(0, (3 * H, NB, P))
        gateT = part(3072, (H, NB, P))
        ktok = part(4096, (H * P,))
        vtok = part(4608, (NB, H * P))
        E0 = 5632
        raw = part(E0, (3 * H, NB, P + 4))
        qkvt = part(E0 + 3168, (NB, 3 * WA))
        rq = part(E0 + 6240, (2 * WA,))
        rtmp = part(E0 + 7264, (2 * WA,))
        attT = part(E0 + 8288, (5, WA))
        ckv = part(E0 + 10848, (2, WA))
        expS = part(E0 + 11872, (2 * H, T))
        PT = part(E0 + 7264, (2, WA))
        sqx = part(E0 + 11872, (KT, T))
        osq = [part(E0 + 8288 + t * 2 * WA, (WA,)) for t in range(NB)]
        ors = [part(E0 + 8288 + t * 2 * WA + WA, (WA,)) for t in range(NB)]
        g_Lt = [part(E0 + g * 3072, (WA,)) for g in range(4)]
        g_att = [part(E0 + g * 3072 + 512, (WA,)) for g in range(4)]
        g_D = [part(E0 + g * 3072 + 1024, (WA,)) for g in range(4)]
        g_DT = [part(E0 + g * 3072 + 1536, (WA,)) for g in range(4)]
        g_X = [part(E0 + g * 3072 + 2048, (WA,)) for g in range(4)]
        g_B = [part(E0 + g * 3072 + 2560, (WA,)) for g in range(4)]
        g_q = [None, None, part(E0 + 12288, (WA,)), part(E0 + 12800, (WA,))]
        S0 = hT[:, H:2 * H, :, :].rearrange("p h t n -> p (h t n)").rearrange("p (d x) -> p d x", d=2)
        uT = part(0, (KT, T))
        vtk = part(2048, (NB, D))
        sqo = part(4096, (KT, T))
        vsq = part(6144, (D,))
        lng = part(14200, (D,))
        lnb = part(15224, (D,))
        wsp = part(16248, (4, P))
        wsT = part(16760, (4, P))
        bsp = part(17272, (4, P))
        hrow = part(0, (NB, KT, P))
        xg = part(2048, (KT, 2 * CAP))
        hid = part(3072, (FE,))
        sg = part(3328, (FE,))
        hidT = part(3584, (2, P))
        pgT = part(3840, (T,))
        yr = part(4608, (KT, P))
        y3 = scratch[:, 9856:9856 + 3 * D // 2].bitcast(BF16).rearrange("p (s k n) -> p s k n", s=3, k=KT)
        ohT = scratch[:, 11904:11904 + T // 2].bitcast(BF16)
        slot_gate = scratch[:, 11400:11401]
        h3 = [scratch[:, at:at + NB * D // 2].bitcast(BF16).rearrange("p (t k n) -> p t k n", t=NB, k=KT)
              for at in (12032, 13056, 17784)]
        Pm = scratch[:, 5888:6016].bitcast(BF16).rearrange("p (t s) -> p t s", t=NB)
        PG = part(6144, (NB, 2 * CAP))
        sqm = part(6400, (KT, T))
        R0 = 8448
        lg = part(R0, (NB, NG + NE))
        em = part(R0 + 72, (NB, NE))
        em2 = part(R0 + 136, (NB, NE))
        cnd = part(R0 + 200, (NB, NE))
        oh1 = part(R0 + 264, (NB, NE))
        oh2 = part(R0 + 328, (NB, NE))
        pos = part(R0 + 392, (NB, NE + 2))
        gat = part(R0 + 460, (NB, NE + 2))
        msk = part(R0 + 528, (NB, NE))
        rs = part(R0 + 592, (64,))
        cnt = part(R0 + 656, (NE,))
        nov = part(R0 + 688, (NE,))
        cumA = part(R0 + 720, (NE,))
        cumB = part(R0 + 752, (NE,))
        lej = part(R0 + 784, (OVF, NE))
        tj = part(R0 + 1040, (OVF, NE))
        ovs = part(R0 + 1296, (64,))
        pos2 = part(R0 + 1360, (NB, OVF))
        gat2 = part(R0 + 1376, (NB, OVF))
        gcls = part(R0 + 1392, (NB, NG))
        yrow = part(12000, (NB, D))
        sqf = part(14100, (KT, T))

        ab = small[:, 0:32]
        gdec = small[:, 32:48]
        beta = small[:, 48:64]
        t16a = small[:, 64:80]
        t16b = small[:, 80:96]
        alog = small[:, 96:104]
        dtb = small[:, 104:112]
        lamc = small[:, 112:113]
        lame = small[:, 114:116]
        subl = small[:, 116:117]
        gcc = small[:, 128:144]
        gll = small[:, 144:160]
        egc = small[:, 160:176]
        ekd = small[:, 176:184]
        lamq = small[:, 192:320]
        lamk = small[:, 320:448]
        smx = small[:, 448:456]
        ssm = small[:, 456:464]
        lnm = small[:, 464:466]
        lns = small[:, 466:468]
        lnr = small[:, 468:470]

        MODC = MT // 4
        stream = []

        def put(kind, *a):
            stream.append((kind,) + a)

        for j in range(4):
            put("mod", 0, j)
        for j in range(7):
            put("in0", j)
        for j in range(4, MODC):
            put("mod", 0, j)
        for j in range(MODC):
            put("mod", 1, j)
        for j in range(2):
            put("out0", j)
        moe_at = [len(stream)]
        stream += [("moe", 0)] * (3 * PAIRS)
        for j in (2, 3, 0, 1):
            put("in1", j)
        for j in range(2):
            put("out1", j)
        moe_at.append(len(stream))
        stream += [("moe", 1)] * (3 * PAIRS)
        index = {s: n for n, s in enumerate(stream) if s[0] != "moe"}

        wm = I["w_mod"].rearrange("l (k p) n -> l p k n", p=P)
        wi0 = I["w_in_even"][0].rearrange("(k p) n -> p k n", p=P)
        wi1 = I["w_in_odd"][0].rearrange("(k p) n -> p k n", p=P)
        wo0 = I["w_out_even"][0].rearrange("(k p) n -> p k n", p=P)
        wo1 = I["w_out_odd"][0].rearrange("(k p) n -> p k n", p=P)
        source = {"in0": wi0, "in1": wi1, "out0": wo0, "out1": wo1}

        def slot_kn(s):
            return ring[:, s, :].rearrange("p (k n) -> p k n", k=KT)

        def chunk_full(eng, name):
            c = index[name]
            eng.wait_ge(full[c % RING], 32 * (c // RING + 1))
            return c % RING

        block = ctx.enter_context(nc.Block())

        @block.sync
        def _(sp):
            def load(c, slot, halves):
                if c is not None and c >= RING:
                    sp.wait_ge(S.used, c - RING + 1)
                for dst, src in halves:
                    sp.dma_start(dst, src).then_inc(full[slot], 16)

            def moe_layer(l):
                wg = I["w_exp_gate"][l].rearrange("(i e) (p k) f -> i e p (k f)", e=4, k=KT)
                wu = I["w_exp_up"][l].rearrange("(i e) (p k) f -> i e p (k f)", e=4, k=KT)
                wd = I["w_exp_down"][l].rearrange("(i e) (a p) n -> i e p a n", e=4, a=2)
                with sp.Fori(0, PAIRS // 2) as i:
                    for u in range(2):
                        for e in range(2):
                            c = moe_at[l] + 3 * u + e
                            sp.wait_ge(S.used, i * 6 + (c - RING + 1))
                            s = c % RING
                            sp.dma_start(ring[:, s, 0:2048], wg[i, 2 * u + e]).then_inc(full[s], 16)
                            sp.dma_start(ring[:, s, 2048:4096], wu[i, 2 * u + e]).then_inc(full[s], 16)
                        c = moe_at[l] + 3 * u + 2
                        sp.wait_ge(S.used, i * 6 + (c - RING + 1))
                        s = c % RING
                        for e in range(2):
                            dst = ring[:, s, 2048 * e:2048 * e + 2048].rearrange("p (a n) -> p a n", a=2)
                            sp.dma_start(dst, wd[i, 2 * u + e]).then_inc(full[s], 16)

            def moe_further(l):
                f = FS[l]
                wg = I["w_exp_gate"][l].rearrange("e (p k) f -> e p (k f)", k=KT)
                wu = I["w_exp_up"][l].rearrange("e (p k) f -> e p (k f)", k=KT)
                wd = I["w_exp_down"][l].rearrange("e (a p) n -> e p a n", a=2)
                end = moe_at[l] + 3 * PAIRS
                sp.wait_ge(S.v_route, l + 1)
                n = sp.value_load(route_i[0:1, l, 0:1], min_val=0, max_val=OVF // 2)
                with sp.If(n > 0):
                    sp.wait_ge(f.f_idx, 1)
                    sp.wait_ge(S.used, end - RING + 3)
                    sp.sem_inc(f.f_pe, 1)
                    with sp.Fori(0, n) as i:
                        sp.wait_ge(f.f_pe, i * 6 + 1)
                        for e in range(2):
                            x = sp.value_load(route_i[0:1, l, bass.ds(i * 2 + (1 + e), 1)], min_val=0, max_val=NE - 1)
                            sp.dma_start(ring[:, (end + e) % RING, 0:2048], wg[x]).then_inc(f.f_w, 16)
                            sp.dma_start(ring[:, (end + e) % RING, 2048:4096], wu[x]).then_inc(f.f_w, 16)
                            dst = ring[:, (end + 2) % RING, 2048 * e:2048 * e + 2048].rearrange("p (a n) -> p a n", a=2)
                            sp.dma_start(dst, wd[x]).then_inc(f.f_w, 16)
                    sp.wait_ge(S.t_fin, l + 1)
                with sp.Else():
                    sp.nop()

            sp.dma_start(const[:, 0:C_LEV], I["consts"][:, 0:C_LEV]).then_inc(S.ld_const, 16)
            sp.dma_start(vec1[0:DEPTH * MT, :], I["b_mod"].rearrange("l (m p) -> (l m) p", p=P)).then_inc(S.ld_vec, 16)
            sp.dma_start(vec1[96:112, :], I["norm_mix"].rearrange("l (m p) -> (l m) p", p=P)).then_inc(S.ld_vec, 16)
            sp.dma_start(vec1[112:120, :], I["c_ctx"].rearrange("(m p) -> m p", p=P)).then_inc(S.ld_vec, 16)
            sp.dma_start(vec1[120:128, :], I["c"][0].rearrange("(m p) -> m p", p=P)).then_inc(S.ld_vec, 16)
            c = 0
            while c < len(stream):
                kind = stream[c][0]
                if kind == "moe":
                    moe_layer(stream[c][1])
                    moe_further(stream[c][1])
                    c += 3 * PAIRS
                    continue
                s = c % RING
                if kind == "mod":
                    _, l, j = stream[c]
                    src = wm[l][:, :, 512 * j:512 * j + 512]
                else:
                    j = stream[c][1]
                    src = source[kind][:, :, 512 * j:512 * j + 512]
                dst = slot_kn(s)
                load(c, s, [(dst[:, 0:4], src[:, 0:4]), (dst[:, 4:8], src[:, 4:8])])
                c += 1
            y = [O["y_prompt"][0], O["y_sample"][0]]
            for half in range(2):
                for t in range(NB):
                    sp.wait_ge([S.v_fin, S.a_fin][t], half + 1)
                    sp.dma_start(y[t][:, half * 512:half * 512 + 512], yrow[:, t, half * 512:half * 512 + 512]).then_inc(S.stored, 16)
            sp.wait_ge(S.stored, 16 * 8)

        @block.tensor
        def _(pe):
            mm = nc.tensor.matmul

            def used(ins):
                ins.then_inc(S.used, 1)

            pe.wait_ge(S.ld_const, 16)
            pe.wait_ge(S.ld_vec, 16 * 9)
            nc.tensor.transpose(bank[0][:, 0:P], vec1[:, :], ident)
            nc.tensor.transpose(bank[0][:, P:P + 86], vec2[0:86, :], const[0:86, C_ID:C_ID + 86]).then_inc(S.t_vec, 1)
            pe.wait_ge(S.ld_x, 32)
            for b in range(4):
                t, kh = b // 2, b % 2
                for k in range(4):
                    last = nc.tensor.transpose(bank[1 + b][:, k * P:(k + 1) * P],
                                               xin[:, t, (kh * 4 + k) * P:(kh * 4 + k + 1) * P], ident)
                last.then_inc(S.t_x, 1)

            def mod_chunk(l, j):
                s = chunk_full(pe, ("mod", l, j))
                w = slot_kn(s)
                g, at = l * MODC // 4 + j // 4, j % 4 * P
                if g > 0 and at == 0:
                    pe.wait_ge(S.a_mrow, g)
                for k in range(KT):
                    for m in range(4):
                        last = mm(bank[7][32 * m:32 * m + NB, at:at + P], condT[:, :, k], w[:, k, m * P:(m + 1) * P],
                                  start=(k == 0), stop=(k == KT - 1))
                used(last)

            def mod_turn(g):
                pe.wait_ge(S.a_mrow, g + 1)
                if g > 0:
                    pe.wait_ge(S.v_mod, g)
                for j in range(4):
                    last = nc.tensor.transpose(bank[6][:, j * P:(j + 1) * P], mrow[:, j * P:(j + 1) * P], ident)
                last.then_inc(S.t_mod, 1)

            pe.wait_ge(S.g_set, 1)
            mm(bank[7], zeros[:, 512:640], zeros[:, 0:512], start=True, stop=True)
            pe.wait_ge(S.a_silu_c, 1)
            def mean_square(n, sq, b):
                for k in range(KT):
                    if n == 1:
                        if k == 0:
                            pe.wait_ge(S.a_sq, 1)
                    elif k % 2 == 0:
                        pe.wait_ge(S.a_sq, SQ0[n] + k // 2 + 1)
                    last = mm(bank[b][:, 0:T], ones, sq[:, k, :], start=(k == 0), stop=(k == KT - 1))
                last.then_inc(S.t_ms, 1)

            def mean_square_of(n, sq, b, t):
                for k in range(KT):
                    if k % 4 == 0:
                        pe.wait_ge(S.a_sq, SQ0[n] + 2 * t + k // 4 + 1)
                    last = mm(bank[b][:, t * P:(t + 1) * P], ones, sq[:, k, t * P:(t + 1) * P], start=(k == 0), stop=(k == KT - 1))
                last.then_inc(S.t_ms, 1)

            def h_ready(n, i):
                pe.wait_ge(S.v_h, 2 * (n - 1) + i + 1)
                pe.wait_ge(S.a_h, 2 * (n - 1) + i + 1)

            mod_chunk(0, 0)
            mod_chunk(0, 1)
            mean_square(1, sqx, 5)
            mod_chunk(0, 2)
            mod_chunk(0, 3)
            mod_turn(0)

            for n in range(3):
                s = chunk_full(pe, ("in0", n))
                w = slot_kn(s)
                for t in range(NB):
                    for k in range(KT):
                        if n == 0 and t == 0 and k % 4 == 0:
                            h_ready(1, k // 4)
                        last = mm(bank[2 * n + t], hT[:, k, t, :], w[:, k, :], start=(k == 0), stop=(k == KT - 1))
                    if t == 0:
                        last.then_inc(S.t_qkv, 1)
                used(last)
            for u in range(8):
                b = u if u < 6 else u - 6
                if u < 6:
                    pe.wait_ge(S.v_qkv if u % 2 == 0 else S.a_qkv, u // 2 + 1)
                else:
                    pe.wait_ge(S.v_cv if u == 6 else S.a_cv, 1)
                if u % 2 == 0:
                    s = chunk_full(pe, ("in0", 3 + u // 2))
                w = slot_kn(s)
                for c2 in range(2):
                    m = (u % 2) * 2 + c2
                    for k in range(KT):
                        last = mm(bank[b][:, c2 * T:(c2 + 1) * T], w[:, k, m * P:(m + 1) * P], hT[:, k, :, :],
                                  start=(k == 0), stop=(k == KT - 1))
                if u % 2 == 1:
                    used(last)
                else:
                    last.then_inc(S.t_cv, 1)
            pe.wait_ge(S.ld_small, 16 * 5)
            pe.wait_ge(S.v_mod, 1)
            for t in range(NB):
                for k in range(KT):
                    last = mm(bank[6][:, t * 16:t * 16 + 16], hT[:, k, t, :], wab[:, k, :],
                              start=(k == 0), stop=(k == KT - 1))
            last.then_inc(S.t_ab, 1)
            pe.wait_ge(S.a_cv, 5)
            for n in range(5):
                if n == 2:
                    pe.wait_ge(S.v_cv, 2)
                    pe.wait_ge(S.v_rope, 1)
                if n == 4:
                    pe.wait_ge(S.ld_attn, 32)
                    pe.wait_ge(S.v_cv, 3)
                src = [qkvt[:, 0, 0:WA], qkvt[:, 0, WA:2 * WA], rq[:, 0:WA], rq[:, WA:2 * WA], ckv[:, 0, :]][n]
                for h in range(H):
                    last = nc.tensor.transpose(bank[n][:, h * P:(h + 1) * P], src[:, h * P:(h + 1) * P], ident)
                last.then_inc(S.t_at, 1)

            for j in range(4, 8):
                mod_chunk(0, j)

            def scores(t):
                pe.wait_ge(S.a_at, 5)
                for hh in range(2 * H):
                    h, half = hh // 2, hh % 2
                    r = slice(half * DH, half * DH + DH)
                    q = attT[r, 2 * t, h * P:(h + 1) * P]
                    keys = [attT[r, 2 * t + 1, h * P:(h + 1) * P]]
                    if t == 1:
                        keys.append(attT[r, 4, h * P:(h + 1) * P])
                    for n, k in enumerate(keys):
                        if t == 0:
                            o = bank[half][:, h * P:(h + 1) * P]
                        else:
                            o = bank[2 + 2 * half + h // 2][:, (h % 2) * T + n * P:(h % 2) * T + (n + 1) * P]
                        last = mm(o, q, k, start=True, stop=True)
                last.then_inc(S.t_sc, 1)

            def values(t):
                pe.wait_ge(S.v_p, t + 1)
                for kt in range(1 + t):
                    for h in range(H):
                        last = nc.tensor.transpose(bank[2 * t + kt][:, h * P:(h + 1) * P],
                                                   expS[:, h, kt * P:(kt + 1) * P], ident)
                last.then_inc(S.t_pt, 1)
                pe.wait_ge(S.a_pt, t + 1)
                for h in range(H):
                    for kt in range(1 + t):
                        v = qkvt[:, t, 2 * WA + h * P:2 * WA + (h + 1) * P] if kt == 0 else ckv[:, 1, h * P:(h + 1) * P]
                        last = mm(bank[1 + 3 * t][:, h * P:(h + 1) * P], v, PT[:, kt, h * P:(h + 1) * P],
                                  start=(kt == 0), stop=(kt == t))
                last.then_inc(S.t_o, 1)
                pe.wait_ge(S.a_osq, t + 1)
                mm(bank[2 * t], ones, osq[t], start=True, stop=True).then_inc(S.t_os, 1)

            scores(0)
            scores(1)
            pe.wait_ge(S.v_ab, 1)
            mod_turn(1)
            for j in range(8, MODC):
                mod_chunk(0, j)
            mod_turn(2)
            values(0)
            mod_chunk(1, 0)
            mod_chunk(1, 1)
            mod_chunk(1, 2)
            mod_chunk(1, 3)
            values(1)
            mod_turn(3)
            mod_chunk(1, 4)
            mod_chunk(1, 5)

            pe.wait_ge(S.v_mixed, 2)
            pe.wait_ge(S.a_silu, 3)
            for n in range(2):
                for h in range(H):
                    last = nc.tensor.transpose(bank[4 + n][:, h * P:(h + 1) * P], convT[:, 2 * H + h, n, :], ident)
                last.then_inc(S.t_at, 1)
            pe.wait_ge(S.a_sqc, 1)
            for n in range(2 * H):
                last = mm(bank[n // 2][:, (n % 2) * T:(n % 2 + 1) * T], ones, sqx[:, n, :], start=True, stop=True)
            last.then_inc(S.t_l2, 1)
            mod_chunk(1, 6)
            mod_chunk(1, 7)
            mod_turn(4)
            pe.wait_ge(S.v_gd, 1)
            pe.wait_ge(S.v_mod, 5)
            for g in range(4):
                t, d = g // 2, g % 2
                last = mm(bank[6][:, g * H:(g + 1) * H], tri[d], gdec[:, g * H:(g + 1) * H], start=True, stop=True)
            last.then_inc(S.t_gc, 1)
            pe.wait_ge(S.v_l2, 1)
            pe.wait_ge(S.a_at, 7)
            for h in range(H):
                last = nc.tensor.transpose(bank[4][:, h * P:(h + 1) * P], convT[:, H + h, 0, :], ident)
            last.then_inc(S.t_at, 1)
            pe.wait_ge(S.a_at, 8)

            def qh(h, t):
                return convT[:, h, t, :]

            def kh(h, t):
                return convT[:, H + h, t, :]

            def delta_tables(g):
                t, d = g // 2, g % 2
                b = 3 * (g % 2)
                if g >= 2:
                    pe.wait_ge(S.v_att, g - 1)
                    pe.wait_ge(S.a_d0, g - 1)
                for h in range(H):
                    last = mm(bank[b][:, h * P:(h + 1) * P], gdec[:, g * H + h:g * H + h + 1].to_broadcast([P, P]),
                              tri[d], start=True, stop=True)
                last.then_inc(S.t_gcb, 1)
                for h in range(H):
                    last = mm(bank[b + 1][:, h * P:(h + 1) * P],
                              beta[:, g * H + h:g * H + h + 1].to_broadcast([P, P]), ident, start=True, stop=True)
                last.then_inc(S.t_bb, 1)
                for h in range(H):
                    last = mm(bank[b + 2][:, h * P:(h + 1) * P], kh(h, t), kh(h, t), start=True, stop=True)
                last.then_inc(S.t_kk, 1)

            def delta_tables2(g):
                t, d = g // 2, g % 2
                b = 3 * (g % 2)
                pe.wait_ge(S.a_dec, g + 1)
                for h in range(H):
                    last = mm(bank[b][:, h * P:(h + 1) * P], kh(h, t), qh(h, t), start=True, stop=True)
                last.then_inc(S.t_qk, 1)
                mod_chunk(1, 8 + g)
                pe.wait_ge(S.v_dt0, g + 1)
                for h in range(H):
                    last = nc.tensor.transpose(bank[b + 1][:, h * P:(h + 1) * P], g_DT[g][:, h * P:(h + 1) * P], ident)
                last.then_inc(S.t_dt, 1)

            for pair in range(2):
                for g in (2 * pair, 2 * pair + 1):
                    delta_tables(g)
                for g in (2 * pair, 2 * pair + 1):
                    delta_tables2(g)
            pe.wait_ge(S.v_att, 4)
            pe.wait_ge(S.a_d0, 4)

            for lev in range(1, LEVELS):
                for pair in range(2):
                    gs = (2 * pair, 2 * pair + 1)
                    n = (lev - 1) * 4
                    for g in gs:
                        b = 3 * (g % 2)
                        pe.wait_ge(S.g_bm, n + g + 1)
                        if lev > 1:
                            pe.wait_ge(S.v_lv, n - 4 + g + 1)
                        for h in range(H):
                            q = slice(h * P, (h + 1) * P)
                            last = mm(bank[b][:, q], g_B[g][:, q], g_D[g][:, q], start=True, stop=True)
                        last.then_inc(S.t_lx, 1)
                    for g in gs:
                        b = 3 * (g % 2)
                        pe.wait_ge(S.a_lx, n + g + 1)
                        if n + g >= 2:
                            pe.wait_ge(S.v_lv, n + g - 1)
                        for h in range(H):
                            q = slice(h * P, (h + 1) * P)
                            if lev < LEVELS - 1:
                                mm(bank[b + 1][:, q], g_DT[g][:, q], g_X[g][:, q], start=True, stop=True)
                            last = mm(bank[b + 2][:, q], g_X[g][:, q], g_DT[g][:, q], start=True, stop=True)
                        last.then_inc(S.t_ld, 1)
                if lev == 2:
                    mod_turn(5)

            pe.wait_ge(S.g_s0, 2)
            pe.wait_ge(S.v_lv, 24)
            for g in (2, 3):
                for h in range(H):
                    q = slice(h * P, (h + 1) * P)
                    last = mm(bank[3 * (g % 2)][:, q], kh(h, 1), g_Lt[g][:, q], start=True, stop=True)
                last.then_inc(S.t_ks, 1)
            VB = [1, 4, 2, 5]
            for g in range(4):
                pe.wait_ge(S.v_r, g + 1)
                for h in range(H):
                    q = slice(h * P, (h + 1) * P)
                    last = mm(bank[VB[g]][:, q], g_DT[g][:, q], g_X[g][:, q], start=True, stop=True)
                last.then_inc(S.t_vn, 1)
            pe.wait_ge(S.v_mod, 6)
            for t in range(NB):
                pe.wait_ge(S.a_vn, 2 * t + 2)
                for h in range(H):
                    q = slice(h * P, (h + 1) * P)
                    terms = []
                    for d in range(2):
                        g = 2 * t + d
                        terms.append((g_B[g][:, q], g_att[g][:, q]))
                        if t == 1:
                            terms.append((g_Lt[g][:, q], g_q[g][:, q]))
                    for n, (a, b) in enumerate(terms):
                        last = mm(bank[6 + t][:, q], a, b, start=(n == 0), stop=(n == len(terms) - 1))
                last.then_inc(S.t_o, 1)
                if t == 0:
                    for g in range(2):
                        pe.wait_ge(S.v_kd, g + 1)
                        for h in range(H):
                            q = slice(h * P, (h + 1) * P)
                            last = mm(bank[3 if g == 0 else 1][:, q], g_D[g][:, q], g_B[g][:, q], start=True, stop=True)
                        last.then_inc(S.t_st, 1)
                pe.wait_ge(S.a_osq, NB + t + 1)
                mm(bank[4 + t], ones, g_X[t], start=True, stop=True).then_inc(S.t_os, 1)

            def project_out(l, name, ready, need):
                w = [None, None]
                for t in range(NB):
                    pe.wait_ge(ready, need[t])
                    for m in range(KT):
                        if t == 0 and m % 4 == 0:
                            w[m // 4] = slot_kn(chunk_full(pe, (name, m // 4)))
                        for k in range(KT):
                            last = mm(bank[2 * t + m // 4][:, (m % 4) * P:(m % 4 + 1) * P],
                                      w[m // 4][:, k, (m % 4) * P:(m % 4 + 1) * P],
                                      hT[:, k, t, :], start=(k == 0), stop=(k == KT - 1))
                        if m % 4 == 3:
                            if t == 1:
                                used(last)
                            else:
                                last.then_inc(S.t_wo, 1)
                        if t == 1 and m == 3:
                            mean_square_of(2 * l + 2, sqm, 5, 0)

            project_out(0, "out0", S.v_mixed, (3, 4))

            def moe(l):
                n = 2 * l + 2
                mean_square_of(n, sqm, 5, 1)
                pe.wait_ge(S.ld_router, 16 * 6)
                for t in range(NB):
                    h_ready(n, t)
                    for k in range(KT):
                        last = mm(bank[0][:, t * 36:t * 36 + 36], hT[:, k, t, :], wrt[:, l, k, :],
                                  start=(k == 0), stop=(k == KT - 1))
                    last.then_inc(S.t_lg, 1)
                    for half in range(2):
                        for k in range(4):
                            last = nc.tensor.transpose(bank[HR[2 * t + half]][:, k * P:(k + 1) * P], hT[:, half * 4 + k, t, :], ident)
                        last.then_inc(S.t_hr, 1)
                pe.wait_ge(S.v_mask, l + 1)
                for t in range(NB):
                    mm(bank[0][:, t * NE:(t + 1) * NE], tri[0], msk[:, t, :], start=True, stop=(t == 0))
                    if t == 1:
                        mm(bank[0][:, NE:2 * NE], ones, msk[:, 0, :], start=False, stop=True)
                for t in range(NB):
                    last = mm(bank[0][:, 2 * NE:3 * NE], ones, msk[:, t, :], start=(t == 0), stop=(t == 1))
                last.then_inc(S.t_pos, 1)

            def gather(half, b, sem):
                for k in range(4):
                    for t in range(NB):
                        for j in range(3):
                            last = mm(bank[b][:, k * P:(k + 1) * P], h3[j][:, t, half * 4 + k, :], Pm[:, t, :],
                                      start=(t == 0 and j == 0), stop=(t == 1 and j == 2))
                last.then_inc(sem, 1)

            def experts_up(s0, s1, sem, n):
                for k in range(KT):
                    for e in range(2):
                        w = ring[:, (s0, s1)[e], :].rearrange("p (a k f) -> p k a f", a=2, k=KT)[:, k, :, :]
                        last = mm(bank[0][e * CAP:(e + 1) * CAP, :], xg[:, k, e * CAP:(e + 1) * CAP], w,
                                  start=(k == 0), stop=(k == KT - 1))
                last.then_inc(sem, n)

            def turn(sem):
                for a in range(2):
                    nc.tensor.transpose(bank[0][:, a * P:(a + 1) * P], hid[:, a * P:(a + 1) * P], ident)
                for t in range(NB):
                    last = nc.tensor.transpose(bank[0][:, (2 + t) * P:(3 + t) * P], PG[:, t, :], ident)
                last.then_inc(sem, 1)

            def experts_down(half, s):
                for a in range(2):
                    for e in range(2):
                        base = e * 2048 + a * D + half * 512
                        last = mm(bank[1 + half][e * CAP:(e + 1) * CAP, :], hidT[:, a, e * CAP:(e + 1) * CAP],
                                  ring[:, s, base:base + 512], start=(a == 0), stop=(a == 1))
                return last

            def scatter():
                for k in range(KT):
                    for j in range(3):
                        last = mm(bank[4 + k // 2][:, (k % 2) * T:(k % 2 + 1) * T], y3[:, j, k, :], ohT,
                                  start=False, stop=True, skip_group_check=True)
                return last

            def moe_experts(l):
                n0 = l * PAIRS
                q0 = l * (PAIRS + 1)
                pe.wait_ge(S.a_hr, 4 * l + 4)
                pe.wait_ge(S.g_h, 6 * l + 6)
                for b in range(4):
                    mm(bank[4 + b], zeros[:, 512:640], zeros[:, 0:512], start=True, stop=True, skip_group_check=True)
                pe.wait_ge(S.v_pos, l + 1)
                pe.wait_ge(S.m_p, 2 * q0 + 1)
                gather(0, 3, S.m_gat)
                gather(1, 0, S.m_gat)
                with pe.Fori(0, PAIRS // 2) as i:
                    for u in range(2):
                        c = moe_at[l] + 3 * u
                        s0, s1, s2 = c % RING, (c + 1) % RING, (c + 2) % RING
                        n = n0 + u
                        q = q0 + u
                        pe.wait_ge(S.m_xg0, i * 2 + (q + 1))
                        pe.wait_ge(S.m_xg1, i * 2 + (q + 1))
                        pe.wait_ge(full[s0], i * 32 + 32 * (c // RING + 1))
                        pe.wait_ge(full[s1], i * 32 + 32 * ((c + 1) // RING + 1))
                        experts_up(s0, s1, S.used, 2)
                        pe.wait_ge(S.m_yr1, i * 2 + (l * YR + u + 1))
                        scatter()
                        pe.wait_ge(S.m_hid, i * 2 + (n + 1))
                        pe.wait_ge(S.m_p, i * 4 + (2 * q + 2))
                        turn(S.m_turn)
                        pe.wait_ge(S.m_p, i * 4 + (2 * q + 3))
                        gather(0, 3, S.m_gat)
                        pe.wait_ge(S.m_td, i * 2 + (n + 1))
                        gather(1, 0, S.m_gat)
                        pe.wait_ge(full[s2], i * 32 + 32 * ((c + 2) // RING + 1))
                        experts_down(0, s2).then_inc(S.m_dn, 1)
                        used(experts_down(1, s2))
                pe.wait_ge(S.m_yr1, (l + 1) * YR)
                scatter()

            def moe_further(l):
                f = FS[l]
                end = moe_at[l] + 3 * PAIRS
                pe.wait_ge(S.v_route, l + 1)
                pe.wait_ge(S.m_xg0, (l + 1) * (PAIRS + 1))
                pe.wait_ge(S.m_xg1, (l + 1) * (PAIRS + 1))
                n = pe.value_load(route_i[0:1, l, 0:1], min_val=0, max_val=OVF // 2)
                with pe.If(n > 0):
                    with pe.Fori(0, n) as i:
                        pe.wait_ge(f.f_dve, i * 5 + 1)
                        gather(0, 3, f.f_pe)
                        gather(1, 0, f.f_pe)
                        pe.wait_ge(f.f_dve, i * 5 + 3)
                        pe.wait_ge(f.f_act, i * 4 + 1)
                        pe.wait_ge(f.f_w, i * 96 + 96)
                        experts_up(end % RING, (end + 1) % RING, f.f_pe, 1)
                        pe.wait_ge(f.f_dve, i * 5 + 4)
                        turn(f.f_pe)
                        pe.wait_ge(f.f_act, i * 4 + 3)
                        experts_down(0, (end + 2) % RING)
                        experts_down(1, (end + 2) % RING).then_inc(f.f_pe, 1)
                        pe.wait_ge(f.f_dve, i * 5 + 5)
                        scatter().then_inc(f.f_pe, 1)
                with pe.Else():
                    pe.nop()
                mm(bank[0][:, 0:16], zeros[:, 512:640], zeros[:, 0:16], start=True, stop=True).then_inc(S.t_fin, 1)

            moe(0)
            moe_experts(0)
            moe_further(0)

            mean_square(3, sqo, 1)
            for j in range(2):
                s = chunk_full(pe, ("in1", 2 + j))
                w = slot_kn(s)
                for t in range(NB):
                    for k in range(KT):
                        if j == 0 and t == 0 and k % 4 == 0:
                            h_ready(3, k // 4)
                        last = mm(bank[4 + 2 * j + t], hT[:, k, t, :], w[:, k, :], start=(k == 0), stop=(k == KT - 1))
                    if t == 0:
                        last.then_inc(S.t_v, 1)
                used(last)
            for j in range(2):
                s = chunk_full(pe, ("in1", j))
                w = slot_kn(s)
                for m in range(4):
                    b = 2 * j + m // 2
                    for k in range(KT):
                        last = mm(bank[b][:, (m % 2) * T:(m % 2 + 1) * T], w[:, k, m * P:(m + 1) * P], hT[:, k, :, :],
                                  start=(k == 0), stop=(k == KT - 1))
                    if m == 1:
                        last.then_inc(S.t_u, 1)
                used(last)
            pe.wait_ge(S.ld_odd, 16 * 4)
            pe.wait_ge(S.a_gv, 4)
            for g in range(4):
                last = nc.tensor.transpose(bank[4][:, g * P:(g + 1) * P], wsp[:, g, :], ident)
            last.then_inc(S.t_ws, 1)
            pe.wait_ge(S.a_ws, 1)
            for t in range(NB):
                pe.wait_ge(S.v_ln, t + 1)
                for m in range(KT):
                    last = mm(bank[4 + 2 * t + m // 4][:, (m % 4) * P:(m % 4 + 1) * P],
                              vtk[:, t, m * P:(m + 1) * P], wsT[:, m // 2, :], start=True, stop=True)
                    if m % 4 == 3:
                        last.then_inc(S.t_mx, 1)
            pe.wait_ge(S.a_gelu, 4)
            project_out(1, "out1", S.v_mix, (2, 4))
            moe(1)
            moe_experts(1)
            moe_further(1)

            mean_square(5, sqf, 1)
            for half in range(2):
                pe.wait_ge(S.v_last, half + 1)
                for t in range(NB):
                    for k in range(4):
                        last = nc.tensor.transpose(bank[2 + 2 * t + half][:, k * P:(k + 1) * P], hT[:, half * 4 + k, t, :], ident)
                    last.then_inc(S.t_last, 1)

        @block.scalar
        def _(act):
            A = nc.scalar.activation

            act.dma_start(vec2[0:16, :], I["norm_ffn"].rearrange("l (m p) -> (l m) p", p=P)).then_inc(S.ld_vec, 16)
            act.dma_start(vec2[16:24, :], I["final_norm"].rearrange("(m p) -> m p", p=P)).then_inc(S.ld_vec, 16)
            act.dma_start(vec2[24:84, :], I["conv_w"][0].rearrange("j (m p) -> (j m) p", p=P)).then_inc(S.ld_vec, 16)
            act.dma_start(vec2[84:85, :], I["delta_norm"]).then_inc(S.ld_vec, 16)
            act.dma_start(vec2[85:86, :], I["subln"]).then_inc(S.ld_vec, 16)
            act.dma_start(xin[:, 0, :], I["x_prompt"][0]).then_inc(S.ld_x, 16)
            act.dma_start(xin[:, 1, :], I["x_sample"][0]).then_inc(S.ld_x, 16)

            def inv_root(dst, src, scale, ev, n):
                A(dst, src, ACT.Ln, bias=epsc, scale=scale).then_inc(S.a_chain, 1)
                count[0] += 1
                act.wait_ge(S.a_chain, count[0])
                A(dst, dst, ACT.Exp, scale=-0.5).then_inc(ev, 1)

            count = [0]

            def squares(n, sq, k0, k1, t0, t1):
                A(sq[:, k0:k1, t0 * P:t1 * P], xT[:, k0:k1, t0:t1, :].rearrange("p k t n -> p k (t n)"), ACT.Square).then_inc(S.a_sq, 1)

            def modulate(n, l, shift, k0, k1, t):
                for k in range(k0, k1):
                    last = A(hT[:, k, t, :], hT[:, k, t, :], ACT.Identity, scale=mulA[:, n - 1, k, t:t + 1],
                             bias=modT[:, l * MT + shift + k, t:t + 1])
                last.then_inc(S.a_h, 1)

            def root_mean(n, b, t0, t1):
                act.wait_ge(S.t_ms, MS0[n] + (t0 if n in (2, 4) else 0) + 1)
                inv_root(rstd[:, t0 * P:t1 * P], bank[b][:, t0 * P:t1 * P], 1.0 / D, S.a_rstd, 0)

            def norm(n, b, l, shift):
                if n == 3:
                    root_mean(n, b, 0, NB)
                else:
                    act.wait_ge(S.v_a, 1)
                for half in range(2):
                    act.wait_ge(S.v_xn, 2 * (n - 1) + half + 1)
                    modulate(n, l, shift, 4 * half, 4 * half + 4, 1)

            def mod_row(g):
                act.wait_ge(S.used, index[("mod", g // 3, 4 * (g % 3) + 3)] + 1)
                if g > 0:
                    act.wait_ge(S.t_mod, g)
                A(mrow, bank[7], ACT.Copy).then_inc(S.a_mrow, 1)

            act.wait_ge(S.v_cols, 1)
            A(condT[:, :, :].rearrange("p t k -> p (t k)"), cols[:, V_COND:V_COND + NB * KT], ACT.Silu).then_inc(S.a_silu_c, 1)
            for b in (2, 3):
                act.wait_ge(S.t_x, b + 1)
                A(xT[:, (b % 2) * 4:(b % 2) * 4 + 4, 1, :], heads(bank[1 + b]), ACT.Copy).then_inc(S.a_xt, 1)
            act.wait_ge(S.a_xt, 2)
            act.wait_ge(S.v_xt, 2)
            squares(1, sqx, 0, KT, 0, NB)
            root_mean(1, 5, 0, NB)
            mod_row(0)
            norm(1, 5, 0, 0)
            act.dma_start(const[:, C_LEV:NC_COLS], I["consts"][:, C_LEV:NC_COLS]).then_inc(S.ld_levels, 16)
            act.dma_start(wab[:, :, :], wi0[:, :, 7 * 512:IN_EVEN]).then_inc(S.ld_small, 16)
            act.dma_start(alog, I["a_log"][0].rearrange("a b -> (a b)").partition_broadcast(P)).then_inc(S.ld_small, 16)
            act.dma_start(dtb, I["dt_bias"][0].rearrange("a b -> (a b)").partition_broadcast(P)).then_inc(S.ld_small, 16)
            act.dma_start(lamq, I["lam_q"][0].rearrange("a b -> (a b)").partition_broadcast(P)).then_inc(S.ld_small, 16)
            act.dma_start(lamk, I["lam_k"][0].rearrange("a b -> (a b)").partition_broadcast(P)).then_inc(S.ld_small, 16)
            act.dma_start(ckv[:, 0, :], I["cache_k"][0, 0].rearrange("t h e -> t (h e)")).then_inc(S.ld_attn, 16)
            act.dma_start(ckv[:, 1, :], I["cache_v"][0, 0].rearrange("t h e -> t (h e)")).then_inc(S.ld_attn, 16)
            act.dma_start(brt[:, :, 0:NG], I["b_router_group"].partition_broadcast(P)).then_inc(S.ld_router, 16)
            act.dma_start(brt[:, :, NG:], I["b_router_expert"].partition_broadcast(P)).then_inc(S.ld_router, 16)

            for n in range(3):
                act.wait_ge(S.used, index[("in0", n)] + 1)
                A(qkvt[:, 1, n * WA:(n + 1) * WA], bank[2 * n + 1], ACT.Copy).then_inc(S.a_qkv, 1)
            act.wait_ge(S.g_set, 2)
            for u in (1, 3, 5):
                act.wait_ge(S.used, index[("in0", 3 + u // 2)] + 1)
                A(raw[:, 2 * u:2 * u + 2, :, 2:P + 2].rearrange("p c t n -> p (c t) n"),
                  bank[u].rearrange("p (c n) -> p c n", n=P), ACT.Copy).then_inc(S.a_cv, 1)
            for u in (6, 7):
                if u == 6:
                    act.wait_ge(S.t_cv, 4)
                else:
                    act.wait_ge(S.used, index[("in0", 6)] + 1)
                A(gateT[:, 2 * (u - 6):2 * (u - 6) + 2, :, :].rearrange("p c t n -> p (c t n)"), bank[u - 6], ACT.Silu).then_inc(S.a_cv, 1)
            act.wait_ge(S.v_qkv, 3)
            act.dma_start(O["new_cache_k"][0, 0].rearrange("t h e -> t (h e)"), qkvt[:, 0, WA:2 * WA]).then_inc(S.stored, 16)
            act.dma_start(O["new_cache_v"][0, 0].rearrange("t h e -> t (h e)"), qkvt[:, 0, 2 * WA:3 * WA]).then_inc(S.stored, 16)
            act.wait_ge(S.t_ab, 1)
            act.dma_start(S0[:, 0, :].rearrange("p (h n) -> p h n", h=H), I["state_fwd"][0, 0].rearrange("h k v -> k h v")).then_inc(S.ld_state, 16)
            act.dma_start(S0[:, 1, :].rearrange("p (h n) -> p h n", h=H), I["state_bwd"][0, 0].rearrange("h k v -> k h v")).then_inc(S.ld_state, 16)
            act.wait_ge(S.v_abx, 1)
            A(t16a, t16a, ACT.Exp).then_inc(S.a_e1, 1)
            A(alog, alog, ACT.Exp).then_inc(S.a_e1, 1)
            A(beta, beta, ACT.Exp, scale=-1.0).then_inc(S.a_e1, 1)
            A(lame, lame, ACT.Exp).then_inc(S.a_e1, 1)
            act.wait_ge(S.a_e1, 4)
            A(t16a, t16a, ACT.Ln, bias=onec).then_inc(S.a_ab, 1)

            for n in range(5):
                act.wait_ge(S.t_at, n + 1)
                A(attT[:, n, :], bank[n], ACT.Copy).then_inc(S.a_at, 1)
            mod_row(1)
            for t in range(NB):
                act.wait_ge(S.v_sub, t + 1)
                w = P * (1 + t)
                A(expS[:, :, 0:w], expS[:, :, 0:w], ACT.Exp, scale=DH ** -0.5).then_inc(S.a_exp, 1)
                if t == 0:
                    mod_row(2)
                act.wait_ge(S.v_p, t + 1)
                if t == 0:
                    act.wait_ge(S.t_pt, 1)
                    A(PT[:, 0, :], bank[0], ACT.Copy).then_inc(S.a_pt, 1)
                else:
                    act.wait_ge(S.t_pt, 2)
                    act.wait_ge(S.t_o, 1)
                    A(PT[:, :, :], psum[:, 2:4, :], ACT.Copy).then_inc(S.a_pt, 1)
                act.wait_ge(S.t_o, t + 1)
                A(osq[t], bank[1 + 3 * t], ACT.Square).then_inc(S.a_osq, 1)
                act.wait_ge(S.t_os, t + 1)
                inv_root(ors[t], bank[2 * t], 1.0 / P, S.a_ors, t + 1)
            mod_row(3)

            for n in range(3):
                act.wait_ge(S.v_conv, 4 * 12 + 4 * (n + 1))
                v = convT[:, 4 * n:4 * n + 4, :, :].rearrange("p h t n -> p (h t n)")
                A(v, v, ACT.Silu).then_inc(S.a_silu, 1)
            act.wait_ge(S.a_silu, 2)
            A(sqx.rearrange("p k n -> p (k n)"), convT[:, 0:8, :, :].rearrange("p h t n -> p (h t n)"), ACT.Square).then_inc(S.a_sqc, 1)
            for n in range(2):
                act.wait_ge(S.t_at, 5 + n + 1)
                A(vtok[:, n, :], bank[4 + n], ACT.Copy).then_inc(S.a_at, 1)
            act.wait_ge(S.t_l2, 1)
            inv_root(sqx.rearrange("p k n -> p (k n)"), psum[:, 0:4, :].rearrange("p b n -> p (b n)"), 1.0, S.a_l2, 1)
            mod_row(4)
            act.wait_ge(S.v_gc, 1)
            A(egc, gcc, ACT.Exp).then_inc(S.a_egc, 1)
            act.wait_ge(S.t_at, 8)
            A(ktok, bank[4], ACT.Copy).then_inc(S.a_at, 1)
            for pair in range(2):
                for g in (2 * pair, 2 * pair + 1):
                    act.wait_ge(S.v_dd, g + 1)
                    if g >= 2:
                        A(g_q[g], bank[3 * (g % 2)], ACT.Exp).then_inc(S.a_qg, 1)
                    A(g_D[g], g_D[g], ACT.Exp).then_inc(S.a_dec, 1)
                for g in (2 * pair, 2 * pair + 1):
                    act.wait_ge(S.t_dt, g + 1)
                    act.wait_ge(S.v_att, g + 1)
                    A(g_D[g], bank[3 * (g % 2) + 1], ACT.Copy).then_inc(S.a_d0, 1)
            mod_row(5)
            act.wait_ge(S.v_gll, 1)
            A(ekd, ekd, ACT.Exp).then_inc(S.a_kd, 1)
            for lev in range(1, LEVELS):
                for g in range(4):
                    act.wait_ge(S.t_lx, (lev - 1) * 4 + g + 1)
                    A(g_X[g], bank[3 * (g % 2)], ACT.Copy).then_inc(S.a_lx, 1)
            act.wait_ge(S.t_mod, 6)
            for l in range(DEPTH):
                act.dma_start(wrt[:, l, :, 0:NG], I["w_router_group"][l].rearrange("(k p) n -> p k n", p=P)).then_inc(S.ld_router, 16)
                act.dma_start(wrt[:, l, :, NG:], I["w_router_expert"][l].rearrange("(k p) n -> p k n", p=P)).then_inc(S.ld_router, 16)

            VB = [1, 4, 2, 5]
            for g in range(4):
                act.wait_ge(S.t_vn, g + 1)
                A(g_B[g], bank[VB[g]], ACT.Copy).then_inc(S.a_vn, 1)
            act.wait_ge(S.t_o, 3)
            A(g_X[0], bank[6], ACT.Square).then_inc(S.a_osq, 1)
            for g in range(2):
                act.wait_ge(S.t_st, g + 1)
                A(g_Lt[g], bank[3 if g == 0 else 1], ACT.Copy).then_inc(S.a_st, 1)
                act.wait_ge(S.a_st, g + 1)
                out = [O["new_state_fwd"], O["new_state_bwd"]][g]
                act.dma_start(out[0, 0].rearrange("h k v -> k h v"), heads(g_Lt[g])).then_inc(S.stored, 16)
            for t in range(NB):
                if t == 1:
                    act.wait_ge(S.t_o, 4)
                    A(g_X[1], bank[7], ACT.Square).then_inc(S.a_osq, 1)
                act.wait_ge(S.t_os, NB + t + 1)
                inv_root(g_X[2 + t], bank[4 + t], 1.0 / P, S.a_ors, NB + t + 1)

            def moe(l):
                n = 2 * l + 2
                for t in range(NB):
                    for half in range(2):
                        act.wait_ge(S.v_x, 4 * l + 2 * t + half + 1)
                        squares(n, sqm, 4 * half, 4 * half + 4, t, t + 1)
                    root_mean(n, 5, t, t + 1)
                    if t == 1:
                        tokens_rows(l, 0)
                    act.wait_ge(S.v_xn, 2 * (n - 1) + t + 1)
                    modulate(n, l, 3 * KT, 4, KT, t)
                if l == 0:
                    act.dma_start(wsp[:, :, :], I["w_spatial"][0].rearrange("g p q -> p g q")).then_inc(S.ld_odd, 16)
                    act.dma_start(bsp, I["b_spatial"][0].partition_broadcast(P)).then_inc(S.ld_odd, 16)
                    act.dma_start(lng, I["sgu_ln_g"][0].partition_broadcast(P)).then_inc(S.ld_odd, 16)
                    act.dma_start(lnb, I["sgu_ln_b"][0].partition_broadcast(P)).then_inc(S.ld_odd, 16)
                tokens_rows(l, 1)
                act.wait_ge(S.v_rexp, 2 * l + 1)
                A(rs[:, 8:16], rs[:, 8:16], ACT.Exp).then_inc(S.a_rexp, 1)
                act.wait_ge(S.v_rexp, 2 * l + 2)
                A(rs[:, 24:26], rs[:, 24:26], ACT.Exp).then_inc(S.a_rexp, 1)

            def tokens_rows(l, t):
                for n in (2 * t, 2 * t + 1):
                    act.wait_ge(S.t_hr, 4 * l + n + 1)
                    at = slice((n % 2) * 64, (n % 2) * 64 + 64)
                    src = bank[HR[n]].rearrange("p (a k) -> p k a", k=KT)
                    A(hrow[:, t, :, at], src, ACT.Copy)
                    A(h3[0][:, t, :, at], src, ACT.Copy).then_inc(S.a_hr, 1)

            def turned(sem):
                A(hidT, bank[0][:, 0:2 * P].rearrange("p (a n) -> p a n", a=2), ACT.Copy)
                A(pgT, bank[0][:, 2 * P:4 * P], ACT.Copy, accum_out=slot_gate).then_inc(sem, 1)

            def moe_experts(l):
                n0, q0 = l * PAIRS, l * (PAIRS + 1)
                act.wait_ge(S.m_gat, 2 * q0 + 2)
                A(xg[:, 4:8, :], heads(bank[0]), ACT.Copy).then_inc(S.m_xg1, 1)
                with act.Fori(0, PAIRS // 2) as i:
                    for u in range(2):
                        n, q = n0 + u, q0 + u
                        c = moe_at[l] + 3 * u
                        act.wait_ge(S.used, i * 6 + (c + 2))
                        A(sg, bank[0][:, 0:FE], ACT.Silu).then_inc(S.m_sg, 1)
                        act.wait_ge(S.m_turn, i * 2 + (n + 1))
                        turned(S.m_td)
                        act.wait_ge(S.m_gat, i * 4 + (2 * q + 4))
                        A(xg[:, 4:8, :], heads(bank[0]), ACT.Copy).then_inc(S.m_xg1, 1)
                        act.wait_ge(S.m_dn, i * 2 + (n + 1))
                        A(yr[:, 0:4, :], heads(bank[1]), ACT.Copy, scale=slot_gate).then_inc(S.m_yr0, 1)

            def moe_further(l):
                f = FS[l]
                act.wait_ge(S.v_route, l + 1)
                n = act.value_load(route_i[0:1, l, 0:1], min_val=0, max_val=OVF // 2)
                with act.If(n > 0):
                    with act.Fori(0, n) as i:
                        act.wait_ge(f.f_pe, i * 6 + 3)
                        A(xg[:, 4:8, :], heads(bank[0]), ACT.Copy).then_inc(f.f_act, 1)
                        act.wait_ge(f.f_pe, i * 6 + 4)
                        A(sg, bank[0][:, 0:FE], ACT.Silu).then_inc(f.f_act, 1)
                        act.wait_ge(f.f_pe, i * 6 + 5)
                        turned(f.f_act)
                        act.wait_ge(f.f_pe, i * 6 + 6)
                        A(yr[:, 0:4, :], heads(bank[1]), ACT.Copy, scale=slot_gate).then_inc(f.f_act, 1)
                with act.Else():
                    act.nop()

            moe(0)
            moe_experts(0)
            moe_further(0)

            def stream_squares(n, sq):
                for b in range(4):
                    act.wait_ge(S.v_y, SQ_Y[n] + b + 1)
                    squares(n, sq, 2 * b, 2 * b + 2, 0, NB)

            SQ_Y = {3: 0, 5: 4}

            def layer_norm_scale():
                for t in range(NB):
                    act.wait_ge(S.v_cen, t + 1)
                    if t == 1:
                        act.wait_ge(S.a_sqv, 1)
                    A(vsq, vtk[:, t, :], ACT.Square, accum_out=lns[:, t:t + 1]).then_inc(S.a_sqv, 1)
                act.wait_ge(S.a_sqv, 2)
                inv_root(lnr, lns, 1.0 / D, S.a_lnr, 1)

            stream_squares(3, sqo)
            norm(3, 1, 1, 0)
            for n in range(4):
                j, t = n // 2, n % 2
                if t == 0:
                    act.wait_ge(S.t_v, j + 1)
                else:
                    act.wait_ge(S.used, index[("in1", 2 + j)] + 1)
                A(vtk[:, t, j * 512:(j + 1) * 512], bank[4 + n], ACT.Gelu_apprx_tanh).then_inc(S.a_gv, 1)
            for b in range(4):
                if b % 2 == 0:
                    act.wait_ge(S.t_u, b // 2 + 1)
                else:
                    act.wait_ge(S.used, index[("in1", b // 2)] + 1)
                A(uT[:, 2 * b:2 * b + 2, :].rearrange("p k n -> p (k n)"), bank[b], ACT.Gelu_apprx_tanh).then_inc(S.a_gelu, 1)
                if b == 1:
                    layer_norm_scale()
            act.wait_ge(S.t_ws, 1)
            A(wsT[:, :, :].rearrange("p g n -> p (g n)"), bank[4], ACT.Copy).then_inc(S.a_ws, 1)

            moe(1)
            moe_experts(1)
            moe_further(1)

            stream_squares(5, sqf)
            root_mean(5, 1, 0, NB)
            for half in range(2):
                act.wait_ge(S.t_last, 2 * half + 2)
                A(yrow[:, 1, 512 * half:512 * half + 512], bank[4 + half], ACT.Copy).then_inc(S.a_fin, 1)

        @block.gpsimd
        def _(pool):
            pool.memset(zeros[:, :], 0.0).then_inc(S.g_set, 1)
            pool.memset(raw[:, :, :, 0:2].rearrange("p c t n -> p (c t) n"), 0.0)
            pool.memset(raw[:, :, :, P + 2:P + 4].rearrange("p c t n -> p (c t) n"), 0.0).then_inc(S.g_set, 1)
            pool.wait_ge(S.ld_levels, 16)
            for lev in range(1, LEVELS):
                for g in range(4):
                    if lev == 1:
                        pool.wait_ge(S.v_att, g + 1)
                    else:
                        pool.wait_ge(S.t_lx, (lev - 2) * 4 + g + 1)
                    nc.gpsimd.tensor_tensor(heads(g_B[g]), heads(g_Lt[g]), bcast_mid(level(g % 2, lev), H), ALU.mult).then_inc(S.g_bm, 1)
            pool.wait_ge(S.ld_state, 32)
            pool.wait_ge(S.g_bm, 4 * (LEVELS - 1))
            for d in range(2):
                pool.tensor_copy(g_Lt[2 + d], S0[:, d, :]).then_inc(S.g_s0, 1)
            for l in range(DEPTH):
                for t in range(NB):
                    n = 6 * l + 3 * t
                    pool.wait_ge(S.a_hr, 4 * l + 2 * t + 2)
                    nc.gpsimd.tensor_tensor(hrow[:, t], hrow[:, t], h3[0][:, t], ALU.subtract).then_inc(S.g_h, 1)
                    pool.wait_ge(S.g_h, n + 1)
                    pool.tensor_copy(h3[1][:, t], hrow[:, t]).then_inc(S.g_h, 1)
                    pool.wait_ge(S.g_h, n + 2)
                    nc.gpsimd.tensor_tensor(h3[2][:, t], hrow[:, t], h3[1][:, t], ALU.subtract).then_inc(S.g_h, 1)

        @block.vector
        def _(dve):
            V = nc.vector
            chain = [0]

            def link(ins):
                chain[0] += 1
                ins.then_inc(S.v_chain, 1)
                dve.wait_ge(S.v_chain, chain[0])

            dve.wait_ge(S.t_vec, 1)
            V.tensor_copy(cols[:, :], bank[0][:, 0:NV]).then_inc(S.v_cols, 1)
            for b in (0, 1):
                dve.wait_ge(S.t_x, b + 1)
                V.tensor_copy(xT[:, b * 4:b * 4 + 4, 0, :], heads(bank[1 + b])).then_inc(S.v_xt, 1)
            dve.wait_ge(S.v_cols, 1)

            def modulation(g):
                dve.wait_ge(S.t_mod, g + 1)
                a = g * 16
                V.tensor_tensor(modT[:, a:a + 16, :].rearrange("p (j m) t -> p j m t", m=4),
                                bank[6].rearrange("p (j m x) -> p j m x", j=4, m=4)[:, :, :, 0:NB],
                                cols[:, V_BMOD + a:V_BMOD + a + 16].rearrange("p (j m) -> p j m", m=4).unsqueeze(3).to_broadcast([P, 4, 4, NB]),
                                ALU.add).then_inc(S.v_mod, 1)

            def gain(n, l, at, norm_col):
                V.scalar_tensor_tensor(mulA[:, n, :, :], modT[:, l * MT + at:l * MT + at + KT, :], 1.0,
                                       bcast_last(cols[:, norm_col:norm_col + KT], NB), ALU.add, ALU.mult).then_inc(S.v_a, 1)

            def modulate(n, l, shift, k0, k1, t):
                for k in range(k0, k1):
                    last = V.tensor_scalar(hT[:, k, t, :], hT[:, k, t, :], mulA[:, n - 1, k, t:t + 1],
                                           modT[:, l * MT + shift + k, t:t + 1], ALU.mult, ALU.add)
                last.then_inc(S.v_h, 1)

            def norm(n, l, shift):
                dve.wait_ge(S.a_rstd, MS0[n] + 1)
                if n == 1:
                    for half in range(2):
                        normalise(4 * half)
                    modulation(0)
                    dve.wait_ge(S.v_mod, 1)
                    gain(0, 0, KT, V_NMIX)
                dve.wait_ge(S.v_a, 1 if n == 1 else 4)
                for half in range(2):
                    k = 4 * half
                    if n == 3:
                        normalise(k)
                    dve.wait_ge(S.v_xn, 2 * (n - 1) + half + 1)
                    modulate(n, l, shift, k, k + 4, 0)

            def normalise(k):
                V.tensor_tensor(hT[:, k:k + 4, :, :].rearrange("p k t n -> p k (t n)"),
                                xT[:, k:k + 4, :, :].rearrange("p k t n -> p k (t n)"),
                                bcast_mid(rstd[:, :], 4), ALU.mult).then_inc(S.v_xn, 1)

            norm(1, 0, 0)

            for n in range(3):
                dve.wait_ge(S.t_qkv, n + 1)
                V.tensor_copy(qkvt[:, 0, n * WA:(n + 1) * WA], bank[2 * n]).then_inc(S.v_qkv, 1)
            dve.wait_ge(S.g_set, 2)
            for u in (0, 2, 4):
                dve.wait_ge(S.t_cv, u // 2 + 1)
                V.tensor_copy(raw[:, 2 * u:2 * u + 2, :, 2:P + 2].rearrange("p c t n -> p (c t) n"),
                              bank[u].rearrange("p (c n) -> p c n", n=P)).then_inc(S.v_cv, 1)

            dve.wait_ge(S.a_qkv, 2)
            qk = qkvt[:, 1, 0:2 * WA]
            link(V.tensor_tensor(rtmp.rearrange("p (a n) -> p a n", n=DH), qk.rearrange("p (a n) -> p a n", n=DH),
                                 bcast_mid(const[:, C_COS:C_COS + DH], 16), ALU.mult))
            sinv = const[:, C_SIN:C_SIN + DH].rearrange("p (x s f) -> p x s f", x=2, s=2)
            qv = qk.rearrange("p (a x s f) -> p a x s f", x=2, s=2, f=16)
            rv = rq.rearrange("p (a x s f) -> p a x s f", x=2, s=2, f=16)
            for s in range(2):
                last = V.tensor_tensor(rv[:, :, :, s, :], qv[:, :, :, 1 - s, :],
                                       sinv[:, :, s, :].unsqueeze(1).to_broadcast([P, 16, 2, 16]), ALU.mult)
            link(last)
            V.tensor_tensor(rq, rq, rtmp, ALU.add).then_inc(S.v_rope, 1)

            dve.wait_ge(S.a_cv, 3)
            dve.wait_ge(S.v_cv, 3)
            for j in range(CONV_K):
                for ch in range(12):
                    tap = cols[:, V_CONV + 12 * j + ch:V_CONV + 12 * j + ch + 1]
                    src = raw[:, ch, :, j:j + P]
                    if j == 0:
                        ins = V.tensor_scalar(convT[:, ch, :, :], src, tap, None, ALU.mult)
                    else:
                        dve.wait_ge(S.v_conv, 12 * (j - 1) + ch + 1)
                        ins = V.scalar_tensor_tensor(convT[:, ch, :, :], src, tap, convT[:, ch, :, :], ALU.mult, ALU.add)
                    ins.then_inc(S.v_conv, 1)

            dve.wait_ge(S.t_ab, 1)
            V.tensor_copy(ab, bank[6][:, 0:32]).then_inc(S.v_ab, 1)
            dve.wait_ge(S.v_ab, 1)
            dve.wait_ge(S.ld_small, 16 * 5)
            abv = ab.rearrange("p (t d w h) -> p t d w h", t=2, d=2, w=2)
            g4 = t16a.rearrange("p (t d h) -> p t d h", t=2, d=2)
            link(V.tensor_tensor(g4, abv[:, :, :, 0, :],
                                 dtb.rearrange("p (d h) -> p d h", d=2).unsqueeze(1).to_broadcast([P, 2, 2, H]), ALU.add))
            link(V.tensor_scalar(t16b, t16a, 0.0, None, ALU.max))
            link(V.scalar_tensor_tensor(t16a, t16a, -1.0, t16a, ALU.mult, ALU.min))
            V.tensor_scalar(beta.rearrange("p (t d h) -> p t d h", t=2, d=2), abv[:, :, :, 1, :], -80.0, None, ALU.max)
            link(V.tensor_tensor(lamq, lamq, lamk, ALU.mult))
            V.tensor_reduce(lame, lamq.rearrange("p (a n) -> p a n", a=2), AX.X, ALU.add).then_inc(S.v_abx, 1)
            dve.wait_ge(S.a_ab, 1)
            link(V.tensor_tensor(t16a, t16a, t16b, ALU.add))
            V.scalar_tensor_tensor(gdec.rearrange("p (t x) -> p t x", t=2), t16a.rearrange("p (t x) -> p t x", t=2), -1.0,
                                   bcast_mid(alog, 2), ALU.mult, ALU.mult)
            link(V.tensor_scalar(beta, beta, 1.0, None, ALU.add))
            link(V.reciprocal(beta, beta))
            V.tensor_scalar(subl, cols[:, V_SUB:V_SUB + 1], 1.0 - LAM_INIT, None, ALU.mult)
            V.scalar_tensor_tensor(lamc, lame[:, 0:1], LAM_INIT, lame[:, 1:2], ALU.add, ALU.subtract).then_inc(S.v_gd, 1)

            for t in range(NB):
                dve.wait_ge(S.t_sc, t + 1)
                w = P * (1 + t)
                sc = psum[:, 0:2, :] if t == 0 else psum[:, 2:6, :]
                sc = sc.rearrange("p b (h n) -> p (b h) n", n=w)
                link(V.tensor_reduce(smx, sc, AX.X, ALU.max))
                if t == 1:
                    dve.wait_ge(S.t_pt, 1)
                V.tensor_tensor(expS[:, :, 0:w], sc, bcast_last(smx, w), ALU.subtract).then_inc(S.v_sub, 1)
                dve.wait_ge(S.a_exp, t + 1)
                link(V.tensor_reduce(ssm, expS[:, :, 0:w], AX.X, ALU.add))
                link(V.reciprocal(ssm, ssm))
                link(V.tensor_scalar(ssm[:, H:], ssm[:, H:], lamc, None, ALU.mult))
                link(V.tensor_tensor(expS[:, :, 0:w], expS[:, :, 0:w], bcast_last(ssm, w), ALU.mult))
                V.tensor_tensor(expS[:, 0:H, 0:w], expS[:, 0:H, 0:w], expS[:, H:, 0:w], ALU.subtract).then_inc(S.v_p, 1)
                modulation(1 + t)

            for t in range(NB):
                dve.wait_ge(S.a_ors, t + 1)
                V.scalar_tensor_tensor(hT[:, 0:H, t, :], heads(bank[1 + 3 * t]), subl, heads(ors[t]), ALU.mult, ALU.mult).then_inc(S.v_mixed, 1)
            modulation(3)

            dve.wait_ge(S.ld_levels, 16)
            dve.wait_ge(S.a_l2, 1)
            qn = convT[:, 0:H, :, :].rearrange("p h t n -> p (h t n)")
            kn = convT[:, H:2 * H, :, :].rearrange("p h t n -> p (h t n)")
            rl = sqx.rearrange("p k n -> p (k n)")
            V.scalar_tensor_tensor(qn, qn, P ** -0.5, rl[:, 0:1024], ALU.mult, ALU.mult)
            V.tensor_tensor(kn, kn, rl[:, 1024:2048], ALU.mult).then_inc(S.v_l2, 1)
            modulation(4)
            dve.wait_ge(S.t_gc, 1)
            V.tensor_copy(gcc, bank[6][:, 0:16]).then_inc(S.v_gc, 1)
            dve.wait_ge(S.v_gc, 1)
            for pair in range(2):
                for g in (2 * pair, 2 * pair + 1):
                    d = g % 2
                    b = 3 * d
                    if g == 0:
                        dve.wait_ge(S.v_l2, 1)
                        dve.wait_ge(S.stored, 16 * 2)
                    dve.wait_ge(S.t_gcb, g + 1)
                    if g < 2:
                        e = P - 1 if d == 0 else 0
                        V.tensor_copy(gll[:, g * H:(g + 1) * H], heads(bank[b])[:, :, e])
                    link(V.tensor_tensor(heads(g_D[g]), heads(bank[b]), bcast_last(gcc[:, g * H:(g + 1) * H], P), ALU.subtract))
                    V.tensor_tensor(heads(g_D[g]), heads(g_D[g]), bcast_mid(tri[d], H), ALU.mult).then_inc(S.v_dd, 1)
                for g in (2 * pair, 2 * pair + 1):
                    t, d = g // 2, g % 2
                    b = 3 * d
                    dve.wait_ge(S.a_dec, g + 1)
                    link(V.tensor_tensor(heads(g_D[g]), heads(g_D[g]), bcast_mid(tri[d], H), ALU.mult))
                    dve.wait_ge(S.t_kk, g + 1)
                    link(V.tensor_tensor(g_Lt[g], bank[b + 2], g_D[g], ALU.mult))
                    link(V.tensor_tensor(g_Lt[g], bank[b + 1], g_Lt[g], ALU.mult))
                    link(V.tensor_tensor(heads(g_DT[g]), heads(g_Lt[g]), bcast_mid(level(d, 0), H), ALU.mult))
                    V.tensor_tensor(heads(g_DT[g]), bcast_mid(ident, H), heads(g_DT[g]), ALU.subtract).then_inc(S.v_dt0, 1)
                    if g >= 2:
                        dve.wait_ge(S.a_qg, g - 1)
                        V.tensor_tensor(heads(g_q[g]), heads(g_q[g]), convT[:, 0:H, t, :], ALU.mult)
                    dve.wait_ge(S.t_qk, g + 1)
                    V.tensor_tensor(g_att[g], bank[b], g_D[g], ALU.mult).then_inc(S.v_att, 1)
                if pair == 0:
                    V.tensor_tensor(ekd, gll[:, 0:8], gcc[:, 0:8], ALU.subtract).then_inc(S.v_gll, 1)
            for lev in range(1, LEVELS):
                for g in range(4):
                    b = 3 * (g % 2)
                    dve.wait_ge(S.t_ld, (lev - 1) * 4 + g + 1)
                    if lev == 1:
                        dve.wait_ge(S.a_d0, g + 1)
                    if lev < LEVELS - 1:
                        V.tensor_tensor(g_D[g], g_D[g], bank[b + 1], ALU.subtract)
                    V.tensor_tensor(g_DT[g], g_DT[g], bank[b + 2], ALU.subtract).then_inc(S.v_lv, 1)
            modulation(5)
            dve.wait_ge(S.v_mod, 6)
            gain(1, 0, 4 * KT, V_NFFN)
            gain(2, 1, KT, V_NMIX + KT)
            gain(3, 1, 4 * KT, V_NFFN + KT)
            dve.wait_ge(S.a_at, 8)
            dve.wait_ge(S.a_egc, 1)
            for g in range(4):
                t = g // 2
                if t == 0:
                    V.tensor_tensor(heads(g_X[g]), heads(vtok[:, 0, :]), bcast_last(beta[:, g * H:(g + 1) * H], P), ALU.mult).then_inc(S.v_r, 1)
                else:
                    dve.wait_ge(S.t_ks, g - 1)
                    link(V.tensor_tensor(heads(g_X[g]), heads(bank[3 * (g % 2)]), bcast_last(egc[:, g * H:(g + 1) * H], P), ALU.mult))
                    link(V.tensor_tensor(g_X[g], vtok[:, 1, :], g_X[g], ALU.subtract))
                    V.tensor_tensor(heads(g_X[g]), heads(g_X[g]), bcast_last(beta[:, g * H:(g + 1) * H], P), ALU.mult).then_inc(S.v_r, 1)
            dve.wait_ge(S.a_kd, 1)
            for g in range(2):
                V.tensor_tensor(heads(g_D[g]), heads(ktok), bcast_last(ekd[:, g * H:(g + 1) * H], P), ALU.mult).then_inc(S.v_kd, 1)
            for t in range(NB):
                dve.wait_ge(S.a_ors, NB + t + 1)
                link(V.scalar_tensor_tensor(g_X[t], bank[6 + t], cols[:, V_DN:V_DN + 1], g_X[2 + t], ALU.mult, ALU.mult))
                V.tensor_tensor(hT[:, H:2 * H, t, :], heads(g_X[t]), gateT[:, :, t, :], ALU.mult).then_inc(S.v_mixed, 1)

            def residual(name, l, t):
                for half in range(2):
                    if t == 0:
                        dve.wait_ge(S.t_wo, 2 * l + half + 1)
                    else:
                        dve.wait_ge(S.used, index[(name, half)] + 1)
                    for m in range(4 * half, 4 * half + 4):
                        last = V.scalar_tensor_tensor(xT[:, m, t, :], bank[2 * t + half][:, (m % 4) * P:(m % 4 + 1) * P],
                                                      modT[:, l * MT + 2 * KT + m, t:t + 1], xT[:, m, t, :], ALU.mult, ALU.add)
                    last.then_inc(S.v_x, 1)

            def add_scaled(src, b, at):
                for m in (2 * b, 2 * b + 1):
                    for t in range(NB):
                        o = (m % 2) * T + t * P
                        ins = V.scalar_tensor_tensor(xT[:, m, t, :], src[:, o:o + P], modT[:, at + m, t:t + 1],
                                                     xT[:, m, t, :], ALU.mult, ALU.add)
                return ins

            def moe(l):
                n = 2 * l + 2
                for t in range(NB):
                    residual(["out0", "out1"][l], l, t)
                    dve.wait_ge(S.a_rstd, MS0[n] + t + 1)
                    dve.wait_ge(S.v_a, 4)
                    V.tensor_tensor(hT[:, :, t, :], xT[:, :, t, :], bcast_mid(rstd[:, t * P:(t + 1) * P], KT), ALU.mult).then_inc(S.v_xn, 1)
                    dve.wait_ge(S.v_xn, 2 * (n - 1) + t + 1)
                    modulate(n, l, 3 * KT, 0, 4, t)
                dve.wait_ge(S.t_lg, 2 * l + 2)
                dve.wait_ge(S.stored, 16 * 4)
                link(V.tensor_tensor(lg, bank[0][:, 0:72].rearrange("p (t n) -> p t n", t=2),
                                     brt[:, l, :].unsqueeze(1).to_broadcast([P, 2, 36]), ALU.add))
                gm, gcm, gs, pg = rs[:, 0:2], rs[:, 2:4], rs[:, 4:6], rs[:, 6:8]
                ge = rs[:, 8:16].rearrange("p (t n) -> p t n", t=2)
                gl = lg[:, :, 0:NG]
                link(V.tensor_reduce(gm, gl, AX.X, ALU.max))
                V.tensor_tensor(ge, gl, bcast_last(gm, NG), ALU.subtract).then_inc(S.v_rexp, 1)
                link(V.tensor_tensor(gcls, gl, bcast_last(gm, NG), ALU.is_equal))
                link(V.tensor_tensor(gcls, gcls, bcast_mid(const[:, C_G4:C_G4 + NG], 2), ALU.mult))
                link(V.tensor_reduce(gcm, gcls, AX.X, ALU.max))
                link(V.tensor_tensor(gcls, gcls, bcast_last(gcm, NG), ALU.is_equal))
                link(V.tensor_scalar(gcls, gcls, BIG, -BIG, ALU.mult, ALU.add))
                e3 = em.rearrange("p t (g e) -> p t g e", g=NG)
                link(V.tensor_tensor(e3, lg[:, :, NG:].rearrange("p t (g e) -> p t g e", g=NG),
                                     gcls.unsqueeze(3).to_broadcast([P, 2, NG, EG]), ALU.add))
                m1, m2, c1 = rs[:, 16:18], rs[:, 18:20], rs[:, 20:22]
                e32 = const[:, C_E32:C_E32 + NE]

                def first_of_max(src, m, oh):
                    link(V.tensor_reduce(m, src, AX.X, ALU.max))
                    link(V.tensor_tensor(cnd, src, bcast_last(m, NE), ALU.is_equal))
                    link(V.tensor_tensor(cnd, cnd, bcast_mid(e32, 2), ALU.mult))
                    link(V.tensor_reduce(c1, cnd, AX.X, ALU.max))
                    link(V.tensor_tensor(oh, cnd, bcast_last(c1, NE), ALU.is_equal))

                first_of_max(em, m1, oh1)
                link(V.scalar_tensor_tensor(em2.rearrange("p t e -> p (t e)"), oh1.rearrange("p t e -> p (t e)"), -3 * BIG,
                                            em.rearrange("p t e -> p (t e)"), ALU.mult, ALU.add))
                first_of_max(em2, m2, oh2)
                V.tensor_tensor(rs[:, 24:26], m2, m1, ALU.subtract).then_inc(S.v_rexp, 1)
                V.tensor_tensor(msk, oh1, oh2, ALU.add).then_inc(S.v_mask, 1)
                V.memset(pos[:, :, NE:], 0.0)
                V.memset(gat[:, :, NE:], 0.0)
                dve.wait_ge(S.a_rexp, 2 * l + 1)
                link(V.tensor_reduce(gs, ge, AX.X, ALU.add))
                link(V.reciprocal(pg, gs))
                dve.wait_ge(S.a_rexp, 2 * l + 2)
                w1, w2 = rs[:, 28:30], rs[:, 30:32]
                link(V.tensor_scalar(w1, rs[:, 24:26], 1.0, None, ALU.add))
                link(V.reciprocal(w1, w1))
                link(V.tensor_tensor(w1, w1, pg, ALU.mult))
                link(V.tensor_tensor(w2, w1, rs[:, 24:26], ALU.mult))
                V.tensor_tensor(oh1, oh1, bcast_last(w1, NE), ALU.mult)
                link(V.tensor_tensor(oh2, oh2, bcast_last(w2, NE), ALU.mult))
                link(V.tensor_tensor(gat[:, :, 0:NE], oh1, oh2, ALU.add))
                dve.wait_ge(S.t_pos, l + 1)
                link(V.tensor_tensor(pos[:, :, 0:NE], bank[0][:, 0:64].rearrange("p (t e) -> p t e", t=2), msk, ALU.mult))
                V.tensor_copy(cnt, bank[0][:, 64:96]).then_inc(S.v_pos, 1)
                dve.wait_ge(S.v_pos, l + 1)
                link(V.tensor_scalar(nov, cnt, float(CAP), None, ALU.is_gt))
                for r in range(2, T // CAP):
                    link(V.scalar_tensor_tensor(nov, cnt, float(CAP * r), nov, ALU.is_gt, ALU.add))
                link(V.tensor_reduce(ovs[:, 0:1], nov, AX.X, ALU.add))
                link(V.tensor_scalar(ovs[:, 1:2], ovs[:, 0:1], 0.0, None, ALU.is_gt))
                for r in range(1, OVF // 2):
                    link(V.scalar_tensor_tensor(ovs[:, 1:2], ovs[:, 0:1], 2.0 * r, ovs[:, 1:2], ALU.is_gt, ALU.add))
                V.tensor_copy(route_i[0:1, l, 0:1], ovs[0:1, 1:2]).then_inc(S.v_route, 1)

            def one_hot(dst, positions):
                return V.tensor_tensor(dst.rearrange("p t (e s) -> p t e s", e=2),
                                       const[:, C_SLOT:C_SLOT + CAP].unsqueeze(1).unsqueeze(1).to_broadcast([P, 2, 2, CAP]),
                                       positions.unsqueeze(3).to_broadcast([P, 2, 2, CAP]), ALU.is_equal)

            def weighted(gates):
                return V.tensor_tensor(PG.rearrange("p t (e s) -> p t e s", e=2), Pm.rearrange("p t (e s) -> p t e s", e=2),
                                       gates.unsqueeze(3).to_broadcast([P, 2, 2, CAP]), ALU.mult)

            def weighted_rows():
                return V.tensor_scalar(yr[:, 4:8, :], heads(bank[2]), slot_gate, None, ALU.mult)

            def split(step):
                if step == 1:
                    return V.tensor_tensor(yr, yr, y3[:, 0, :, :], ALU.subtract)
                if step == 3:
                    return V.tensor_tensor(y3[:, 2, :, :], yr, y3[:, 1, :, :], ALU.subtract)
                return V.tensor_copy(y3[:, step // 2, :, :], yr)

            def hidden(ev):
                V.tensor_tensor(hid, bank[0][:, FE:2 * FE], sg, ALU.mult).then_inc(ev, 1)

            def further_tables(l):
                f = FS[l]
                dve.wait_ge(S.v_route, l + 1)
                n = dve.value_load(route_i[0:1, l, 0:1], min_val=0, max_val=OVF // 2)
                with dve.If(n > 0):
                    pre = [0]

                    def flink(ins):
                        pre[0] += 1
                        ins.then_inc(f.f_vpre, 1)
                        dve.wait_ge(f.f_vpre, pre[0])

                    a, b = nov, cumA
                    for sft in (1, 2, 4, 8, 16):
                        V.tensor_copy(b[:, 0:sft], a[:, 0:sft])
                        flink(V.tensor_tensor(b[:, sft:], a[:, sft:], a[:, 0:NE - sft], ALU.add))
                        a, b = b, (cumB if b is cumA else cumA)
                    upto = a
                    flink(V.tensor_tensor(lej, bcast_mid(upto, OVF), bcast_last(const[:, C_J8:C_J8 + OVF], NE), ALU.is_le))
                    ex, exc, rj, en = ovs[:, 8:16], ovs[:, 16:24], ovs[:, 24:32], ovs[:, 32:40]
                    flink(V.tensor_reduce(ex, lej, AX.X, ALU.add))
                    flink(V.tensor_tensor(tj, lej, bcast_mid(nov, OVF), ALU.mult))
                    flink(V.tensor_reduce(exc, tj, AX.X, ALU.add))
                    flink(V.tensor_tensor(rj, const[:, C_J8:C_J8 + OVF], exc, ALU.subtract))
                    flink(V.tensor_scalar(rj, rj, float(CAP), float(CAP), ALU.mult, ALU.add))
                    flink(V.tensor_scalar(en, ex, -1.0, float(NE), ALU.mult, ALU.add))
                    flink(V.tensor_tensor(lej, bcast_mid(const[:, C_E32:C_E32 + NE], OVF), bcast_last(en, NE), ALU.is_equal))
                    for t in range(NB):
                        flink(V.tensor_tensor(tj, lej, bcast_mid(pos[:, t, 0:NE], OVF), ALU.mult))
                        flink(V.tensor_reduce(pos2[:, t, :], tj, AX.X, ALU.add))
                        flink(V.tensor_tensor(tj, lej, bcast_mid(gat[:, t, 0:NE], OVF), ALU.mult))
                        flink(V.tensor_reduce(gat2[:, t, :], tj, AX.X, ALU.add))
                    flink(V.tensor_tensor(pos2, pos2, bcast_mid(rj, 2), ALU.subtract))
                    flink(V.tensor_scalar(ex, ex, float(NE - 1), None, ALU.min))
                    V.tensor_copy(route_i[0:1, l, 1:1 + OVF], ex[0:1, :]).then_inc(f.f_idx, 1)
                with dve.Else():
                    dve.nop()

            def moe_experts(l):
                n0, q0 = l * PAIRS, l * (PAIRS + 1)
                one_hot(Pm, pos[:, :, 0:2]).then_inc(S.m_p, 1)
                dve.wait_ge(S.m_p, 2 * q0 + 1)
                weighted(gat[:, :, 0:2]).then_inc(S.m_p, 1)
                V.tensor_scalar(ohT, const[:, 0:T], 0.0, None, ALU.mult)
                V.tensor_scalar(y3, ones.unsqueeze(1).unsqueeze(1).to_broadcast([P, 3, KT, P]), 0.0, None, ALU.mult).then_inc(S.m_yr1, 1)
                dve.wait_ge(S.m_gat, 2 * q0 + 1)
                V.tensor_copy(xg[:, 0:4, :], heads(bank[3])).then_inc(S.m_xg0, 1)
                further_tables(l)
                with dve.Fori(0, PAIRS // 2) as i:
                    for u in range(2):
                        n, q = n0 + u, q0 + u
                        c = moe_at[l] + 3 * u
                        dve.wait_ge(S.m_gat, i * 4 + (2 * q + 2))
                        dve.wait_ge(S.m_p, i * 4 + (2 * q + 2))
                        one_hot(Pm, pos[:, :, bass.ds(i * 4 + (2 * u + 2), 2)]).then_inc(S.m_p, 1)
                        dve.wait_ge(S.m_sg, i * 2 + (n + 1))
                        hidden(S.m_hid)
                        dve.wait_ge(S.m_turn, i * 2 + (n + 1))
                        dve.wait_ge(S.m_p, i * 4 + (2 * q + 3))
                        weighted(gat[:, :, bass.ds(i * 4 + (2 * u + 2), 2)]).then_inc(S.m_p, 1)
                        dve.wait_ge(S.m_td, i * 2 + (n + 1))
                        V.tensor_scalar(ohT, pgT, 0.0, None, ALU.is_gt)
                        dve.wait_ge(S.m_gat, i * 4 + (2 * q + 3))
                        V.tensor_copy(xg[:, 0:4, :], heads(bank[3])).then_inc(S.m_xg0, 1)
                        dve.wait_ge(S.used, i * 6 + (c + 3))
                        weighted_rows().then_inc(S.m_v, 1)
                        dve.wait_ge(S.m_yr0, i * 2 + (n + 1))
                        for step in range(3):
                            dve.wait_ge(S.m_v, i * 8 + (4 * n + 1 + step))
                            split(step).then_inc(S.m_v, 1)
                        dve.wait_ge(S.m_v, i * 8 + (4 * n + 4))
                        split(3).then_inc(S.m_yr1, 1)

            def moe_further(l):
                f = FS[l]
                n = dve.value_load(route_i[0:1, l, 0:1], min_val=0, max_val=OVF // 2)
                with dve.If(n > 0):
                    dve.wait_ge(S.m_gat, 2 * (l + 1) * (PAIRS + 1))
                    dve.wait_ge(S.m_p, 2 * (l + 1) * (PAIRS + 1))
                    with dve.Fori(0, n) as i:
                        dve.wait_ge(f.f_pe, i * 6 + 1)
                        one_hot(Pm, pos2[:, :, bass.ds(i * 2, 2)]).then_inc(f.f_dve, 1)
                        dve.wait_ge(f.f_dve, i * 5 + 1)
                        weighted(gat2[:, :, bass.ds(i * 2, 2)]).then_inc(f.f_dve, 1)
                        dve.wait_ge(f.f_pe, i * 6 + 2)
                        V.tensor_copy(xg[:, 0:4, :], heads(bank[3])).then_inc(f.f_dve, 1)
                        dve.wait_ge(f.f_act, i * 4 + 2)
                        hidden(f.f_dve)
                        dve.wait_ge(f.f_act, i * 4 + 3)
                        V.tensor_scalar(ohT, pgT, 0.0, None, ALU.is_gt)
                        dve.wait_ge(f.f_pe, i * 6 + 6)
                        weighted_rows().then_inc(f.f_v, 1)
                        dve.wait_ge(f.f_act, i * 4 + 4)
                        for step in range(3):
                            dve.wait_ge(f.f_v, i * 4 + (1 + step))
                            split(step).then_inc(f.f_v, 1)
                        dve.wait_ge(f.f_v, i * 4 + 4)
                        split(3).then_inc(f.f_dve, 1)
                with dve.Else():
                    dve.nop()
                dve.wait_ge(S.t_fin, l + 1)
                for b in range(4):
                    add_scaled(bank[4 + b], b, l * MT + 5 * KT).then_inc(S.v_y, 1)

            moe(0)
            moe_experts(0)
            moe_further(0)

            norm(3, 1, 0)
            for t in range(NB):
                dve.wait_ge(S.a_gv, 3 + t)
                link(V.tensor_reduce(lnm[:, t:t + 1], vtk[:, t, :], AX.X, ALU.add))
                link(V.tensor_scalar(lnm[:, t:t + 1], lnm[:, t:t + 1], 1.0 / D, None, ALU.mult))
                V.tensor_scalar(vtk[:, t, :], vtk[:, t, :], lnm[:, t:t + 1], None, ALU.subtract).then_inc(S.v_cen, 1)
            dve.wait_ge(S.a_lnr, 1)
            dve.wait_ge(S.ld_odd, 16 * 4)
            for t in range(NB):
                link(V.scalar_tensor_tensor(vtk[:, t, :], vtk[:, t, :], lnr[:, t:t + 1], lng, ALU.mult, ALU.mult))
                V.tensor_tensor(vtk[:, t, :], vtk[:, t, :], lnb, ALU.add).then_inc(S.v_ln, 1)
            dve.wait_ge(S.a_gelu, 4)
            for n in range(4):
                t, half = n // 2, n % 2
                dve.wait_ge(S.t_mx, n + 1)
                out = hT[:, 4 * half:4 * half + 4, t, :]
                link(V.tensor_tensor(out.rearrange("p (g c) n -> p g c n", c=2), bank[4 + n].rearrange("p (g c n) -> p g c n", g=2, c=2),
                                     bsp[:, 2 * half:2 * half + 2, :].unsqueeze(2).to_broadcast([P, 2, 2, P]), ALU.add))
                V.tensor_tensor(out, out, uT[:, 4 * half:4 * half + 4, t * P:(t + 1) * P], ALU.mult).then_inc(S.v_mix, 1)
            moe(1)
            moe_experts(1)
            moe_further(1)

            dve.wait_ge(S.a_rstd, MS0[5] + 1)
            for k in range(KT):
                last = V.scalar_tensor_tensor(hT[:, k, :, :].rearrange("p t n -> p (t n)"), xT[:, k, :, :].rearrange("p t n -> p (t n)"),
                                              cols[:, V_FIN + k:V_FIN + k + 1], rstd[:, :], ALU.mult, ALU.mult)
                if k % 4 == 3:
                    last.then_inc(S.v_last, 1)
            for half in range(2):
                dve.wait_ge(S.t_last, 2 * half + 1)
                V.tensor_copy(yrow[:, 0, 512 * half:512 * half + 512], bank[2 + half]).then_inc(S.v_fin, 1)


_INS = ["x_prompt", "x_sample", "cache_k", "cache_v", "state_fwd", "state_bwd", "c", "c_ctx", "norm_mix", "norm_ffn",
        "w_mod", "b_mod", "w_in_even", "conv_w", "a_log", "dt_bias", "delta_norm", "lam_q", "lam_k", "subln",
        "w_out_even", "w_in_odd", "sgu_ln_g", "sgu_ln_b", "w_spatial", "b_spatial", "w_out_odd", "w_router_group",
        "b_router_group", "w_router_expert", "b_router_expert", "w_exp_gate", "w_exp_up", "w_exp_down", "final_norm"]
_OUTS = {"y_prompt": (1, P, D), "y_sample": (1, P, D), "new_cache_k": (1, 1, P, H, P), "new_cache_v": (1, 1, P, H, P),
         "new_state_fwd": (1, 1, H, P, P), "new_state_bwd": (1, 1, H, P, P)}


def kernel(**inputs):
    import concourse.bacc as bacc
    from concourse.bass_utils import run_bass_kernel_spmd as run

    nc = bacc.Bacc("TRN2", target_bir_lowering=False, num_devices=1)
    arrays = {f"in_{n}": np.ascontiguousarray(inputs[n]) for n in _INS}
    arrays["in_consts"] = shape_constants()
    ins = {n[3:]: nc.dram_tensor(n, a.shape, mybir.dt.from_np(a.dtype), kind="ExternalInput").ap() for n, a in arrays.items()}
    outs = {n: nc.dram_tensor(f"out_{n}", s, F32, kind="ExternalOutput").ap() for n, s in _OUTS.items()}
    build(nc, ins, outs)
    r = run(nc, [arrays], core_ids=[0])
    return tuple(r.results[0][f"out_{n}"] for n in _OUTS)
```
